# Optimizing a Trainium2 kernel written in Bass

```python
import jax, jax.numpy as jnp
from jax import lax
import numpy as np
import jax
import jax.numpy as jnp

D_MODEL = 1024
BATCH = 1
SEQ = 512
DEPTH = 2

N_MIXERS = 2
N_HGRN_LAYERS = (DEPTH + 1) // 2
N_ATTN_LAYERS = DEPTH // 2

HGRN_EXPAND = 128
HGRN_HEADS = D_MODEL // HGRN_EXPAND
HGRN_KEY_DIM = HGRN_EXPAND
HGRN_VAL_DIM = D_MODEL // HGRN_HEADS
HGRN_QK_WIDTH = HGRN_HEADS * HGRN_KEY_DIM
HGRN_V_WIDTH = HGRN_HEADS * HGRN_VAL_DIM
HGRN_IN_WIDTH = 2 * HGRN_QK_WIDTH + 2 * HGRN_V_WIDTH
HGRN_CHUNK = 64

ATTN_HEAD_DIM = 128
DILATED_GROUPS = ((128, 1), (512, 4), (2048, 16))
HEADS_PER_GROUP = 4
N_GROUPS = len(DILATED_GROUPS)
ATTN_HEADS = HEADS_PER_GROUP * N_GROUPS
ATTN_WIDTH = ATTN_HEADS * ATTN_HEAD_DIM
ROPE_THETA = 10000.0

D_FF = ((8 * D_MODEL // 3 + 255) // 256) * 256

NORM_EPS = 1e-6


def rmsnorm(x, gain):
    xf = x.astype(jnp.float32)
    y = xf * lax.rsqrt(jnp.mean(xf * xf, axis=-1, keepdims=True) + NORM_EPS)
    return (y * gain.astype(jnp.float32)).astype(x.dtype)

def rope_tables(seq_len):
    inv_freq = 1.0 / (ROPE_THETA ** (jnp.arange(0, ATTN_HEAD_DIM, 2, dtype=jnp.float32) / ATTN_HEAD_DIM))
    pos = jnp.arange(seq_len, dtype=jnp.float32)
    ang = pos[:, None] * inv_freq[None, :]
    return jnp.cos(ang)[:, None, :], jnp.sin(ang)[:, None, :]

def apply_rope(x, cos, sin):
    xf = x.astype(jnp.float32)
    x1, x2 = jnp.split(xf, 2, axis=-1)
    out = jnp.concatenate([x1 * cos - x2 * sin, x2 * cos + x1 * sin], axis=-1)
    return out.astype(x.dtype)

def hgrn2_mixer(u, w_in, lower_bound, out_gain, w_out):
    B, S, _ = u.shape
    H, K, V, C = HGRN_HEADS, HGRN_KEY_DIM, HGRN_VAL_DIM, HGRN_CHUNK
    proj = u @ w_in
    q, f, i, g = jnp.split(proj, [HGRN_QK_WIDTH, 2 * HGRN_QK_WIDTH, 2 * HGRN_QK_WIDTH + HGRN_V_WIDTH], axis=-1)
    lb = lower_bound.astype(jnp.float32)
    forget = lb + (1.0 - lb) * jax.nn.sigmoid(f.astype(jnp.float32))
    key = 1.0 - forget
    log_f = jnp.log(forget)
    query = jax.nn.silu(q.astype(jnp.float32))
    value = i.astype(jnp.float32)

    def to_chunks(t, d):
        return t.reshape(B, S // C, C, H, d).transpose(1, 0, 3, 2, 4)

    xs = (to_chunks(query, K), to_chunks(key, K), to_chunks(value, V), to_chunks(log_f, K))
    causal = jnp.tril(jnp.ones((C, C), dtype=bool))[:, :, None]

    def chunk_step(state, inp):
        qc, kc, vc, gc = inp
        b = jnp.cumsum(gc, axis=2)
        o_inter = jnp.einsum('bhck,bhkv->bhcv', qc * jnp.exp(b), state)
        diff = b[:, :, :, None, :] - b[:, :, None, :, :]
        decay = jnp.exp(jnp.where(causal, diff, -jnp.inf))
        scores = jnp.einsum('bhtk,bhsk,bhtsk->bhts', qc, kc, decay)
        o_intra = jnp.einsum('bhts,bhsv->bhtv', scores, vc)
        b_last = b[:, :, -1, :]
        k_to_end = kc * jnp.exp(b_last[:, :, None, :] - b)
        new_state = jnp.exp(b_last)[..., None] * state + jnp.einsum('bhck,bhcv->bhkv', k_to_end, vc)
        return new_state, o_inter + o_intra

    state0 = jnp.zeros((B, H, K, V), dtype=jnp.float32)
    _, o = lax.scan(chunk_step, state0, xs)
    o = o.transpose(1, 0, 3, 2, 4).reshape(B, S, H, V)
    o = rmsnorm(o, out_gain)
    o = o * jax.nn.silu(g.astype(jnp.float32)).reshape(B, S, H, V)
    return o.reshape(B, S, H * V).astype(u.dtype) @ w_out

def dilated_window_group(q, k, v, window, dilation):
    B, S, Hg, D = q.shape
    span = window // dilation
    L = S // dilation
    nb = -(-L // span)
    Lp = nb * span

    def to_blocks(t):
        t = t.reshape(B, L, dilation, Hg, D).transpose(0, 2, 3, 1, 4)
        t = jnp.pad(t, ((0, 0), (0, 0), (0, 0), (0, Lp - L), (0, 0)))
        return t.reshape(B, dilation, Hg, nb, span, D)

    qb, kb, vb = to_blocks(q), to_blocks(k), to_blocks(v)

    def with_prev(t):
        prev = jnp.pad(t, ((0, 0), (0, 0), (0, 0), (1, 0), (0, 0), (0, 0)))[:, :, :, :-1]
        return jnp.concatenate([prev, t], axis=4)

    kw, vw = with_prev(kb), with_prev(vb)
    scores = jnp.einsum('bdhnqe,bdhnke->bdhnqk', qb, kw, preferred_element_type=jnp.float32) * (D ** -0.5)
    blk = jnp.arange(nb)[:, None, None] * span
    qpos = blk + jnp.arange(span)[None, :, None]
    kpos = blk - span + jnp.arange(2 * span)[None, None, :]
    mask = (kpos <= qpos) & (kpos >= qpos - span) & (kpos >= 0)
    scores = jnp.where(mask, scores, -jnp.inf)
    m = jnp.max(scores, axis=-1, keepdims=True)
    p = jnp.exp(scores - m)
    l = jnp.sum(p, axis=-1, keepdims=True)
    out = jnp.einsum('bdhnqk,bdhnke->bdhnqe', p, vw.astype(jnp.float32)) / l
    lse = (m + jnp.log(l))[..., 0]
    out = out.reshape(B, dilation, Hg, Lp, D)[:, :, :, :L].transpose(0, 3, 1, 2, 4).reshape(B, S, Hg, D)
    lse = lse.reshape(B, dilation, Hg, Lp)[:, :, :, :L].transpose(0, 3, 1, 2).reshape(B, S, Hg)
    return out, lse

def dilated_attention_mixer(u, w_qkv, w_out, cos, sin):
    B, S, _ = u.shape
    qkv = (u @ w_qkv).reshape(B, S, 3, ATTN_HEADS, ATTN_HEAD_DIM)
    q = apply_rope(qkv[:, :, 0], cos, sin)
    k = apply_rope(qkv[:, :, 1], cos, sin)
    v = qkv[:, :, 2]
    outs, lses = [], []
    for gi, (window, dilation) in enumerate(DILATED_GROUPS):
        hs = slice(gi * HEADS_PER_GROUP, (gi + 1) * HEADS_PER_GROUP)
        o_g, lse_g = dilated_window_group(q[:, :, hs], k[:, :, hs], v[:, :, hs], window, dilation)
        outs.append(o_g)
        lses.append(lse_g)
    o = jnp.stack(outs, axis=2)
    lse = jnp.stack(lses, axis=2)
    alpha = jax.nn.softmax(lse, axis=2)
    o = (o * alpha[..., None]).reshape(B, S, ATTN_WIDTH).astype(u.dtype)
    return o @ w_out

def swiglu_ffn(u, w_in, w_down):
    gate, up = jnp.split(u @ w_in, 2, axis=-1)
    return (jax.nn.silu(gate) * up) @ w_down

def first_inputs(seed: int = 0) -> dict:
    key = jax.random.key(seed)
    ks = jax.random.split(key, 13)
    f32 = jnp.float32

    def dense(k, shape, fan_in):
        return jax.random.normal(k, shape, f32) * (fan_in ** -0.5)

    def gain(k, shape):
        return 1.0 + 0.02 * jax.random.normal(k, shape, f32)

    return {
        "x": jax.random.normal(ks[0], (BATCH, SEQ, D_MODEL), f32),
        "norm_mix": gain(ks[1], (DEPTH, D_MODEL)),
        "norm_ffn": gain(ks[2], (DEPTH, D_MODEL)),
        "hgrn_w_in": dense(ks[3], (N_HGRN_LAYERS, D_MODEL, HGRN_IN_WIDTH), D_MODEL),
        "hgrn_lb_logits": 0.5 * jax.random.normal(ks[4], (DEPTH + 1, HGRN_QK_WIDTH), f32),
        "hgrn_out_norm": gain(ks[5], (N_HGRN_LAYERS, HGRN_VAL_DIM)),
        "hgrn_w_out": dense(ks[6], (N_HGRN_LAYERS, HGRN_V_WIDTH, D_MODEL), HGRN_V_WIDTH),
        "attn_w_qkv": dense(ks[7], (N_ATTN_LAYERS, D_MODEL, 3 * ATTN_WIDTH), D_MODEL),
        "attn_w_out": dense(ks[8], (N_ATTN_LAYERS, ATTN_WIDTH, D_MODEL), ATTN_WIDTH),
        "ffn_w_in": dense(ks[9], (DEPTH, D_MODEL, 2 * D_FF), D_MODEL),
        "ffn_w_down": dense(ks[10], (DEPTH, D_FF, D_MODEL), D_FF),
        "final_norm": gain(ks[11], (D_MODEL,)),
    }

def first_block(x, norm_mix, norm_ffn, hgrn_w_in, hgrn_lb_logits, hgrn_out_norm, hgrn_w_out,
              attn_w_qkv, attn_w_out, ffn_w_in, ffn_w_down, final_norm):
    lb_table = jnp.cumsum(jax.nn.softmax(hgrn_lb_logits.astype(jnp.float32), axis=0), axis=0)
    cos, sin = rope_tables(x.shape[1])
    h = x
    for layer in range(DEPTH):
        u = rmsnorm(h, norm_mix[layer])
        if layer % N_MIXERS == 0:
            a = layer // N_MIXERS
            mix = hgrn2_mixer(u, hgrn_w_in[a], lb_table[layer], hgrn_out_norm[a], hgrn_w_out[a])
        else:
            a = layer // N_MIXERS
            mix = dilated_attention_mixer(u, attn_w_qkv[a], attn_w_out[a], cos, sin)
        h = h + mix
        h = h + swiglu_ffn(rmsnorm(h, norm_ffn[layer]), ffn_w_in[layer], ffn_w_down[layer])
    return rmsnorm(h, final_norm)


DEPTH_2 = 1

NSA_HEADS = 8
NSA_KV_GROUPS = 2
NSA_HPG = NSA_HEADS // NSA_KV_GROUPS
NSA_HEAD_DIM = 64
N_NSA_BRANCH = 3
CMP_LEN = 32
CMP_STRIDE = 16
CMP_HIDDEN = 128
SLC_LEN = 64
SLC_TOPK = 16
WINDOW = 512
Q_BLOCK = 128
FORCE_SCORE = 1.0e4

GLA_HEADS = 4
GLA_DK = 64
GLA_DV = 128
GLA_GATE_RANK = 16
GLA_GATE_TAU = 16.0
GLA_CHUNK = 64

ROPE_THETA_2 = 500000.0
ROPE_DIM = NSA_HEAD_DIM // 4

D_FF_2 = (8 * D_MODEL + 3 * 256 - 1) // (3 * 256) * 256

EPS = 1e-6
NEG_INF = -1e30

NSA_Q_COLS = NSA_HEADS * NSA_HEAD_DIM
NSA_KV_COLS = N_NSA_BRANCH * 2 * NSA_KV_GROUPS * NSA_HEAD_DIM
NSA_GATE_COLS = NSA_HEADS * N_NSA_BRANCH
GLA_QK_COLS = GLA_HEADS * GLA_DK
GLA_V_COLS = GLA_HEADS * GLA_DV
MERGE_COLS = 2 * D_MODEL
IN_COLS = NSA_Q_COLS + NSA_KV_COLS + NSA_GATE_COLS + 2 * GLA_QK_COLS + 2 * GLA_V_COLS + GLA_GATE_RANK + MERGE_COLS


def rmsnorm_2(x, gain):
    xf = x.astype(jnp.float32)
    y = xf * lax.rsqrt(jnp.mean(xf * xf, axis=-1, keepdims=True) + EPS)
    return (y * gain.astype(jnp.float32)).astype(x.dtype)

def partial_rope(x, pos):
    half = ROPE_DIM // 2
    inv_freq = ROPE_THETA_2 ** (-jnp.arange(half, dtype=jnp.float32) / half)
    ang = pos.astype(jnp.float32)[:, None] * inv_freq[None, :]
    cos = jnp.cos(ang).astype(x.dtype)
    sin = jnp.sin(ang).astype(x.dtype)
    x1 = x[..., :half]
    x2 = x[..., half:ROPE_DIM]
    return jnp.concatenate([x1 * cos - x2 * sin, x2 * cos + x1 * sin, x[..., ROPE_DIM:]], axis=-1)

def masked_softmax(scores, mask):
    p = jax.nn.softmax(jnp.where(mask, scores, NEG_INF), axis=-1)
    return p * mask

def compress_blocks(kv, pe, w1, w2):
    b, g, t, d = kv.shape
    ratio = CMP_LEN // CMP_STRIDE
    n_sub = t // CMP_STRIDE
    n_cmp = n_sub - ratio + 1
    sub = kv.reshape(b, g, n_sub, CMP_STRIDE, d)
    blocks = jnp.concatenate([sub[:, :, r:r + n_cmp] for r in range(ratio)], axis=3)
    blocks = (blocks + pe).reshape(b, g, n_cmp, CMP_LEN * d)
    return jax.nn.silu(blocks @ w1) @ w2

def selection_overlap(n_cmp, n_slc):
    c_start = np.arange(n_cmp)[:, None] * CMP_STRIDE
    s_start = np.arange(n_slc)[None, :] * SLC_LEN
    ov = (c_start < s_start + SLC_LEN) & (c_start + CMP_LEN > s_start)
    return jnp.asarray(ov, dtype=jnp.float32)

def nsa_attention(q, k_cmp, v_cmp, k_slc, v_slc, k_win, v_win, gates):
    b, g, hg, t_len, d = q.shape
    pos = jnp.arange(t_len)
    scale = NSA_HEAD_DIM ** -0.5
    q_rot = partial_rope(q, pos)
    k_slc = partial_rope(k_slc, pos)
    k_win = partial_rope(k_win, pos)
    n_cmp = k_cmp.shape[2]
    cmp_end = jnp.arange(n_cmp) * CMP_STRIDE + CMP_LEN - 1
    n_slc = t_len // SLC_LEN
    topk = min(SLC_TOPK, n_slc)
    overlap = selection_overlap(n_cmp, n_slc)
    kb = k_slc.reshape(b, g, n_slc, SLC_LEN, d)
    vb = v_slc.reshape(b, g, n_slc, SLC_LEN, d)
    kw = jnp.pad(k_win, ((0, 0), (0, 0), (WINDOW, 0), (0, 0)))
    vw = jnp.pad(v_win, ((0, 0), (0, 0), (WINDOW, 0), (0, 0)))
    bi = jnp.arange(b)[:, None, None, None]
    gi = jnp.arange(g)[None, :, None, None]
    blk_ids = jnp.arange(n_slc)

    def query_block(i):
        s = i * Q_BLOCK
        t = s + jnp.arange(Q_BLOCK)
        q_raw = lax.dynamic_slice_in_dim(q, s, Q_BLOCK, axis=3) * scale
        q_pos = lax.dynamic_slice_in_dim(q_rot, s, Q_BLOCK, axis=3) * scale
        sc = jnp.einsum('bghqd,bgnd->bghqn', q_raw, k_cmp, preferred_element_type=jnp.float32)
        p_c = masked_softmax(sc, cmp_end[None, :] <= t[:, None])
        o_c = jnp.einsum('bghqn,bgnd->bghqd', p_c.astype(v_cmp.dtype), v_cmp)
        imp = jnp.einsum('bgqn,nj->bgqj', p_c.sum(axis=2), overlap)
        cur = t[:, None] // SLC_LEN
        valid = blk_ids[None, :] * SLC_LEN <= t[:, None]
        forced = (blk_ids[None, :] == 0) | (blk_ids[None, :] == cur) | (blk_ids[None, :] == cur - 1)
        score = jnp.where(valid, jnp.where(forced, FORCE_SCORE, imp), -jnp.inf)
        top_v, idx = lax.top_k(score, topk)
        ks = kb[bi, gi, idx]
        vs = vb[bi, gi, idx].reshape(b, g, Q_BLOCK, topk * SLC_LEN, d)
        ss = jnp.einsum('bghqd,bgqnld->bghqnl', q_pos, ks, preferred_element_type=jnp.float32)
        ss = ss.reshape(b, g, hg, Q_BLOCK, topk * SLC_LEN)
        tok = idx[..., None] * SLC_LEN + jnp.arange(SLC_LEN)
        m_s = (jnp.isfinite(top_v)[..., None] & (tok <= t[None, None, :, None, None]))
        m_s = m_s.reshape(b, g, 1, Q_BLOCK, topk * SLC_LEN)
        p_s = masked_softmax(ss, m_s)
        o_s = jnp.einsum('bghqm,bgqmd->bghqd', p_s.astype(vs.dtype), vs)
        kwin = lax.dynamic_slice_in_dim(kw, s, WINDOW + Q_BLOCK, axis=2)
        vwin = lax.dynamic_slice_in_dim(vw, s, WINDOW + Q_BLOCK, axis=2)
        kpos = s - WINDOW + jnp.arange(WINDOW + Q_BLOCK)
        dist = t[:, None] - kpos[None, :]
        m_w = (kpos[None, :] >= 0) & (dist >= 0) & (dist < WINDOW)
        sw = jnp.einsum('bghqd,bgkd->bghqk', q_pos, kwin, preferred_element_type=jnp.float32)
        p_w = masked_softmax(sw, m_w)
        o_w = jnp.einsum('bghqk,bgkd->bghqd', p_w.astype(vwin.dtype), vwin)
        gt = lax.dynamic_slice_in_dim(gates, s, Q_BLOCK, axis=3)
        return gt[..., 0:1] * o_c + gt[..., 1:2] * o_s + gt[..., 2:3] * o_w

    out = lax.map(query_block, jnp.arange(t_len // Q_BLOCK))
    return out.transpose(1, 0, 4, 2, 3, 5).reshape(b, t_len, g * hg * d)

def gla_chunked(q, k, v, log_a):
    b, h, t_len, dk = q.shape
    dv = v.shape[-1]
    n_chunk = t_len // GLA_CHUNK

    def to_chunks(a):
        return jnp.moveaxis(a.astype(jnp.float32).reshape(b, h, n_chunk, GLA_CHUNK, a.shape[-1]), 2, 0)

    causal = jnp.tril(jnp.ones((GLA_CHUNK, GLA_CHUNK), dtype=bool))

    def step(state, inp):
        qc, kc, vc, gc = inp
        cum = jnp.cumsum(gc, axis=2)
        last = cum[:, :, -1:, :]
        inter = jnp.einsum('bhtd,bhdv->bhtv', qc * jnp.exp(cum), state)
        diff = jnp.where(causal[:, :, None], cum[:, :, :, None, :] - cum[:, :, None, :, :], -jnp.inf)
        attn = jnp.einsum('bhtd,bhsd,bhtsd->bhts', qc, kc, jnp.exp(diff))
        out = inter + jnp.einsum('bhts,bhsv->bhtv', attn, vc)
        state = jnp.exp(last)[:, :, 0, :, None] * state + jnp.einsum('bhsd,bhsv->bhdv', kc * jnp.exp(last - cum), vc)
        return state, out

    s0 = jnp.zeros((b, h, dk, dv), jnp.float32)
    _, o = lax.scan(step, s0, (to_chunks(q), to_chunks(k), to_chunks(v), to_chunks(log_a)))
    return jnp.moveaxis(o, 0, 2).reshape(b, h, t_len, dv)

def split_in_proj(proj):
    widths = [NSA_Q_COLS, NSA_KV_COLS, NSA_GATE_COLS, GLA_QK_COLS, GLA_QK_COLS, GLA_V_COLS,
              GLA_GATE_RANK, GLA_V_COLS, MERGE_COLS]
    cuts = [int(c) for c in np.cumsum(widths)[:-1]]
    return jnp.split(proj, cuts, axis=-1)

def second_inputs(seed: int = 0) -> dict:
    key = jax.random.key(seed)
    ks = jax.random.split(key, 20)
    L = DEPTH_2

    def nrm(k, shape, scale):
        return jax.random.normal(k, shape, jnp.float32) * scale

    flat_blk = CMP_LEN * NSA_HEAD_DIM
    return {
        'x': nrm(ks[0], (BATCH, SEQ, D_MODEL), 1.0),
        'norm_mix': 1.0 + nrm(ks[1], (L, D_MODEL), 0.02),
        'w_in': nrm(ks[2], (L, D_MODEL, IN_COLS), D_MODEL ** -0.5),
        'cmp_pe_k': nrm(ks[3], (L, CMP_LEN, NSA_HEAD_DIM), 0.1),
        'cmp_pe_v': nrm(ks[4], (L, CMP_LEN, NSA_HEAD_DIM), 0.1),
        'cmp_k_w1': nrm(ks[5], (L, flat_blk, CMP_HIDDEN), flat_blk ** -0.5),
        'cmp_k_w2': nrm(ks[6], (L, CMP_HIDDEN, NSA_HEAD_DIM), CMP_HIDDEN ** -0.5),
        'cmp_v_w1': nrm(ks[7], (L, flat_blk, CMP_HIDDEN), flat_blk ** -0.5),
        'cmp_v_w2': nrm(ks[8], (L, CMP_HIDDEN, NSA_HEAD_DIM), CMP_HIDDEN ** -0.5),
        'gla_gate_w2': nrm(ks[9], (L, GLA_GATE_RANK, GLA_QK_COLS), GLA_GATE_RANK ** -0.5),
        'gla_gate_b': nrm(ks[10], (L, GLA_QK_COLS), 0.1),
        'gla_norm': 1.0 + nrm(ks[11], (L, GLA_DV), 0.02),
        'w_up_nsa': nrm(ks[12], (L, NSA_Q_COLS, D_MODEL), NSA_Q_COLS ** -0.5),
        'w_up_gla': nrm(ks[13], (L, GLA_V_COLS, D_MODEL), GLA_V_COLS ** -0.5),
        'w_out': nrm(ks[14], (L, D_MODEL, D_MODEL), D_MODEL ** -0.5),
        'norm_ffn': 1.0 + nrm(ks[15], (L, D_MODEL), 0.02),
        'w_ffn_gate': nrm(ks[16], (L, D_MODEL, D_FF_2), D_MODEL ** -0.5),
        'w_ffn_up': nrm(ks[17], (L, D_MODEL, D_FF_2), D_MODEL ** -0.5),
        'w_ffn_down': nrm(ks[18], (L, D_FF_2, D_MODEL), D_FF_2 ** -0.5),
        'norm_final': 1.0 + nrm(ks[19], (D_MODEL,), 0.02),
    }

def second_block(x, norm_mix, w_in, cmp_pe_k, cmp_pe_v, cmp_k_w1, cmp_k_w2, cmp_v_w1, cmp_v_w2,
              gla_gate_w2, gla_gate_b, gla_norm, w_up_nsa, w_up_gla, w_out, norm_ffn,
              w_ffn_gate, w_ffn_up, w_ffn_down, norm_final):
    b, t_len, _ = x.shape
    for layer in range(DEPTH_2):
        h = rmsnorm_2(x, norm_mix[layer])
        proj = h @ w_in[layer]
        q_nsa, kv_nsa, g_nsa, q_gla, k_gla, v_gla, lr_gla, r_gla, g_merge = split_in_proj(proj)
        q_a = q_nsa.reshape(b, t_len, NSA_KV_GROUPS, NSA_HPG, NSA_HEAD_DIM).transpose(0, 2, 3, 1, 4)
        kv = kv_nsa.reshape(b, t_len, 2 * N_NSA_BRANCH, NSA_KV_GROUPS, NSA_HEAD_DIM).transpose(2, 0, 3, 1, 4)
        k_cmp = compress_blocks(kv[0], cmp_pe_k[layer], cmp_k_w1[layer], cmp_k_w2[layer])
        v_cmp = compress_blocks(kv[1], cmp_pe_v[layer], cmp_v_w1[layer], cmp_v_w2[layer])
        gates_a = jax.nn.sigmoid(g_nsa).reshape(b, t_len, NSA_KV_GROUPS, NSA_HPG, N_NSA_BRANCH).transpose(0, 2, 3, 1, 4)
        o_a = nsa_attention(q_a, k_cmp, v_cmp, kv[2], kv[3], kv[4], kv[5], gates_a)
        log_a = jax.nn.log_sigmoid((lr_gla @ gla_gate_w2[layer] + gla_gate_b[layer]).astype(jnp.float32)) / GLA_GATE_TAU
        heads = lambda a, dh: a.reshape(b, t_len, GLA_HEADS, dh).transpose(0, 2, 1, 3)
        o_b = gla_chunked(heads(q_gla * GLA_DK ** -0.5, GLA_DK), heads(k_gla, GLA_DK),
                          heads(v_gla, GLA_DV), heads(log_a, GLA_DK))
        o_b = rmsnorm_2(o_b.transpose(0, 2, 1, 3).astype(x.dtype), gla_norm[layer])
        o_b = (o_b * jax.nn.silu(r_gla.reshape(b, t_len, GLA_HEADS, GLA_DV))).reshape(b, t_len, GLA_V_COLS)
        gate_a, gate_b = jnp.split(jax.nn.sigmoid(g_merge), 2, axis=-1)
        merged = gate_a * (o_a @ w_up_nsa[layer]) + gate_b * (o_b @ w_up_gla[layer])
        x = x + merged @ w_out[layer]
        h = rmsnorm_2(x, norm_ffn[layer])
        x = x + (jax.nn.silu(h @ w_ffn_gate[layer]) * (h @ w_ffn_up[layer])) @ w_ffn_down[layer]
    return rmsnorm_2(x, norm_final)


def setup_inputs(seed=0):
    out = dict(first_inputs(seed))
    for name, value in second_inputs(seed + 1).items():
        if name != "x":
            out[name + "_2"] = value
    return out


def reference(
    x, norm_mix, norm_ffn, hgrn_w_in, hgrn_lb_logits, hgrn_out_norm, hgrn_w_out, attn_w_qkv,
    attn_w_out, ffn_w_in, ffn_w_down, final_norm, norm_mix_2, w_in_2, cmp_pe_k_2, cmp_pe_v_2,
    cmp_k_w1_2, cmp_k_w2_2, cmp_v_w1_2, cmp_v_w2_2, gla_gate_w2_2, gla_gate_b_2, gla_norm_2,
    w_up_nsa_2, w_up_gla_2, w_out_2, norm_ffn_2, w_ffn_gate_2, w_ffn_up_2, w_ffn_down_2,
    norm_final_2,
):
    x = first_block(
        x, norm_mix, norm_ffn, hgrn_w_in, hgrn_lb_logits, hgrn_out_norm, hgrn_w_out, attn_w_qkv,
        attn_w_out, ffn_w_in, ffn_w_down, final_norm,
    )
    return second_block(
        x, norm_mix_2, w_in_2, cmp_pe_k_2, cmp_pe_v_2, cmp_k_w1_2, cmp_k_w2_2, cmp_v_w1_2,
        cmp_v_w2_2, gla_gate_w2_2, gla_gate_b_2, gla_norm_2, w_up_nsa_2, w_up_gla_2, w_out_2,
        norm_ffn_2, w_ffn_gate_2, w_ffn_up_2, w_ffn_down_2, norm_final_2,
    )


_drawn_inputs = setup_inputs


def setup_inputs(seed=0):
    import zlib

    import numpy as np

    out = dict(_drawn_inputs(seed))
    spreads = {}
    factors = {'hgrn_out_norm': 3.049,
     'norm_mix_2': 3.783,
     'cmp_pe_k_2': 8.0,
     'cmp_pe_v_2': 22.821,
     'gla_gate_b_2': 3.461,
     'gla_norm_2': 7.57,
     'norm_ffn_2': 12.243}
    for name, (base, spread) in spreads.items():
        noise = np.random.default_rng([zlib.crc32(name.encode()), seed]).standard_normal(out[name].shape)
        drawn = base * np.exp(spread * noise) if base else spread * noise
        out[name] = jnp.asarray(drawn.astype(out[name].dtype))
    for name, factor in factors.items():
        out[name] = (out[name] * factor).astype(out[name].dtype)
    return out
```

```python
import concourse.bass as bass
from concourse import mybir
from contextlib import ExitStack

F32 = mybir.dt.float32
U32 = mybir.dt.uint32
ALU = mybir.AluOpType
ACT = mybir.ActivationFunctionType
AX = mybir.AxisListType

P = 128
T = 512
D = 1024
DC = D // P
TT = T // P
FF = 2816
FC = FF // P
HEADS_H = 8
C = 128
NCH = T // C
LEVELS = 7
NORMS = 8
GROUPS = 3
HPG = 4
RESIDUES = 4
NEG = -1e30
HEADS_N = 8
HD = 64
NB = 32
TM_COLS = 2 * P + 3 * HEADS_N
HEADS_G = 4
RANK = 16
TAU = 16.0
EPS = 1e-6
RING = 4
SLOT = 12 * P

SECTIONS = [
    ("hgrn", 4 * HEADS_H, 8 * P), ("hgrn_out", DC, 8 * P), ("gu0", 2 * FC, 8 * P), ("down0", 2 * DC, 11 * P),
    ("attn_v", 4 * GROUPS, 8 * P), ("attn_qk", 2 * GROUPS * HPG, 8 * P), ("attn_out", DC, 12 * P),
    ("gu1", 2 * FC, 8 * P), ("down1", 2 * DC, 11 * P),
    ("nsa_fm", 8, 8 * P), ("nsa_tm", 2, 4 * TM_COLS), ("gla_v", 4, 8 * P), ("gla_fm", 4, 8 * P),
    ("gla_lr", 1, 8 * RANK), ("gla_r", HEADS_G, 8 * P), ("merge", 3 * DC, 8 * P), ("mix_out", DC, 8 * P),
    ("gu2", 2 * FC, 8 * P), ("down2", 2 * DC, 11 * P),
]
FIRST = {}
_n = 0
for _name, _units, _ in SECTIONS:
    FIRST[_name] = _n
    _n += _units


def ring_use(section, k, i=None, per=0):
    n = FIRST[section] + k
    count = 16 * (n // RING + 1)
    return n % RING, count if i is None else i * (16 * per // RING) + count


def program(nc, a, out):
    names = """x_loaded consts_loaded w_used h_ready sq_ready ms_ready rstd u_ready lb_steps lb_done
        hq hf hg hv sig_f sig_q sig_g vf_ready forget key query silu_g log_f cum dec_in dec_out chunk_decay
        x_ready vt_ps vt_ready kt_ps kt_ready score_ps scores st_ps states o_ps o_sq o_ms o_rstd o_scaled o_ready
        gate_ps up_ps gate_sig gate_silu gu_ready ffn_ps out_ps stored credit
        av_ready raw_ready rot_ps rope_cos rope_sin qk_ready sc_ps sc_masked sc_max sc_negmax p_exp p_logsum
        p_recip lse lse_diag p_norm pt_ps pt_ready lse_ps lse_rows ao_ps mix_max1 mix_max mix_diff mix_exp mix_sum1
        mix_sum mix_recip mix_weight ao_ready
        nt_ready nrot_ps nrope_cos nrope_sin nrope ntm_ready ngate_ready gv_ready cmp_loaded kvpe_zero kvpe hid_ps
        hid_sig hid kc_ps kc_ready vc_ps vbd cs_ps cs_masked cs_max cs_sub cs_exp cs_sum cs_rec cs_gate cs_valid cs_w
        ct_ps ct_ready co_ps oa_ready ns_ps ns_masked ns_max ns_neg ns_exp nt_ps npt_ready no_ps n_rec n_w n_scaled
        oa_acc oat_ps oat_ready gz_ps z_b z_abs z_exp z_ln z_min log_a gr_sig gr_silu gb_ready mg_sig mg_a mg_b
        merged""".split()
    with ExitStack() as ctx:
        def sb(name, *shape):
            return ctx.enter_context(nc.sbuf_tensor(name, [P, *shape], F32))

        s = {n: ctx.enter_context(nc.semaphore(n)) for n in names}
        w_ready = [ctx.enter_context(nc.semaphore(f"w_ready{r}")) for r in range(RING)]

        h = sb("h_res", DC, T)
        u = sb("u_norm", DC, T)
        ring = sb("ring", RING, SLOT)
        arena = sb("arena", 31000)
        rs = sb("rs_norm", T)
        gains = sb("gains_sb", NORMS, DC)
        ident = sb("ident_sb", P)
        ones = sb("ones_sb", P)
        lvl_mask = sb("lvl_mask_sb", LEVELS + 1, P)
        reset = sb("reset_sb", T)
        lbl = sb("lbl_sb", 3, DC)
        lbt = sb("lbt", 8, DC)
        hgain = sb("hgain_sb", 1)
        rot_a = sb("rot_a_sb", P)
        cos_a = sb("cos_a_sb", T)
        sin_a = sb("sin_a_sb", T)
        win_mask = sb("win_mask_sb", TT, 2 * P)
        res_mask = sb("res_mask_sb", 2, P)
        rot_n = sb("rot_n_sb", P)
        cos_n = sb("cos_n_sb", T)
        sin_n = sb("sin_n_sb", T)
        cmp_mask = sb("cmp_mask_sb", 2, TT * NB)
        pos_kv = sb("pos_kv_sb", 2, 32)
        gw2 = sb("gw2_sb", 2 * P)
        gbias = sb("gbias_sb", 2)
        ggain = sb("ggain_sb", 1)
        eps = sb("eps_sb", 1)
        waited = sb("waited", 1)
        start = sb("start", 4)
        ps = ctx.enter_context(nc.psum_tensor("ps", [P, 8, 512], F32))

        def views(used=0):
            at = [used]

            def take(*shape):
                n = 1
                for x in shape:
                    n *= x
                v = arena[:, at[0]:at[0] + n]
                at[0] += n
                assert at[0] <= 31000, at[0]
                if len(shape) == 2:
                    v = v.rearrange("p (a b) -> p a b", a=shape[0])
                if len(shape) == 3:
                    v = v.rearrange("p (a b c) -> p a b c", a=shape[0], b=shape[1])
                return v
            return take

        take = views()
        O = take(HEADS_H, T)
        sq_, sf_, sg_ = take(T), take(T), take(T)
        vf, fg, key, qry, lf = take(T), take(T), take(T), take(T), take(T)
        sgl, bcum = take(T), take(T)
        dec = take(LEVELS + 2, T)
        vT = take(NCH, C)
        kT = take(NCH, C)
        sc_mat = take(T)
        st = take(NCH, P)
        chd = take(NCH)
        osq, ors, otmp = take(T), take(T), take(T)
        L_END, L_STATE = LEVELS, LEVELS + 1

        take = views()
        gu = take(FC, T)
        sgate = take(2, T)

        omlb, lb = lbt[:, 6], lbt[:, 5]
        take = views()
        aO = take(GROUPS * HPG, T)
        aV = take(GROUPS, TT * T).rearrange("p g (b n) -> p g b n", b=TT)
        QK = [take(2 * GROUPS, T) for _ in range(2)]
        raw, tcos, tsin = take(2, T), take(2, T), take(2, T)
        scm = take(4 * T)
        PTs = take(4 * T)
        dgl = take(GROUPS * TT, P)
        lrow = take(GROUPS, T)
        mxw, sum_, rec = take(T), take(T), take(T)
        mx, nmx, lsum, lrec, lsev = [take(GROUPS, TT) for _ in range(5)]
        SC = [scm[:, 0:1024].rearrange("p (b n) -> p b n", b=4), scm[:, 1024:1536].rearrange("p (b n) -> p b n", b=4),
              scm[:, 1536:2048].rearrange("p (b n) -> p b n", b=4)]
        SC_BANKS = [ps[:, 4:6].rearrange("p a (b n) -> p (a b) n", b=2), ps[:, 6].rearrange("p (b n) -> p b n", b=4),
                    ps[:, 7].rearrange("p (b n) -> p b n", b=4)]

        take = views()
        oaT = take(4, T)
        qg, kg = take(2, T), take(2, T)
        vG = take(TT, HEADS_G * P)
        la = take(2, T)
        own = views(used=sum((4 * T, 4 * T, TT * HEADS_G * P, 2 * T)))
        take = own
        qraw, qrot = take(4, T), take(4, T)
        kvraw, kraw, kr = take(2, T), take(2, T), take(2, T)
        ncos, nsin = take(2, T), take(2, T)
        vsw = take(TT, 2 * P)
        ngate = take(TT, 3 * HEADS_N)
        lrS = take(T)
        zab = take(T)
        hidv, hsig = take(4 * 2 * NB), take(2, 2 * NB)
        hidk = take(2 * NB)
        kc = take(NB)
        vbd = take(2, 4 * HD)
        sC = take(TT, HEADS_N, NB)
        PTc = take(TT * 2, P)
        oa = take(TT, HEADS_N * HD)
        oscl = take(TT, HD)
        cmx, csum, crec, cw = [take(TT, HEADS_N) for _ in range(4)]
        nmax, nneg, nsum, nrec, nw = [take(2, TT) for _ in range(5)]
        w2k, w2v = take(3 * HD), take(HD)
        shared = take(6144)
        w1 = shared[:, 0:4096].rearrange("p (x l m) -> p x l m", x=2, l=16)
        kvp = shared[:, 4096:6144].rearrange("p (x l n) -> p x l n", x=2, l=16)
        prob, probT = [shared[:, k * 2560:(k + 1) * 2560].rearrange("p (a n) -> p a n", a=2) for k in range(2)]
        OFF = [0, P, 3 * P, 6 * P]
        BOFF = [0, P, 512, 1024]

        take = views(used=sum((4 * T, 4 * T, TT * HEADS_G * P, 2 * T)))
        gcum = take(2, T)
        gdec = [take(LEVELS + 2, T) for _ in range(2)]
        gkT = take(2, 3 * P)
        gchd = take(2, NCH)
        gsc, gst = take(T), take(NCH, P)
        gsig = take(2, T)
        gsr = take(HEADS_G, T)
        goT = take(HEADS_G, T)
        gosq, gors, gotmp = take(T), take(T), take(T)
        take = views(used=sum((4 * T, 4 * T, TT * HEADS_G * P, 2 * T)))
        take(2, T)
        mrg = take(DC, T)
        msig = take(4, T)
        assert 2 * T + DC * T + 4 * T <= 2 * T + 2 * (LEVELS + 2) * T

        def tokens(g, b):
            return slice(b * P, (b + 1) * P) if g == 0 else slice(b, T, RESIDUES)

        def natural(g, v):
            return v.rearrange("p (b m) -> p b m", b=TT) if g == 0 else v.rearrange("p (r m) -> p m r", r=RESIDUES)

        block = ctx.enter_context(nc.Block())

        constants = ((gains, "gains"), (ident, "ident"), (ones, "ones"), (lvl_mask, "lvl_mask"), (reset, "reset"),
                     (lbl, "lbl"), (hgain, "hgain"), (rot_a, "rot_a"), (cos_a, "cos_a"), (sin_a, "sin_a"),
                     (win_mask, "win_mask"), (res_mask, "res_mask"), (rot_n, "rot_n"), (cos_n, "cos_n"),
                     (sin_n, "sin_n"), (cmp_mask, "cmp_mask"), (pos_kv, "pos_kv"), (gw2[0:RANK], "gw2"),
                     (gbias, "gbias"), (ggain, "ggain"))
        ALL_CONSTANTS = 16 * len(constants)

        @block.sync
        def _(sp):
            for c in range(DC):
                sp.dma_start(h[:, c], a["x"][:, c]).then_inc(s["x_loaded"], 16)
            for dst, name in constants:
                sp.dma_start(dst if name == "gw2" else dst[:], a[name]).then_inc(s["consts_loaded"], 16)
            for name, units, width in SECTIONS:
                w, n0 = a["w_" + name], FIRST[name]
                k0 = 0
                if n0 == 0:
                    for k in range(RING):
                        sp.dma_start(ring[:, k, 0:width], w[k]).then_inc(w_ready[k], 16)
                    k0 = RING
                loops = (units - k0) // RING
                if loops > 1:
                    with sp.Fori(0, loops) as i:
                        for k in range(k0, k0 + RING):
                            r = (n0 + k) % RING
                            sp.wait_ge(s["w_used"], i * RING + (n0 + k - RING + 1))
                            sp.dma_start(ring[:, r, 0:width], w[bass.ds(i * RING + k, 1)].rearrange("a p n -> (a p) n")
                                         ).then_inc(w_ready[r], 16)
                    k0 += loops * RING
                for k in range(k0, units):
                    r = (n0 + k) % RING
                    sp.wait_ge(s["w_used"], n0 + k - RING + 1)
                    sp.dma_start(ring[:, r, 0:width], w[k]).then_inc(w_ready[r], 16)

        H_CREDIT = 2
        def h_done(k, n):
            return 8 * k + n + 1 + H_CREDIT

        @block.tensor
        def _(pe):
            def unit(section, k, rhs, bank, i=None, per=0, first=True, last=True, n=8):
                r, v = ring_use(section, k, i, per)
                pe.wait_ge(w_ready[r], v)
                for c in range(n):
                    m = nc.tensor.matmul(ps[:, bank], ring[:, r, c * P:(c + 1) * P], rhs(c),
                                         start=first and c == 0, stop=last and c == n - 1)
                return m

            def used(m):
                m.then_inc(s["w_used"], 1)

            def mean_square(n):
                for c in range(DC):
                    pe.wait_ge(s["sq_ready"], 8 * n + c + 1)
                    m = nc.tensor.matmul(ps[:, 6], ones[:], u[:, c], start=c == 0, stop=c == DC - 1)
                m.then_inc(s["ms_ready"], 1)

            U = lambda c: u[:, c]

            def project(section, k_upd, K, rhs):
                with pe.Fori(0, DC // RING) as i:
                    for j in range(RING):
                        pe.wait_ge(s["h_ready"], i * RING + (8 * k_upd + j + 1))
                        used(unit(section, j, rhs, j % 2, i, RING, n=K))

            def ffn(f, k_upd):
                with pe.Fori(0, FC // 2) as i:
                    for j in range(2):
                        pe.wait_ge(s["gu_ready"], i * 2 + (FC * f + j + 1))
                        if j == 0:
                            pass
                        used(unit(f"gu{f}", 2 * j, U, 2 * j, i, 4))
                        used(unit(f"gu{f}", 2 * j + 1, U, 2 * j + 1, i, 4))
                pe.wait_ge(s["gu_ready"], FC * (f + 1) + 2)
                with pe.Fori(0, DC // 2) as i:
                    for j in range(2):
                        pe.wait_ge(s["h_ready"], i * 2 + (8 * k_upd + j + 1))
                        used(unit(f"down{f}", 2 * j, lambda c: gu[:, c], 4 + j, i, 4, last=False, n=11))
                        used(unit(f"down{f}", 2 * j + 1, lambda c: gu[:, 11 + c], 4 + j, i, 4, first=False, n=11))

            def hgrn_project(i=None, k0=0, first=False):
                order = (("sig_f", 1), ("query", 0), ("silu_g", 2), ("vf_ready", 3))
                for k, (freed, bank) in enumerate(order):
                    if not first:
                        pe.wait_ge(s[freed], i + 1)
                    used(unit("hgrn", k0 + k, U, bank, i, 4))

            def chunk_scores(i, it, dv, k_, q_, rows, first_x=True):
                for n, l in enumerate(list(range(LEVELS - 1, -1, -1)) + [None]):
                    if l is not None and first_x:
                        pe.wait_ge(s["x_ready"], it * 9 + (n + 3))
                    if n >= 2:
                        pe.wait_ge(s["scores"], i * 8 + (n - 1))
                    for c in range(NCH):
                        t = slice(c * C, (c + 1) * C)
                        kk, qq = (k_[rows, t], q_[rows, t]) if l is None else (dv[rows, l, t], dv[rows, l, t])
                        m = nc.tensor.matmul(ps[:, 4 + n % 2, t], kk, qq, start=True, stop=True)
                    m.then_inc(s["score_ps"], 1)

            def chunk_states(i, keys, values):
                for c in range(NCH - 1):
                    m = nc.tensor.matmul(ps[:, 6, c * C:(c + 1) * C], keys(c), values(c), start=True, stop=True)
                m.then_inc(s["st_ps"], 1)

            def chunk_outputs(i, values, sc, stv, dv, rows, sq):
                pe.wait_ge(s["scores"], i * 8 + 8)
                pe.wait_ge(s["states"], i * 3 + 3)
                for c in range(NCH):
                    t = slice(c * C, (c + 1) * C)
                    m = nc.tensor.matmul(ps[:, 7, t], values(c), sc[:, t], start=True, stop=c == 0)
                    if c:
                        m = nc.tensor.matmul(ps[:, 7, t], stv[rows, c], dv[rows, L_STATE, t], start=False, stop=True)
                m.then_inc(s["o_ps"], 1)
                pe.wait_ge(s["o_sq"], i + 1)
                nc.tensor.matmul(ps[:, 6], ones[:], sq, start=True, stop=True).then_inc(s["o_ms"], 1)

            ALL = slice(0, P)

            def hgrn_core(i):
                pe.wait_ge(s["vf_ready"], i + 1)
                for c in range(NCH):
                    m = nc.tensor.transpose(ps[:, 6, c * C:(c + 1) * C], vf[:, c * C:(c + 1) * C], ident[:])
                m.then_inc(s["vt_ps"], 1)
                chunk_scores(i, i, dec, key, qry, ALL)
                pe.wait_ge(s["vt_ready"], i + 1)
                for c in range(NCH - 1):
                    m = nc.tensor.transpose(ps[:, 6, c * C:(c + 1) * C], dec[:, L_END, c * C:(c + 1) * C], ident[:])
                m.then_inc(s["kt_ps"], 1)
                pe.wait_ge(s["kt_ready"], i + 1)
                chunk_states(i, lambda c: kT[:, c], lambda c: vT[:, c])
                chunk_outputs(i, lambda c: vT[:, c], sc_mat, st, dec, ALL, osq)

            pe.wait_ge(s["consts_loaded"], ALL_CONSTANTS)
            mean_square(0)
            pe.wait_ge(s["u_ready"], 8)
            hgrn_project(0, first=True)
            with pe.Fori(0, HEADS_H - 1) as i:
                hgrn_project(i, k0=4)
                hgrn_core(i)
            hgrn_core(HEADS_H - 1)
            pe.wait_ge(s["o_ready"], HEADS_H)
            project("hgrn_out", 0, 8, lambda c: O[:, c])
            mean_square(1)
            pe.wait_ge(s["u_ready"], 16)
            ffn(0, 1)

            mean_square(2)
            pe.wait_ge(s["u_ready"], 24)
            for g in range(GROUPS):
                base = 4 * (g % 2)
                for n in range(4):
                    rr, v = ring_use("attn_v", 4 * g + n)
                    pe.wait_ge(w_ready[rr], v)
                    for tt in range(TT):
                        if g == 2 and n == 0:
                            pe.wait_ge(s["av_ready"], tt + 1)
                        for cc in range(2):
                            m = nc.tensor.matmul(ps[:, base + tt], u[:, 2 * n + cc, tokens(g, tt)],
                                                 ring[:, rr, cc * 512:(cc + 1) * 512],
                                                 start=n == 0 and cc == 0, stop=n == 3 and cc == 1)
                    used(m)

            def qk_tile(N):
                if N >= 2:
                    pe.wait_ge(s["raw_ready"], N - 1)
                elif N == 0:
                    pe.wait_ge(s["av_ready"], GROUPS * TT)
                used(unit("attn_qk", N, U, N % 2))

            def rotate(N):
                pe.wait_ge(s["raw_ready"], N + 1)
                if N >= 2:
                    pe.wait_ge(s["rope_sin"], N - 1)
                nc.tensor.matmul(ps[:, 2 + N % 2], rot_a[:], raw[:, N % 2], start=True, stop=True
                                 ).then_inc(s["rot_ps"], 1)

            def attn_scores(j):
                pe.wait_ge(s["qk_ready"], 6 * (j + 1))
                if j:
                    pe.wait_ge(s["ao_ready"], 3 * j)
                for g in range(GROUPS):
                    q, k = QK[j % 2][:, 2 * g], QK[j % 2][:, 2 * g + 1]
                    for b in range(TT):
                        if g:
                            m = nc.tensor.matmul(SC_BANKS[g][:, b], q[:, tokens(g, b)], k[:, tokens(g, b)],
                                                 start=True, stop=True)
                        elif b:
                            m = nc.tensor.matmul(SC_BANKS[0][:, b], q[:, tokens(0, b)], k[:, (b - 1) * P:(b + 1) * P],
                                                 start=True, stop=True)
                        else:
                            for half in range(2):
                                m = nc.tensor.matmul(SC_BANKS[0][:, 0, half * P:(half + 1) * P], q[:, 0:P], k[:, 0:P],
                                                     start=True, stop=True)
                    m.then_inc(s["sc_ps"], 1)

            def attn_core(j):
                for g in range(GROUPS):
                    pe.wait_ge(s["p_norm"], 2 * j + 1 + (g > 0))
                    for b in range(TT):
                        for half in range(2 if g == 0 else 1):
                            m = nc.tensor.transpose(SC_BANKS[g][:, b, half * P:(half + 1) * P],
                                                    SC[g][:, b, half * P:(half + 1) * P], ident[:])
                    m.then_inc(s["pt_ps"], 1)
                pe.wait_ge(s["lse_diag"], j + 1)
                pe.wait_ge(s["rope_sin"], min(6 * (j + 2), 24))
                for g, bank in enumerate((2, 3, 7)):
                    if g == 2:
                        pe.wait_ge(s["pt_ready"], 3 * j + 3)
                    for b in range(TT):
                        m = nc.tensor.matmul(ps[:, bank, b * P:(b + 1) * P], ones[:], dgl[:, g * TT + b],
                                             start=True, stop=True)
                    m.then_inc(s["lse_ps"], 1)
                for g in range(GROUPS):
                    hd = slice(j * P, (j + 1) * P)
                    for b in range(TT):
                        o = ps[:, 4 + g, b * P:(b + 1) * P]
                        if g:
                            m = nc.tensor.matmul(o, aV[:, g, b, hd], PTs[:, (g + 1) * T + b * P:(g + 1) * T + (b + 1) * P],
                                                 start=True, stop=True)
                        else:
                            m = nc.tensor.matmul(o, aV[:, 0, b, hd], PTs[:, b * 2 * P + P:(b + 1) * 2 * P],
                                                 start=True, stop=b == 0)
                            if b:
                                m = nc.tensor.matmul(o, aV[:, 0, b - 1, hd], PTs[:, b * 2 * P:b * 2 * P + P],
                                                     start=False, stop=True)
                    m.then_inc(s["ao_ps"], 1)

            for n in range(6):
                qk_tile(n)
                if n:
                    rotate(n - 1)
            rotate(5)
            for j in range(HPG):
                N = 6 * (j + 1)
                if j + 1 < HPG:
                    if j:
                        pe.wait_ge(s["lse_rows"], 3 * j)
                    qk_tile(N)
                    qk_tile(N + 1)
                    rotate(N)
                    qk_tile(N + 2)
                    rotate(N + 1)
                attn_scores(j)
                if j + 1 < HPG:
                    for n in range(3, 6):
                        qk_tile(N + n)
                        rotate(N + n - 1)
                    rotate(N + 5)
                attn_core(j)
            pe.wait_ge(s["ao_ready"], GROUPS * HPG)
            project("attn_out", 2, 12, lambda c: aO[:, c])
            mean_square(3)
            pe.wait_ge(s["u_ready"], 32)
            ffn(1, 3)

            mean_square(4)
            mean_square(5)
            pe.wait_ge(s["u_ready"], 40)
            ROT = {0: 0, 1: 1, 2: 2, 3: 3, 6: 4, 7: 5}

            def fm_tile(n):
                if n >= 2:
                    pe.wait_ge(s["nt_ready"], n - 1)
                used(unit("nsa_fm" if n < 8 else "gla_fm", n % 8, U, n % 2))

            def nsa_rotate(n):
                x = ROT[n]
                pe.wait_ge(s["nt_ready"], n + 1)
                if x >= 2:
                    pe.wait_ge(s["nrope_sin"], x - 1)
                src = qraw[:, n] if n < 4 else kraw[:, n - 6]
                nc.tensor.matmul(ps[:, 2 + x % 2], rot_n[:], src, start=True, stop=True).then_inc(s["nrot_ps"], 1)

            def token_major(section, units, per, width, freed):
                for n in range(units):
                    rr, v = ring_use(section, n)
                    pe.wait_ge(w_ready[rr], v)
                    for tt in range(TT):
                        if n == 0 and freed:
                            pe.wait_ge(s[freed], tt + 1)
                        for cc in range(per):
                            m = nc.tensor.matmul(ps[:, 4 + tt, 0:width], u[:, per * n + cc, tokens(0, tt)],
                                                 ring[:, rr, cc * width:(cc + 1) * width],
                                                 start=n == 0 and cc == 0, stop=n == units - 1 and cc == per - 1)
                    used(m)

            for n in range(8):
                fm_tile(n)
                if n - 1 in ROT:
                    nsa_rotate(n - 1)
            token_major("nsa_tm", 2, 4, TM_COLS, None)
            nsa_rotate(7)
            token_major("gla_v", 4, 2, 512, "ngate_ready")
            for n in range(8, 12):
                fm_tile(n)
            pe.wait_ge(s["nt_ready"], 11)
            rr, v = ring_use("gla_lr", 0)
            pe.wait_ge(w_ready[rr], v)
            for c in range(DC):
                m = nc.tensor.matmul(ps[0:RANK, 0], ring[:, rr, c * RANK:(c + 1) * RANK], u[:, c],
                                     start=c == 0, stop=c == DC - 1)
            used(m)

            pe.wait_ge(s["cmp_loaded"], 48)
            for x in range(2):
                pe.wait_ge(s["kvpe"], 8 * (x + 1))
                pe.wait_ge(s["nt_ready"], 12 + x)
                bank = 1 - x
                for l in range(16):
                    m = nc.tensor.matmul(ps[:, bank, 0:2 * NB], w1[:, x, l], kvp[:, x, l], start=l == 0, stop=l == 15)
                m.then_inc(s["hid_ps"], 1)
            pe.wait_ge(s["nrope_sin"], 6)
            for p in range(2):
                m = nc.tensor.matmul(ps[:, 2 + p], gw2[0:RANK, p * P:(p + 1) * P], lrS[0:RANK], start=True, stop=True)
            m.then_inc(s["gz_ps"], 1)
            pe.wait_ge(s["gv_ready"], TT)
            pe.wait_ge(s["hid"], 2)
            nc.tensor.matmul(ps[:, 6, 0:NB], w2k[:, HD:3 * HD], hidk[:, 0:NB], start=True, stop=False)
            nc.tensor.matmul(ps[:, 6, 0:NB], w2k[:, 0:2 * HD], hidk[:, NB:2 * NB], start=False, stop=True
                             ).then_inc(s["kc_ps"], 1)
            for g in range(2):
                m = nc.tensor.matmul(ps[:, 7, g * HD:(g + 1) * HD], hidv[:, g * P:(g + 1) * P], w2v, start=True, stop=True)
            m.then_inc(s["vc_ps"], 1)

            pe.wait_ge(s["kc_ready"], 1)
            cs = ps[:, 4:6].rearrange("p g (t h n) -> p g t h n", t=TT, h=4)
            for tt in range(TT):
                for hh in range(HEADS_N):
                    rows = slice(hh // 4 * HD, hh // 4 * HD + HD)
                    m = nc.tensor.matmul(cs[:, hh // 4, tt, hh % 4], qraw[rows, hh % 4, tt * P:(tt + 1) * P], kc[rows],
                                         start=True, stop=True)
            m.then_inc(s["cs_ps"], 1)
            pe.wait_ge(s["vbd"], 8)
            pe.wait_ge(s["cs_w"], 1)
            for b in range(2):
                for k in range(4):
                    tt, g = divmod(b * 4 + k, 2)
                    m = nc.tensor.transpose(ps[:, 6 + b, k * P:(k + 1) * P],
                                            sC[:, tt, 4 * g:4 * g + 4].rearrange("p h n -> p (h n)"), ident[:])
                m.then_inc(s["ct_ps"], 1)
            pe.wait_ge(s["ct_ready"], 2)
            pe.wait_ge(s["z_b"], 2)
            for tt in range(TT):
                for g in range(2):
                    m = nc.tensor.matmul(ps[:, tt, g * 256:(g + 1) * 256], PTc[:, 2 * tt + g], vbd[:, g], start=True, stop=True)
                m.then_inc(s["co_ps"], 1)

            def nsa_scores(e):
                hh, x = divmod(e, 2)
                rows = slice(hh // 4 * HD, hh // 4 * HD + HD)
                if e == 0:
                    pe.wait_ge(s["oa_ready"], 3)
                elif e == 1:
                    pe.wait_ge(s["oa_ready"], 4)
                else:
                    pe.wait_ge(s["npt_ready"], 3 * (e - 1))
                base = ps[:, 3 * (e % 2):3 * (e % 2) + 3].rearrange("p a n -> p (a n)")
                for tt in range(TT):
                    m = nc.tensor.matmul(base[:, BOFF[tt]:BOFF[tt] + (tt + 1) * P], qrot[rows, hh % 4, tt * P:(tt + 1) * P],
                                         kr[rows, x, 0:(tt + 1) * P], start=True, stop=True)
                m.then_inc(s["ns_ps"], 1)

            def nsa_transposes(e):
                pe.wait_ge(s["ns_exp"], 4 * (e + 1))
                base = ps[:, 3 * (e % 2):3 * (e % 2) + 3].rearrange("p a n -> p (a n)")
                for k in range(10):
                    m = nc.tensor.transpose(base[:, k * P:(k + 1) * P], prob[:, e % 2, k * P:(k + 1) * P], ident[:])
                m.then_inc(s["nt_ps"], 1)

            def nsa_values(e):
                hh, x = divmod(e, 2)
                pe.wait_ge(s["npt_ready"], 3 * (e + 1))
                if e >= 2:
                    pe.wait_ge(s["n_scaled"], e - 1)
                vcols = slice(x * P + hh // 4 * HD, x * P + hh // 4 * HD + HD)
                for tt in range(TT):
                    for k in range(tt + 1):
                        at = OFF[tt] + k * P
                        m = nc.tensor.matmul(ps[:, 6 + e % 2, tt * HD:(tt + 1) * HD], probT[:, e % 2, at:at + P],
                                             vsw[:, k, vcols], start=k == 0, stop=k == tt)
                m.then_inc(s["no_ps"], 1)

            pe.wait_ge(s["nrope"], 6)
            E = 2 * HEADS_N
            nsa_scores(0)
            for e in range(E):
                if e + 1 < E:
                    nsa_scores(e + 1)
                nsa_transposes(e)
                if e:
                    nsa_values(e - 1)
            nsa_values(E - 1)
            pe.wait_ge(s["oa_acc"], E)
            for ft in range(4):
                for tt in range(TT):
                    m = nc.tensor.transpose(ps[:, ft, tt * P:(tt + 1) * P], oa[:, tt, ft * P:(ft + 1) * P], ident[:])
                m.then_inc(s["oat_ps"], 1)

            for n in range(HEADS_G):
                pe.wait_ge(s["oat_ready"], n + 1)
                used(unit("gla_r", n, U, n))
            for hh in range(HEADS_G):
                p, I = hh // 2, HEADS_H + hh
                rows = slice(hh % 2 * HD, hh % 2 * HD + HD)
                dv = gdec[p]
                vals = lambda c: vG[:, c, hh * P:(hh + 1) * P]
                chunk_scores(I, HEADS_H + p, dv, kg[:, p], qg[:, p], rows, first_x=hh % 2 == 0)
                if hh % 2 == 0:
                    if hh:
                        pe.wait_ge(s["o_rstd"], 2 * I)
                    for c in range(NCH - 1):
                        m = nc.tensor.transpose(ps[:, 6, c * C:(c + 1) * C], dv[:, L_END, c * C:(c + 1) * C], ident[:])
                    m.then_inc(s["kt_ps"], 1)
                    pe.wait_ge(s["kt_ready"], HEADS_H + p + 1)
                else:
                    pe.wait_ge(s["o_rstd"], 2 * I)
                chunk_states(I, lambda c: gkT[:, p, c * P:(c + 1) * P], vals)
                if hh:
                    pe.wait_ge(s["o_scaled"], I)
                chunk_outputs(I, vals, gsc, gst, dv, rows, gosq)

            pe.wait_ge(s["gb_ready"], HEADS_G)
            with pe.Fori(0, 2) as i:
                for j in range(4):
                    b = 4 * (j % 2)
                    pe.wait_ge(s["merged"], i * 4 + (j + 1))
                    used(unit("merge", 3 * j, U, b, i, 12))
                    used(unit("merge", 3 * j + 1, U, b + 1, i, 12))
                    rr, v = ring_use("merge", 3 * j + 2, i, 12)
                    pe.wait_ge(w_ready[rr], v)
                    for c in range(8):
                        src = oaT[:, c] if c < 4 else goT[:, c - 4]
                        m = nc.tensor.matmul(ps[:, b + 2 + c // 4], ring[:, rr, c * P:(c + 1) * P], src,
                                             start=c % 4 == 0, stop=c % 4 == 3)
                    used(m)
            pe.wait_ge(s["merged"], DC + 2)
            project("mix_out", 5, 8, lambda c: mrg[:, c])
            mean_square(6)
            pe.wait_ge(s["u_ready"], 48)
            ffn(2, 6)
            mean_square(7)

        @block.scalar
        def _(act):
            def norm(n):
                for c in range(DC):
                    if n == 0:
                        act.wait_ge(s["x_loaded"], 16 * 8)
                    else:
                        act.wait_ge(s["h_ready"], h_done(n - 1, c))
                    nc.scalar.activation(u[:, c], h[:, c], ACT.Square).then_inc(s["sq_ready"], 1)
                act.wait_ge(s["ms_ready"], n + 1)
                nc.scalar.activation(rs[:], ps[:, 6], ACT.Ln, scale=1.0 / D, bias=eps[:, 0:1]).then_inc(s["rstd"], 1)
                act.wait_ge(s["rstd"], 2 * n + 1)
                nc.scalar.activation(rs[:], rs[:], ACT.Exp, scale=-0.5).then_inc(s["rstd"], 1)

            def ffn(f):
                with act.Fori(0, FC // 2) as i:
                    for j in range(2):
                        act.wait_ge(s["w_used"], i * 4 + (FIRST[f"gu{f}"] + 2 * j + 1))
                        nc.scalar.activation(sgate[:, j], ps[:, 2 * j], ACT.Sigmoid).then_inc(s["gate_sig"], 1)

            def decay_exps(it, cum, dv, ends):
                act.wait_ge(s["cum"], it + 1)
                nc.scalar.activation(dv[:, L_STATE], cum, ACT.Exp).then_inc(s["dec_out"], 1)
                act.wait_ge(s["dec_out"], it * 4 + 1)
                nc.scalar.copy(ends, dv[:, L_STATE, C - 1::C]).then_inc(s["chunk_decay"], 1)
                for lo, hi, ready in ((6, 8, 2), (3, 6, 5), (0, 3, 8)):
                    act.wait_ge(s["dec_in"], it * 8 + ready)
                    nc.scalar.activation(dv[:, lo:hi], dv[:, lo:hi], ACT.Exp).then_inc(s["dec_out"], 1)

            def output_rstd(i, sq, r):
                act.wait_ge(s["o_ps"], i + 1)
                nc.scalar.activation(sq, ps[:, 7], ACT.Square).then_inc(s["o_sq"], 1)
                act.wait_ge(s["o_ms"], i + 1)
                nc.scalar.activation(r, ps[:, 6], ACT.Ln, scale=1.0 / P, bias=eps[:, 0:1]).then_inc(s["o_rstd"], 1)
                act.wait_ge(s["o_rstd"], i * 2 + 1)
                nc.scalar.activation(r, r, ACT.Exp, scale=-0.5).then_inc(s["o_rstd"], 1)

            act.wait_ge(s["credit"], 2)
            norm(0)
            act.wait_ge(s["lb_steps"], 5)
            nc.scalar.activation(lbt[:, 0:3], lbt[:, 0:3], ACT.Exp).then_inc(s["lb_steps"], 1)
            with act.Fori(0, HEADS_H) as i:
                w0 = FIRST["hgrn"]
                for k, (src, dst, done) in enumerate(((1, sf_, "sig_f"), (0, sq_, "sig_q"), (2, sg_, "sig_g"))):
                    act.wait_ge(s["w_used"], i * 4 + (w0 + k + 1))
                    nc.scalar.activation(dst, ps[:, src], ACT.Sigmoid).then_inc(s[done], 1)
                act.wait_ge(s["w_used"], i * 4 + (w0 + 4))
                nc.scalar.copy(vf, ps[:, 3]).then_inc(s["vf_ready"], 1)
                act.wait_ge(s["forget"], i + 1)
                nc.scalar.activation(lf, fg, ACT.Ln).then_inc(s["log_f"], 1)
                decay_exps(i, bcum, dec, chd)
                act.wait_ge(s["vt_ps"], i + 1)
                nc.scalar.copy(vT, ps[:, 6].rearrange("p (c t) -> p c t", c=NCH)).then_inc(s["vt_ready"], 1)
                act.wait_ge(s["kt_ps"], i + 1)
                nc.scalar.copy(kT[:, 0:3], ps[:, 6, 0:3 * C].rearrange("p (c t) -> p c t", c=3)).then_inc(s["kt_ready"], 1)
                output_rstd(i, osq, ors)
            norm(1)
            ffn(0)

            norm(2)
            for g in range(GROUPS):
                for tt in range(TT):
                    act.wait_ge(s["w_used"], FIRST["attn_v"] + 4 * (g + 1))
                    nc.scalar.copy(aV[:, g, tt], ps[:, 4 * (g % 2) + tt]).then_inc(s["av_ready"], 1)

            def take_raw(N):
                act.wait_ge(s["w_used"], FIRST["attn_qk"] + N + 1)
                if N >= 2:
                    act.wait_ge(s["rope_cos"], N - 1)
                    act.wait_ge(s["rot_ps"], N - 1)
                nc.scalar.copy(raw[:, N % 2], ps[:, N % 2]).then_inc(s["raw_ready"], 1)

            for n in range(6):
                take_raw(n)
            for j in range(HPG):
                N = 6 * (j + 1)
                if j + 1 < HPG:
                    for n in range(3):
                        take_raw(N + n)
                for g in range(GROUPS):
                    act.wait_ge(s["sc_negmax"], 3 * j + g + 1)
                    for b in range(TT):
                        nc.scalar.activation(SC[g][:, b], SC[g][:, b], ACT.Exp, bias=nmx[:, g, b:b + 1],
                                             accum_out=lsum[:, g, b:b + 1]).then_inc(s["p_exp"], 1)
                act.wait_ge(s["p_exp"], 12 * (j + 1))
                nc.scalar.activation(lsev, lsum, ACT.Ln).then_inc(s["p_logsum"], 1)
                if j + 1 < HPG:
                    for n in range(3, 6):
                        take_raw(N + n)
                for g in range(GROUPS):
                    act.wait_ge(s["pt_ps"], 3 * j + g + 1)
                    if g == 0:
                        nc.scalar.copy(PTs[:, 0:1024], ps[:, 4:6].rearrange("p a n -> p (a n)")).then_inc(s["pt_ready"], 1)
                    else:
                        nc.scalar.copy(PTs[:, (g + 1) * T:(g + 2) * T], ps[:, 5 + g]).then_inc(s["pt_ready"], 1)
                for g, bank in enumerate((2, 3, 7)):
                    act.wait_ge(s["lse_ps"], 3 * j + g + 1)
                    dst = lrow[:, g].rearrange("p (b m) -> p b m", b=TT if g == 0 else P)
                    nc.scalar.copy(dst, natural(g, ps[:, bank])).then_inc(s["lse_rows"], 1)
                act.wait_ge(s["mix_diff"], j + 1)
                nc.scalar.activation(lrow, lrow, ACT.Exp).then_inc(s["mix_exp"], 1)
            norm(3)
            ffn(1)

            act.wait_ge(s["h_ready"], h_done(3, 7))
            for dst, name in ((w1, "cmp_w1"), (w2k, "cmp_w2k"), (w2v, "cmp_w2v")):
                act.dma_start(dst, a[name]).then_inc(s["cmp_loaded"], 16)
            norm(4)
            norm(5)
            fm_dst = [qraw[:, n] for n in range(4)] + [kvraw[:, 0], kvraw[:, 1], kraw[:, 0], kraw[:, 1],
                                                       qg[:, 0], qg[:, 1], kg[:, 0], kg[:, 1]]

            def take_fm(n):
                scale = float(HD) ** -0.5 if n < 4 or n in (8, 9) else 1.0
                act.wait_ge(s["w_used"], (FIRST["nsa_fm"] + n if n < 8 else FIRST["gla_fm"] + n - 8) + 1)
                nc.scalar.activation(fm_dst[n], ps[:, n % 2], ACT.Copy, scale=scale).then_inc(s["nt_ready"], 1)

            for n in range(8):
                take_fm(n)
            for tt in range(TT):
                act.wait_ge(s["w_used"], FIRST["nsa_tm"] + 2)
                nc.scalar.copy(vsw[:, tt], ps[:, 4 + tt, 0:2 * P]).then_inc(s["ntm_ready"], 1)
                nc.scalar.activation(ngate[:, tt], ps[:, 4 + tt, 2 * P:TM_COLS], ACT.Sigmoid).then_inc(s["ngate_ready"], 1)
            for tt in range(TT):
                act.wait_ge(s["w_used"], FIRST["gla_v"] + 4)
                nc.scalar.copy(vG[:, tt], ps[:, 4 + tt]).then_inc(s["gv_ready"], 1)
            for n in range(8, 12):
                take_fm(n)
            act.wait_ge(s["w_used"], FIRST["gla_lr"] + 1)
            nc.scalar.copy(lrS[0:RANK], ps[0:RANK, 0]).then_inc(s["nt_ready"], 1)
            for x in range(2):
                act.wait_ge(s["hid_ps"], x + 1)
                nc.scalar.activation(hsig[:, x], ps[:, 1 - x, 0:2 * NB], ACT.Sigmoid).then_inc(s["hid_sig"], 1)
            act.wait_ge(s["kc_ps"], 1)
            nc.scalar.copy(kc, ps[:, 6, 0:NB]).then_inc(s["kc_ready"], 1)
            act.wait_ge(s["vc_ps"], 1)
            act.wait_ge(s["kvpe_zero"], 2)
            for g in range(2):
                for k in range(4):
                    rows = slice(32 * k, 32 * k + 32)
                    nc.scalar.copy(vbd[rows, g, k * HD:(k + 1) * HD], ps[rows, 7, g * HD:(g + 1) * HD]).then_inc(s["vbd"], 1)
            for p in range(2):
                act.wait_ge(s["z_b"], p + 1)
                if p:
                    act.wait_ge(s["z_min"], 1)
                nc.scalar.activation(zab, la[:, p], ACT.Abs).then_inc(s["z_abs"], 1)
                act.wait_ge(s["z_abs"], p + 1)
                nc.scalar.activation(zab, zab, ACT.Exp, scale=-1.0).then_inc(s["z_exp"], 1)
                act.wait_ge(s["z_exp"], p + 1)
                nc.scalar.activation(zab, zab, ACT.Ln, bias=ones[:, 0:1]).then_inc(s["z_ln"], 1)
            act.wait_ge(s["cs_sub"], 1)
            nc.scalar.activation(sC, sC, ACT.Exp).then_inc(s["cs_exp"], 1)
            for b in range(2):
                act.wait_ge(s["ct_ps"], b + 1)
                nc.scalar.copy(PTc[:, 4 * b:4 * b + 4], ps[:, 6 + b].rearrange("p (k n) -> p k n", k=4)).then_inc(s["ct_ready"], 1)
            for tt in range(TT):
                act.wait_ge(s["co_ps"], tt + 1)
                nc.scalar.copy(oa[:, tt], ps[:, tt]).then_inc(s["oa_ready"], 1)
            act.wait_ge(s["hid"], 2)
            def nsa_exps(i, x):
                base = ps[:, 3 * x:3 * x + 3].rearrange("p a n -> p (a n)")
                act.wait_ge(s["ns_neg"], i * 2 + (x + 1))
                for tt in range(TT):
                    nc.scalar.activation(prob[:, x, OFF[tt]:OFF[tt] + (tt + 1) * P], base[:, BOFF[tt]:BOFF[tt] + (tt + 1) * P],
                                         ACT.Exp, bias=nneg[:, x, tt:tt + 1], accum_out=nsum[:, x, tt:tt + 1]
                                         ).then_inc(s["ns_exp"], 1)

            def nsa_copies(i, x):
                base = ps[:, 3 * x:3 * x + 3].rearrange("p a n -> p (a n)")
                act.wait_ge(s["nt_ps"], i * 2 + (x + 1))
                for k in range(3):
                    lo, hi = 512 * k, min(512 * (k + 1), 1280)
                    nc.scalar.copy(probT[:, x, lo:hi], base[:, lo:hi]).then_inc(s["npt_ready"], 1)

            nsa_exps(0, 0)
            with act.Fori(0, HEADS_N - 1) as i:
                nsa_exps(i, 1)
                nsa_copies(i, 0)
                nsa_exps(i + 1, 0)
                nsa_copies(i, 1)
            nsa_exps(HEADS_N - 1, 1)
            nsa_copies(HEADS_N - 1, 0)
            nsa_copies(HEADS_N - 1, 1)
            for ft in range(4):
                act.wait_ge(s["oat_ps"], ft + 1)
                nc.scalar.copy(oaT[:, ft], ps[:, ft]).then_inc(s["oat_ready"], 1)
            for n in range(HEADS_G):
                act.wait_ge(s["w_used"], FIRST["gla_r"] + n + 1)
                if n >= 2:
                    act.wait_ge(s["gr_silu"], n - 1)
                nc.scalar.activation(gsig[:, n % 2], ps[:, n], ACT.Sigmoid).then_inc(s["gr_sig"], 1)
            for p in range(2):
                decay_exps(HEADS_H + p, gcum[:, p], gdec[p], gchd[:, p])
            for hh in range(HEADS_G):
                if hh % 2 == 0:
                    act.wait_ge(s["kt_ps"], HEADS_H + hh // 2 + 1)
                    nc.scalar.copy(gkT[:, hh // 2], ps[:, 6, 0:3 * C]).then_inc(s["kt_ready"], 1)
                output_rstd(HEADS_H + hh, gosq, gors)
            act.wait_ge(s["gb_ready"], HEADS_G)
            with act.Fori(0, 2) as i:
                for j in range(4):
                    for k in range(2):
                        act.wait_ge(s["w_used"], i * 12 + (FIRST["merge"] + 3 * j + k + 1))
                        nc.scalar.activation(msig[:, 2 * (j % 2) + k], ps[:, 4 * (j % 2) + k], ACT.Sigmoid
                                             ).then_inc(s["mg_sig"], 1)
            norm(6)
            ffn(2)
            norm(7)
            for c in range(DC):
                act.wait_ge(s["credit"], 3 + c)
                act.dma_start(out[:, c], h[:, c]).then_inc(s["stored"], 16)
            act.wait_ge(s["stored"], 16 * DC)

        @block.gpsimd
        def _(pool):
            def decayed(it, dv, k_, q_, operands):
                for n, l in enumerate((L_END, L_STATE, 6, 5, 4, 3, 2, 1, 0)):
                    if n == 0:
                        pool.wait_ge(s["dec_out"], it * 4 + 2)
                        for sem, v in operands:
                            pool.wait_ge(sem, v)
                        nc.gpsimd.tensor_tensor(dv[:, l], dv[:, l], k_, ALU.mult).then_inc(s["x_ready"], 1)
                        continue
                    if n == 1:
                        pool.wait_ge(s["chunk_decay"], it + 1)
                        nc.gpsimd.tensor_tensor(dv[:, l], dv[:, l], q_, ALU.mult).then_inc(s["x_ready"], 1)
                        continue
                    if n in (3, 6):
                        pool.wait_ge(s["dec_out"], it * 4 + n // 3 + 2)
                    m = 1 << l
                    x = dv[:, l].rearrange("p (b h m) -> p b h m", h=2, m=m)
                    kk = k_.rearrange("p (b h m) -> p b h m", h=2, m=m)
                    qq = q_.rearrange("p (b h m) -> p b h m", h=2, m=m)
                    nc.gpsimd.tensor_tensor(x[:, :, 0], x[:, :, 0], kk[:, :, 0], ALU.mult)
                    nc.gpsimd.tensor_tensor(x[:, :, 1], x[:, :, 1], qq[:, :, 1], ALU.mult).then_inc(s["x_ready"], 1)

            with pool.Fori(0, HEADS_H) as i:
                decayed(i, dec, key, qry, ((s["query"], i + 1), (s["key"], i + 1)))

            def times_cos(N):
                pool.wait_ge(s["raw_ready"], N + 1)
                if N >= 2:
                    pool.wait_ge(s["qk_ready"], N - 1)
                nc.gpsimd.tensor_tensor(tcos[:, N % 2], raw[:, N % 2], cos_a[:], ALU.mult).then_inc(s["rope_cos"], 1)

            for n in range(6):
                times_cos(n)
            for j in range(HPG):
                N = 6 * (j + 1)
                if j + 1 < HPG:
                    for n in range(3):
                        times_cos(N + n)
                pool.wait_ge(s["p_recip"], j + 1)
                nc.gpsimd.tensor_tensor(SC[0], SC[0], lrec[:, 0, :, None].broadcast_to((P, TT, 2 * P)), ALU.mult
                                        ).then_inc(s["p_norm"], 1)
                both = scm[:, 1024:2048].rearrange("p (b n) -> p b n", b=2 * TT)
                r12 = lrec[:, 1:3].rearrange("p g b -> p (g b)")[:, :, None]
                nc.gpsimd.tensor_tensor(both, both, r12.broadcast_to((P, 2 * TT, P)), ALU.mult).then_inc(s["p_norm"], 1)
                pool.wait_ge(s["lse"], j + 1)
                nc.gpsimd.tensor_tensor(dgl, ident[:, None, :].broadcast_to((P, GROUPS * TT, P)),
                                        lsev.rearrange("p g b -> p (g b)")[:, :, None].broadcast_to((P, GROUPS * TT, P)),
                                        ALU.mult).then_inc(s["lse_diag"], 1)
                if j + 1 < HPG:
                    for n in range(3, 6):
                        times_cos(N + n)
                pool.wait_ge(s["mix_max"], j + 1)
                nc.gpsimd.tensor_tensor(lrow, lrow, mxw[:, None, :].broadcast_to((P, GROUPS, T)), ALU.subtract
                                        ).then_inc(s["mix_diff"], 1)
                pool.wait_ge(s["mix_recip"], j + 1)
                nc.gpsimd.tensor_tensor(lrow, lrow, rec[:, None, :].broadcast_to((P, GROUPS, T)), ALU.mult
                                        ).then_inc(s["mix_weight"], 1)

            pool.wait_ge(s["h_ready"], h_done(3, 7))
            nc.gpsimd.memset(kvp, 0.0).then_inc(s["kvpe_zero"], 1)
            nc.gpsimd.memset(vbd, 0.0).then_inc(s["kvpe_zero"], 1)
            for x, n in enumerate((0, 1, 2, 3, 6, 7)):
                pool.wait_ge(s["nt_ready"], n + 1)
                if x >= 2:
                    pool.wait_ge(s["nrope"], x - 1)
                src = qraw[:, n] if n < 4 else kraw[:, n - 6]
                nc.gpsimd.tensor_tensor(ncos[:, x % 2], src, cos_n[:], ALU.mult).then_inc(s["nrope_cos"], 1)
            for p in range(2):
                decayed(HEADS_H + p, gdec[p], kg[:, p], qg[:, p], ())

        @block.vector
        def _(dve):
            def norm(n, dst=u, done=s["u_ready"]):
                dve.wait_ge(s["rstd"], 2 * n + 2)
                for c in range(DC):
                    nc.vector.scalar_tensor_tensor(out=dst[:, c], in0=h[:, c], scalar=gains[:, n, c:c + 1], in1=rs[:],
                                                   op0=ALU.mult, op1=ALU.mult).then_inc(done, 1)

            def residual(section, k_upd, units, base, body):
                n = body
                with dve.Fori(0, DC // n) as i:
                    for j in range(n):
                        dve.wait_ge(s["w_used"], i * (n * units) + (FIRST[section] + units * (j + 1)))
                        hj = h[:, bass.ds(i * n + j, 1)].rearrange("p a t -> p (a t)")
                        nc.vector.tensor_tensor(hj, hj, ps[:, base + j % 2], ALU.add).then_inc(s["h_ready"], 1)

            def ffn(f, k_upd):
                with dve.Fori(0, FC // 2) as i:
                    for j in range(2):
                        dve.wait_ge(s["gate_sig"], i * 2 + (FC * f + j + 1))
                        nc.vector.tensor_tensor(sgate[:, j], sgate[:, j], ps[:, 2 * j], ALU.mult).then_inc(s["gate_silu"], 1)
                        dve.wait_ge(s["w_used"], i * 4 + (FIRST[f"gu{f}"] + 2 * j + 2))
                        dve.wait_ge(s["gate_silu"], i * 2 + (FC * f + j + 1))
                        nc.vector.tensor_tensor(gu[:, bass.ds(i * 2 + j, 1)].rearrange("p a t -> p (a t)"), sgate[:, j],
                                                ps[:, 2 * j + 1], ALU.mult).then_inc(s["gu_ready"], 1)
                residual(f"down{f}", k_upd, 2, 4, 2)

            nc.vector.memset(eps[:], EPS).then_inc(s["credit"], 1)
            nc.vector.memset(chd, 0.0).then_inc(s["credit"], 1)
            nc.vector.memset(start[:, 0:1], 0.0).then_inc(s["gu_ready"], 2)
            nc.vector.memset(start[:, 1:2], 0.0).then_inc(s["h_ready"], 2)
            nc.vector.memset(start[:, 3:4], 0.0).then_inc(s["merged"], 2)
            dve.wait_ge(s["consts_loaded"], ALL_CONSTANTS)
            lbs = s["lb_steps"]
            nc.vector.tensor_tensor(lbt[:, 3], lbl[:, 0], lbl[:, 1], ALU.max).then_inc(lbs, 1)
            dve.wait_ge(lbs, 1)
            nc.vector.tensor_tensor(lbt[:, 3], lbt[:, 3], lbl[:, 2], ALU.max).then_inc(lbs, 1)
            dve.wait_ge(lbs, 2)
            for r in range(3):
                nc.vector.tensor_tensor(lbt[:, r], lbl[:, r], lbt[:, 3], ALU.subtract).then_inc(lbs, 1)
            dve.wait_ge(lbs, 6)
            nc.vector.tensor_tensor(lbt[:, 3], lbt[:, 0], lbt[:, 1], ALU.add).then_inc(lbs, 1)
            dve.wait_ge(lbs, 7)
            nc.vector.tensor_tensor(lbt[:, 3], lbt[:, 3], lbt[:, 2], ALU.add).then_inc(lbs, 1)
            dve.wait_ge(lbs, 8)
            nc.vector.reciprocal(lbt[:, 4], lbt[:, 3]).then_inc(lbs, 1)
            dve.wait_ge(lbs, 9)
            nc.vector.tensor_tensor(lb, lbt[:, 0], lbt[:, 4], ALU.mult).then_inc(lbs, 1)
            dve.wait_ge(lbs, 10)
            nc.vector.tensor_scalar(omlb, lb, -1.0, 1.0, ALU.mult, ALU.add).then_inc(lbs, 1)
            dve.wait_ge(lbs, 11)
            def exponents(it, b, log_decay, dv):
                nc.vector.tensor_tensor_scan(b, reset[:], log_decay, 0.0, ALU.mult, ALU.add).then_inc(s["cum"], 1)
                dve.wait_ge(s["cum"], it + 1)
                b2 = b.rearrange("p (c t) -> p c t", c=NCH)
                nc.vector.tensor_tensor(dv[:, L_END].rearrange("p (c t) -> p c t", c=NCH),
                                        b2[:, :, C - 1:C].broadcast_to((P, NCH, C)), b2, ALU.subtract
                                        ).then_inc(s["dec_in"], 1)
                for l in range(LEVELS - 1, -1, -1):
                    m = 1 << l
                    bb = b.rearrange("p (b h m) -> p b h m", h=2, m=m)
                    x = dv[:, l].rearrange("p (b h m) -> p b h m", h=2, m=m)
                    ref = bb[:, :, 0, m - 1:m].broadcast_to((P, T // (2 * m), m))
                    nc.vector.tensor_tensor(x[:, :, 0], ref, bb[:, :, 0], ALU.subtract)
                    nc.vector.tensor_tensor(x[:, :, 1], bb[:, :, 1], ref, ALU.subtract).then_inc(s["dec_in"], 1)

            def gather_scores(i, sc):
                for n, l in enumerate(list(range(LEVELS - 1, -1, -1)) + [LEVELS]):
                    dve.wait_ge(s["score_ps"], i * 8 + (n + 1))
                    if n:
                        dve.wait_ge(s["scores"], i * 8 + n)
                    mk = lvl_mask[:, l:l + 1].broadcast_to((P, NCH, P))
                    sv = sc.rearrange("p (c t) -> p c t", c=NCH)
                    pv = ps[:, 4 + n % 2].rearrange("p (c t) -> p c t", c=NCH)
                    if n == 0:
                        nc.vector.tensor_tensor(sv, pv, mk, ALU.mult).then_inc(s["scores"], 1)
                    else:
                        nc.vector.memset(waited[:], 0.0)
                        nc.vector.copy_predicated(sv, mk.bitcast(U32), pv).then_inc(s["scores"], 1)

            def chain_states(i, it, stv, ends):
                dve.wait_ge(s["st_ps"], i + 1)
                nc.vector.tensor_copy(stv[:, 1], ps[:, 6, 0:C]).then_inc(s["states"], 1)
                for c in (1, 2):
                    dve.wait_ge(s["states"], i * 3 + c)
                    dve.wait_ge(s["chunk_decay"], it + 1)
                    nc.vector.scalar_tensor_tensor(out=stv[:, c + 1], in0=stv[:, c], scalar=ends[:, c:c + 1],
                                                   in1=ps[:, 6, c * C:(c + 1) * C], op0=ALU.mult, op1=ALU.add
                                                   ).then_inc(s["states"], 1)

            def head_output(i, gain, r, tmp, gate, dst, done):
                dve.wait_ge(s["o_rstd"], i * 2 + 2)
                nc.vector.scalar_tensor_tensor(out=tmp, in0=ps[:, 7], scalar=gain[:, 0:1], in1=r,
                                               op0=ALU.mult, op1=ALU.mult).then_inc(s["o_scaled"], 1)
                dve.wait_ge(s["o_scaled"], i + 1)
                nc.vector.tensor_tensor(dst, tmp, gate, ALU.mult).then_inc(done, 1)

            norm(0)
            with dve.Fori(0, HEADS_H) as i:
                dve.wait_ge(s["sig_f"], i + 1)
                nc.vector.tensor_scalar(fg, sf_, omlb[:, bass.ds(i, 1)], lb[:, bass.ds(i, 1)], ALU.mult, ALU.add
                                        ).then_inc(s["forget"], 1)
                dve.wait_ge(s["forget"], i + 1)
                nc.vector.tensor_scalar(key, fg, -1.0, 1.0, ALU.mult, ALU.add).then_inc(s["key"], 1)
                dve.wait_ge(s["sig_q"], i + 1)
                nc.vector.tensor_tensor(qry, sq_, ps[:, 0], ALU.mult).then_inc(s["query"], 1)
                dve.wait_ge(s["sig_g"], i + 1)
                nc.vector.tensor_tensor(sgl, sg_, ps[:, 2], ALU.mult).then_inc(s["silu_g"], 1)
                dve.wait_ge(s["log_f"], i + 1)
                exponents(i, bcum, lf, dec)
                gather_scores(i, sc_mat)
                chain_states(i, i, st, chd)
                head_output(i, hgain, ors, otmp, sgl, O[:, bass.ds(i, 1)].rearrange("p a t -> p (a t)"), s["o_ready"])
            residual("hgrn_out", 0, 1, 0, RING)
            norm(1)
            ffn(0, 1)

            norm(2)

            def rope(N):
                dve.wait_ge(s["rot_ps"], N + 1)
                nc.vector.tensor_tensor(tsin[:, N % 2], ps[:, 2 + N % 2], sin_a[:], ALU.mult).then_inc(s["rope_sin"], 1)
                dve.wait_ge(s["rope_sin"], N + 1)
                dve.wait_ge(s["rope_cos"], N + 1)
                nc.vector.tensor_tensor(QK[N // 6 % 2][:, N % 6], tcos[:, N % 2], tsin[:, N % 2], ALU.add
                                        ).then_inc(s["qk_ready"], 1)

            for n in range(6):
                rope(n)
            for j in range(HPG):
                N = 6 * (j + 1)
                if j + 1 < HPG:
                    rope(N)
                    rope(N + 1)
                for g in range(GROUPS):
                    dve.wait_ge(s["sc_ps"], 3 * j + g + 1)
                    if g == 0:
                        nc.vector.scalar_tensor_tensor(out=SC[0], in0=SC_BANKS[0], scalar=float(P) ** -0.5,
                                                       in1=win_mask[:], op0=ALU.mult, op1=ALU.add
                                                       ).then_inc(s["sc_masked"], 1)
                    else:
                        nc.vector.scalar_tensor_tensor(out=SC[g], in0=SC_BANKS[g], scalar=float(P) ** -0.5,
                                                       in1=res_mask[:, g - 1:g].broadcast_to((P, TT, P)),
                                                       op0=ALU.mult, op1=ALU.add).then_inc(s["sc_masked"], 1)
                    dve.wait_ge(s["sc_masked"], 3 * j + g + 1)
                    nc.vector.tensor_reduce(mx[:, g], SC[g], AX.X, ALU.max).then_inc(s["sc_max"], 1)
                    dve.wait_ge(s["sc_max"], 3 * j + g + 1)
                    nc.vector.tensor_scalar(nmx[:, g], mx[:, g], -1.0, None, ALU.mult).then_inc(s["sc_negmax"], 1)
                dve.wait_ge(s["p_exp"], 12 * (j + 1))
                nc.vector.reciprocal(lrec, lsum).then_inc(s["p_recip"], 1)
                dve.wait_ge(s["p_logsum"], j + 1)
                nc.vector.tensor_tensor(lsev, lsev, mx, ALU.add).then_inc(s["lse"], 1)
                if j + 1 < HPG:
                    for n in range(2, 6):
                        rope(N + n)
                dve.wait_ge(s["lse_rows"], 3 * j + 3)
                nc.vector.tensor_tensor(mxw, lrow[:, 0], lrow[:, 1], ALU.max).then_inc(s["mix_max1"], 1)
                dve.wait_ge(s["mix_max1"], j + 1)
                nc.vector.tensor_tensor(mxw, mxw, lrow[:, 2], ALU.max).then_inc(s["mix_max"], 1)
                dve.wait_ge(s["mix_exp"], j + 1)
                nc.vector.tensor_tensor(sum_, lrow[:, 0], lrow[:, 1], ALU.add).then_inc(s["mix_sum1"], 1)
                dve.wait_ge(s["mix_sum1"], j + 1)
                nc.vector.tensor_tensor(sum_, sum_, lrow[:, 2], ALU.add).then_inc(s["mix_sum"], 1)
                dve.wait_ge(s["mix_sum"], j + 1)
                nc.vector.reciprocal(rec, sum_).then_inc(s["mix_recip"], 1)
                dve.wait_ge(s["mix_weight"], j + 1)
                for g in range(GROUPS):
                    dve.wait_ge(s["ao_ps"], 3 * j + g + 1)
                    n = TT if g == 0 else P
                    nc.vector.tensor_tensor(aO[:, g * HPG + j].rearrange("p (b m) -> p b m", b=n), natural(g, ps[:, 4 + g]),
                                            lrow[:, g].rearrange("p (b m) -> p b m", b=n), ALU.mult
                                            ).then_inc(s["ao_ready"], 1)
            residual("attn_out", 2, 1, 0, RING)
            norm(3)
            ffn(1, 3)

            norm(4, h, s["h_ready"])
            norm(5)

            def nsa_rope(x):
                n = (0, 1, 2, 3, 6, 7)[x]
                dve.wait_ge(s["nrot_ps"], x + 1)
                nc.vector.tensor_tensor(nsin[:, x % 2], ps[:, 2 + x % 2], sin_n[:], ALU.mult).then_inc(s["nrope_sin"], 1)
                dve.wait_ge(s["nrope_sin"], x + 1)
                dve.wait_ge(s["nrope_cos"], x + 1)
                dst = qrot[:, n] if n < 4 else kr[:, n - 6]
                nc.vector.tensor_tensor(dst, ncos[:, x % 2], nsin[:, x % 2], ALU.add).then_inc(s["nrope"], 1)

            for x in range(4):
                nsa_rope(x)
            dve.wait_ge(s["kvpe_zero"], 2)
            for x in range(2):
                dve.wait_ge(s["nt_ready"], 5 + x)
                for g in range(2):
                    src = slice(g * HD, (g + 1) * HD)
                    kv = kvraw[src, x].rearrange("p (n l o) -> p o l n", l=8, o=2)
                    pos = pos_kv[src, x].rearrange("p (l o) -> p o l", o=2)
                    for odd in range(2):
                        for hi in range(2):
                            dst = kvp[odd * HD:(odd + 1) * HD, x, 8 * hi:8 * hi + 8, g * NB:g * NB + 31]
                            nc.vector.tensor_tensor(dst, kv[:, odd, :, hi:hi + 31],
                                                    pos[:, odd, 8 * hi:8 * hi + 8, None].broadcast_to((HD, 8, 31)),
                                                    ALU.add).then_inc(s["kvpe"], 1)
            for x in (4, 5):
                nsa_rope(x)
            for x in range(2):
                dve.wait_ge(s["hid_sig"], x + 1)
                if x == 0:
                    nc.vector.tensor_tensor(hidk, hsig[:, 0], ps[:, 1, 0:2 * NB], ALU.mult).then_inc(s["hid"], 1)
                else:
                    for g in range(2):
                        src = slice(g * NB, (g + 1) * NB)
                        m = nc.vector.tensor_tensor(hidv[:, g * P:(g + 1) * P].rearrange("p (k n) -> p k n", k=4),
                                                    hsig[:, 1, None, src].broadcast_to((P, 4, NB)),
                                                    ps[:, 0, src][:, None, :].broadcast_to((P, 4, NB)), ALU.mult)
                    m.then_inc(s["hid"], 1)
            dve.wait_ge(s["gz_ps"], 1)
            for p in range(2):
                nc.vector.tensor_scalar(la[:, p], ps[:, 2 + p], gbias[:, p:p + 1], None, ALU.add).then_inc(s["z_b"], 1)
            for p in range(2):
                dve.wait_ge(s["z_ln"], p + 1)
                nc.vector.scalar_tensor_tensor(out=la[:, p], in0=la[:, p], scalar=0.0, in1=zab, op0=ALU.min,
                                               op1=ALU.subtract).then_inc(s["z_min"], 1)
                dve.wait_ge(s["z_min"], p + 1)
                nc.vector.tensor_scalar(la[:, p], la[:, p], 1.0 / TAU, None, ALU.mult).then_inc(s["log_a"], 1)
            SH = (P, TT, HEADS_N, NB)
            cs = ps[:, 4:6].rearrange("p g (t h n) -> p g t h n", t=TT, h=4)
            mk = cmp_mask[:].rearrange("p k (t n) -> p k t n", t=TT)
            dve.wait_ge(s["cs_ps"], 1)
            for g in range(2):
                nc.vector.tensor_tensor(sC[:, :, 4 * g:4 * g + 4], cs[:, g], mk[:, 0, :, None, :].broadcast_to((P, TT, 4, NB)),
                                        ALU.add).then_inc(s["cs_masked"], 1)
            dve.wait_ge(s["cs_masked"], 2)
            nc.vector.tensor_reduce(cmx, sC, AX.X, ALU.max).then_inc(s["cs_max"], 1)
            dve.wait_ge(s["cs_max"], 1)
            nc.vector.tensor_tensor(sC, sC, cmx[:, :, :, None].broadcast_to(SH), ALU.subtract).then_inc(s["cs_sub"], 1)
            dve.wait_ge(s["cs_exp"], 1)
            nc.vector.tensor_reduce(csum, sC, AX.X, ALU.add).then_inc(s["cs_sum"], 1)
            dve.wait_ge(s["cs_sum"], 1)
            nc.vector.reciprocal(crec, csum).then_inc(s["cs_rec"], 1)
            nc.vector.tensor_tensor(sC, sC, mk[:, 1, :, None, :].broadcast_to(SH), ALU.mult).then_inc(s["cs_valid"], 1)
            dve.wait_ge(s["cs_rec"], 1)
            dve.wait_ge(s["ngate_ready"], TT)
            nc.vector.tensor_tensor(cw, crec, ngate.rearrange("p t (h b) -> p t h b", b=3)[:, :, :, 0], ALU.mult
                                    ).then_inc(s["cs_gate"], 1)
            dve.wait_ge(s["cs_gate"], 1)
            dve.wait_ge(s["cs_valid"], 1)
            nc.vector.tensor_tensor(sC, sC, cw[:, :, :, None].broadcast_to(SH), ALU.mult).then_inc(s["cs_w"], 1)

            def nsa_stats(i, x):
                base = ps[:, 3 * x:3 * x + 3].rearrange("p a n -> p (a n)")
                dve.wait_ge(s["ns_ps"], i * 2 + (x + 1))
                for tt in range(TT):
                    diag = base[:, BOFF[tt] + tt * P:BOFF[tt] + (tt + 1) * P]
                    nc.vector.tensor_tensor(diag, diag, res_mask[:, 0], ALU.add).then_inc(s["ns_masked"], 1)
                for tt in range(TT):
                    dve.wait_ge(s["ns_masked"], i * 8 + (4 * x + tt + 1))
                    nc.vector.tensor_reduce(nmax[:, x, tt:tt + 1], base[:, BOFF[tt]:BOFF[tt] + (tt + 1) * P], AX.X, ALU.max
                                            ).then_inc(s["ns_max"], 1)
                dve.wait_ge(s["ns_max"], i * 8 + (4 * x + 4))
                nc.vector.tensor_scalar(nneg[:, x], nmax[:, x], -1.0, None, ALU.mult).then_inc(s["ns_neg"], 1)

            def nsa_weight(i, x):
                dve.wait_ge(s["ns_exp"], i * 8 + (4 * x + 4))
                nc.vector.reciprocal(nrec[:, x], nsum[:, x]).then_inc(s["n_rec"], 1)
                dve.wait_ge(s["n_rec"], i * 2 + (x + 1))
                nc.vector.tensor_tensor(nw[:, x, :, None], nrec[:, x, :, None], ngate[:, :, bass.ds(i * 3 + (1 + x), 1)],
                                        ALU.mult).then_inc(s["n_w"], 1)

            def nsa_add(i, x):
                dve.wait_ge(s["n_w"], i * 2 + (x + 1))
                dve.wait_ge(s["no_ps"], i * 2 + (x + 1))
                nc.vector.tensor_tensor(oscl, ps[:, 6 + x, 0:TT * HD].rearrange("p (t d) -> p t d", t=TT),
                                        nw[:, x, :, None].broadcast_to((P, TT, HD)), ALU.mult).then_inc(s["n_scaled"], 1)
                dve.wait_ge(s["n_scaled"], i * 2 + (x + 1))
                o = oa[:, :, bass.ds(i * HD, HD)]
                nc.vector.tensor_tensor(o, o, oscl, ALU.add).then_inc(s["oa_acc"], 1)

            dve.wait_ge(s["oa_ready"], TT)
            nsa_stats(0, 0)
            nsa_stats(0, 1)
            with dve.Fori(0, HEADS_N - 1) as i:
                for x in range(2):
                    nsa_weight(i, x)
                    nsa_stats(i + 1, x)
                    nsa_add(i, x)
            for x in range(2):
                nsa_weight(HEADS_N - 1, x)
                nsa_add(HEADS_N - 1, x)

            dve.wait_ge(s["oat_ready"], 4)
            for p in range(2):
                dve.wait_ge(s["log_a"], p + 1)
                exponents(HEADS_H + p, gcum[:, p], la[:, p], gdec[p])
            for n in range(HEADS_G):
                dve.wait_ge(s["gr_sig"], n + 1)
                nc.vector.tensor_tensor(gsr[:, n], gsig[:, n % 2], ps[:, n], ALU.mult).then_inc(s["gr_silu"], 1)
            dve.wait_ge(s["gr_silu"], HEADS_G)
            for hh in range(HEADS_G):
                gather_scores(HEADS_H + hh, gsc)
                chain_states(HEADS_H + hh, HEADS_H + hh // 2, gst, gchd[:, hh // 2])
                head_output(HEADS_H + hh, ggain, gors, gotmp, gsr[:, hh], goT[:, hh], s["gb_ready"])

            with dve.Fori(0, 2) as i:
                for j in range(4):
                    b, x = 4 * (j % 2), 2 * (j % 2)
                    dve.wait_ge(s["w_used"], i * 12 + (FIRST["merge"] + 3 * j + 3))
                    dve.wait_ge(s["mg_sig"], i * 8 + (2 * j + 2))
                    nc.vector.tensor_tensor(msig[:, x], msig[:, x], ps[:, b + 2], ALU.mult).then_inc(s["mg_a"], 1)
                    nc.vector.tensor_tensor(msig[:, x + 1], msig[:, x + 1], ps[:, b + 3], ALU.mult).then_inc(s["mg_b"], 1)
                    dve.wait_ge(s["mg_a"], i * 4 + (j + 1))
                    dve.wait_ge(s["mg_b"], i * 4 + (j + 1))
                    nc.vector.tensor_tensor(mrg[:, bass.ds(i * 4 + j, 1)].rearrange("p a t -> p (a t)"), msig[:, x],
                                            msig[:, x + 1], ALU.add).then_inc(s["merged"], 1)
            residual("mix_out", 5, 1, 0, RING)
            norm(6)
            ffn(2, 6)
            norm(7, h, s["credit"])


def kernel(**inputs):
    import numpy as np
    from concourse import bacc
    from concourse.bass_utils import run_bass_kernel_spmd

    g = {n: np.asarray(v) for n, v in inputs.items()}

    def fm(w):
        K, N = w.shape
        return np.ascontiguousarray(w.reshape(K // P, P, N // P, P).transpose(2, 1, 0, 3).reshape(N // P, P, K))

    def down(w):
        return np.ascontiguousarray(w.reshape(2, 11, P, DC, P).transpose(3, 0, 2, 1, 4).reshape(2 * DC, P, 11 * P))

    def cols(v):
        return v.reshape(-1, P).T

    arrays = {"x": np.ascontiguousarray(g["x"][0].reshape(T, DC, P).transpose(2, 1, 0))}
    w = fm(g["hgrn_w_in"][0]).reshape(4, 8, P, D)
    arrays["w_hgrn"] = np.ascontiguousarray(w[[1, 0, 3, 2]].transpose(1, 0, 2, 3).reshape(32, P, D))
    arrays["w_hgrn_out"] = fm(g["hgrn_w_out"][0])
    ffns = [(g["ffn_w_in"][n][:, :FF], g["ffn_w_in"][n][:, FF:], g["ffn_w_down"][n]) for n in range(2)]
    ffns.append((g["w_ffn_gate_2"][0], g["w_ffn_up_2"][0], g["w_ffn_down_2"][0]))
    for n, (gate, up, w_down) in enumerate(ffns):
        arrays[f"w_gu{n}"] = np.ascontiguousarray(np.stack([fm(gate), fm(up)], 1).reshape(2 * FC, P, D))
        arrays[f"w_down{n}"] = down(w_down)

    def tm(w):
        return np.ascontiguousarray(w.reshape(4, 2, P, -1).transpose(0, 2, 1, 3).reshape(4, P, -1))

    AW = GROUPS * HPG * P
    qkv = g["attn_w_qkv"][0]
    arrays["w_attn_v"] = np.concatenate([tm(qkv[:, 2 * AW + n * 512:2 * AW + (n + 1) * 512]) for n in range(GROUPS)])
    w = fm(qkv[:, :2 * AW]).reshape(2, GROUPS, HPG, P, D)
    arrays["w_attn_qk"] = np.ascontiguousarray(w.transpose(2, 1, 0, 3, 4).reshape(24, P, D))
    arrays["w_attn_out"] = fm(g["attn_w_out"][0])
    arrays["gains"] = np.ascontiguousarray(np.stack([cols(v) for v in (
        g["norm_mix"][0], g["norm_ffn"][0], g["norm_mix"][1], g["norm_ffn"][1], g["final_norm"],
        g["norm_mix_2"][0], g["norm_ffn_2"][0], g["norm_final_2"])], 1))
    arrays["lbl"] = np.ascontiguousarray(g["hgrn_lb_logits"].reshape(3, DC, P).transpose(2, 0, 1))
    arrays["hgain"] = np.ascontiguousarray(g["hgrn_out_norm"].reshape(P, 1))
    arrays["ident"] = np.eye(P, dtype=np.float32)
    arrays["ones"] = np.ones((P, P), np.float32)
    si, ti = np.arange(P)[:, None], np.arange(P)[None, :]
    masks = [(si // (2 << l) == ti // (2 << l)) & (si // (1 << l) % 2 == 0) & (ti // (1 << l) % 2 == 1)
             for l in range(LEVELS)] + [si == ti]
    arrays["lvl_mask"] = np.ascontiguousarray(np.stack(masks, 1).astype(np.float32))
    arrays["reset"] = np.ascontiguousarray(np.broadcast_to((np.arange(T) % C != 0).astype(np.float32), (P, T)))

    w = g["w_in_2"][0]
    cuts = np.cumsum([0, HEADS_N * HD, 12 * HD, 3 * HEADS_N, HEADS_G * HD, HEADS_G * HD, HEADS_G * P, RANK,
                      HEADS_G * P, 2 * D])
    wq, wkv, wgate, wgq, wgk, wgv, wlr, wr, wmerge = [w[:, lo:hi] for lo, hi in zip(cuts[:-1], cuts[1:])]
    wq = wq.reshape(D, 2, 4, HD).transpose(0, 2, 1, 3).reshape(D, 512)
    kv = [wkv[:, n * P:(n + 1) * P] for n in range(6)]
    arrays["w_nsa_fm"] = fm(np.concatenate([wq, kv[0], kv[1], kv[2], kv[4]], 1))
    w = np.concatenate([kv[3], kv[5], wgate], 1)
    arrays["w_nsa_tm"] = np.ascontiguousarray(w.reshape(2, 4, P, TM_COLS).transpose(0, 2, 1, 3).reshape(2, P, -1))
    arrays["w_gla_v"] = tm(wgv)
    arrays["w_gla_fm"] = fm(np.concatenate([wgq, wgk], 1))
    arrays["w_gla_lr"] = np.ascontiguousarray(wlr.reshape(DC, P, RANK).transpose(1, 0, 2).reshape(1, P, -1))
    arrays["w_gla_r"] = fm(wr)
    up = np.concatenate([g["w_up_nsa_2"][0], g["w_up_gla_2"][0]], 0)
    arrays["w_merge"] = np.ascontiguousarray(
        np.stack([fm(wmerge[:, :D]), fm(wmerge[:, D:]), fm(up)], 1).reshape(3 * DC, P, D))
    arrays["w_mix_out"] = fm(g["w_out_2"][0])
    arrays["cmp_w1"] = np.ascontiguousarray(np.stack(
        [g[n][0].reshape(16, P, P).transpose(1, 0, 2) for n in ("cmp_k_w1_2", "cmp_v_w1_2")], 1))
    zero = np.zeros((P, HD), np.float32)
    arrays["cmp_w2k"] = np.ascontiguousarray(np.concatenate([zero, g["cmp_k_w2_2"][0], zero], 1))
    arrays["cmp_w2v"] = np.ascontiguousarray(g["cmp_v_w2_2"][0])
    arrays["pos_kv"] = np.ascontiguousarray(np.stack(
        [np.concatenate([g[n][0].T] * 2) for n in ("cmp_pe_k_2", "cmp_pe_v_2")], 1))
    arrays["gw2"] = np.ascontiguousarray(g["gla_gate_w2_2"][0])
    arrays["gbias"] = np.ascontiguousarray(g["gla_gate_b_2"][0].reshape(2, P).T)
    arrays["ggain"] = np.ascontiguousarray(g["gla_norm_2"].reshape(P, 1))
    half = 8
    rot = np.zeros((P, P), np.float32)
    for base in (0, HD):
        for m in range(half):
            rot[base + m + half, base + m], rot[base + m, base + m + half] = -1.0, 1.0
    arrays["rot_n"] = rot
    inv = (np.float32(500000.0) ** (-np.arange(half, dtype=np.float32) / np.float32(half))).astype(np.float32)
    ang = (np.arange(T, dtype=np.float32)[None, :] * inv[:, None]).astype(np.float32)
    one, nil = np.ones((HD - 2 * half, T), np.float32), np.zeros((HD - 2 * half, T), np.float32)
    arrays["cos_n"] = np.concatenate([np.cos(ang), np.cos(ang), one] * 2).astype(np.float32)
    arrays["sin_n"] = np.concatenate([np.sin(ang), np.sin(ang), nil] * 2).astype(np.float32)
    blk = np.arange(NB)
    seen = (blk * 16 + 31 <= np.arange(T)[:, None]) & (blk < NB - 1)
    seen = seen.reshape(TT, P, NB).transpose(1, 0, 2).reshape(P, TT * NB)
    arrays["cmp_mask"] = np.ascontiguousarray(np.stack([np.where(seen, 0.0, NEG), seen], 1).astype(np.float32))
    rot = np.zeros((P, P), np.float32)
    for m in range(64):
        rot[m + 64, m], rot[m, m + 64] = -1.0, 1.0
    arrays["rot_a"] = rot
    inv = (1.0 / (np.float32(10000.0) ** (np.arange(0, P, 2, dtype=np.float32) / np.float32(P)))).astype(np.float32)
    ang = (np.arange(T, dtype=np.float32)[None, :] * inv[:, None]).astype(np.float32)
    arrays["cos_a"] = np.concatenate([np.cos(ang)] * 2).astype(np.float32)
    arrays["sin_a"] = np.concatenate([np.sin(ang)] * 2).astype(np.float32)
    cur, prev = si >= ti, si <= ti
    first = np.concatenate([np.zeros((P, P), bool), cur], 1)
    later = np.concatenate([prev, cur], 1)
    arrays["win_mask"] = np.ascontiguousarray(
        np.where(np.stack([first, later, later, later], 1), 0.0, NEG).astype(np.float32))
    arrays["res_mask"] = np.ascontiguousarray(
        np.where(np.stack([cur, cur & (si % 4 == ti % 4)], 1), 0.0, NEG).astype(np.float32))

    nc = bacc.Bacc("TRN2", target_bir_lowering=False, num_devices=1)
    aps = {n: nc.dram_tensor("in_" + n, v.shape, F32, kind="ExternalInput").ap() for n, v in arrays.items()}
    out = nc.dram_tensor("out_h", (P, DC, T), F32, kind="ExternalOutput").ap()
    program(nc, aps, out)
    r = run_bass_kernel_spmd(nc, [{"in_" + n: v for n, v in arrays.items()}], core_ids=[0])
    y = r.results[0]["out_h"]
    return np.ascontiguousarray(y.transpose(2, 1, 0).reshape(1, T, D))
```

```python
import concourse.bass as bass
from concourse import mybir
from contextlib import ExitStack

F32 = mybir.dt.float32
R32 = mybir.dt.float32r
U32 = mybir.dt.uint32
ALU = mybir.AluOpType
ACT = mybir.ActivationFunctionType
AX = mybir.AxisListType

P = 128
T = 512
D = 1024
DC = D // P
TT = T // P
FF = 2816
FC = FF // P
HEADS_H = 8
C = 128
NCH = T // C
LEVELS = 7
NORMS = 8
GROUPS = 3
HPG = 4
RESIDUES = 4
NEG = -1e30
HEADS_N = 8
HD = 64
NB = 32
TM_COLS = 2 * P + 3 * HEADS_N
HEADS_G = 4
RANK = 16
TAU = 16.0
EPS = 1e-6
RING = 4
SLOT = 11 * P
HC = FC // 2
ARENA = 28832
H_AT = ARENA - DC * T

SECTIONS = [
    ("hgrn", 4 * HEADS_H, 8 * P), ("hgrn_out", DC, 8 * P),
    ("gu0a", 2 * HC, 8 * P), ("down0a", DC, HC * P), ("gu0b", 2 * HC, 8 * P), ("down0b", DC, HC * P),
    ("attn_v", 4 * GROUPS, 8 * P), ("attn_qk", 2 * GROUPS * HPG, 8 * P), ("attn_out", 2 * DC, 6 * P),
    ("gu1a", 2 * HC, 8 * P), ("down1a", DC, HC * P), ("gu1b", 2 * HC, 8 * P), ("down1b", DC, HC * P),
    ("nsa_fm", 8, 8 * P), ("nsa_tm", 2, 4 * TM_COLS), ("gla_v", 4, 8 * P), ("gla_fm", 4, 8 * P),
    ("gla_lr", 1, 8 * P), ("gla_r", HEADS_G, 8 * P), ("merge", 3 * DC, 8 * P), ("mix_out", DC, 8 * P),
    ("gu2a", 2 * HC, 8 * P), ("down2a", DC, HC * P), ("gu2b", 2 * HC, 8 * P), ("down2b", DC, HC * P),
]
WIDTH = {name: width for name, _, width in SECTIONS}
FIRST = {}
_n = 0
for _name, _units, _ in SECTIONS:
    FIRST[_name] = _n
    _n += _units


SPLIT = [(name, k) for name, units, _ in SECTIONS for k in range(units)
         if name != "attn_out" and not (name == "merge" and k % 3 == 2)]
SPLIT_AT = {unit: n for n, unit in enumerate(SPLIT)}


def split_use(section, k, i=None, per=0):
    n = SPLIT_AT[(section, k)]
    done = n + 1 if i is None else i * per + (n + 1)
    if n < 2:
        return n % 2, done, None
    last, lk = SPLIT[n - 2]
    free = FIRST[last] + lk + 1
    return n % 2, done, free if i is None else i * per + free


def ring_use(section, k, i=None, per=0):
    n = FIRST[section] + k
    count = 16 * (n // RING + 1)
    return n % RING, count if i is None else i * (16 * per // RING) + count


def program(nc, a, out):
    names = """x_loaded consts_loaded w_hi w_lo u_tmp u_hi u_lo_even u_lo_odd g_full g_hi g_lo o_full o_hi o_lo
        m_full m_hi m_lo spilled reloaded nsa_consts w_used h_ready sq_ready ms_ready rstd lb_steps 
        sig_f sig_q sig_g vf_ready forget key query silu_g log_f cum dec_in dec_out chunk_decay
        x_ready vt_ps vt_ready kt_ps kt_ready score_ps scores st_ps states o_ps o_sq o_ms o_rstd o_scaled 
        gate_sig gate_silu stored credit
        av_ready raw_ready rot_ps rope_cos rope_sin qk_ready sc_ps sc_masked sc_max sc_negmax p_exp p_logsum
        p_recip lse lse_diag p_norm pt_ps pt_ready lse_ps lse_rows ao_ps mix_max1 mix_max mix_diff mix_exp mix_sum1
        mix_sum mix_recip mix_weight ao_ready
        nt_ready nrot_ps nrope_cos nrope_sin nrope ntm_ready ngate_ready gv_ready cmp_loaded kvpe_zero kvpe hid_ps
        hid_sig hid kc_ps kc_ready vc_ps vbd cs_ps cs_masked cs_max cs_sub cs_exp cs_sum cs_rec cs_gate cs_valid cs_w
        ct_ps ct_ready co_ps oa_ready ns_ps ns_masked ns_max ns_neg ns_exp nt_ps npt_ready no_ps n_rec n_w n_scaled
        oa_acc oat_ps oat_ready gz_ps z_b z_abs z_exp z_ln z_min log_a gr_sig gr_silu gb_ready mg_sig mg_a 
        merged""".split()
    with ExitStack() as ctx:
        def sb(name, *shape):
            return ctx.enter_context(nc.sbuf_tensor(name, [P, *shape], F32))

        s = {n: ctx.enter_context(nc.semaphore(n)) for n in names}
        w_ready = [ctx.enter_context(nc.semaphore(f"w_ready{r}")) for r in range(RING)]

        arena_at = (nc.sbuf_base + 31) // 32 * 32
        arena = sb("arena", ARENA)
        h = arena[:, H_AT:ARENA].rearrange("p (c t) -> p c t", c=DC)
        hid = nc.alloc_sbuf_tensor_at("hid", [P, 2, HC, T], R32, offset=arena_at)
        us = ctx.enter_context(nc.sbuf_tensor("u_split", [P, 2, DC, T], R32))
        ws = ctx.enter_context(nc.sbuf_tensor("w_split", [P, 2, 2, SLOT], R32))
        ring = sb("ring", RING, SLOT)
        rs = sb("rs_norm", T)
        gains = sb("gains_sb", NORMS, DC)
        ident = sb("ident_sb", P)
        ones = sb("ones_sb", P)
        lvl_mask = sb("lvl_mask_sb", LEVELS + 1, P)
        reset = sb("reset_sb", T)
        lbl = sb("lbl_sb", 3, DC)
        lbt = sb("lbt", 8, DC)
        small = sb("small", 16)
        hgain, ggain, eps, waited = [small[:, n:n + 1] for n in range(4)]
        gbias, start = small[:, 4:6], small[:, 8:12]
        mixer_consts = sb("mixer_consts", 2 * T + 9 * P)
        rot_a = mixer_consts[:, 0:P]
        cos_a = mixer_consts[:, P:P + T]
        sin_a = mixer_consts[:, P + T:P + 2 * T]
        win_mask = mixer_consts[:, P + 2 * T:P + 4 * T].rearrange("p (b n) -> p b n", b=TT)
        res_mask = sb("res_mask_sb", 2, P)
        rot_n, cos_n, sin_n = rot_a, cos_a, sin_a
        at = P + 2 * T
        cmp_mask = mixer_consts[:, at:at + 2 * TT * NB].rearrange("p (k n) -> p k n", k=2)
        pos_kv = mixer_consts[:, at + 256:at + 320].rearrange("p (k n) -> p k n", k=2)
        gw2 = mixer_consts[:, at + 320:at + 576]
        ps = ctx.enter_context(nc.psum_tensor("ps", [P, 8, 512], F32))

        def views(used=0):
            at = [used]

            def take(*shape):
                n = 1
                for x in shape:
                    n *= x
                v = arena[:, at[0]:at[0] + n]
                at[0] += n
                assert at[0] <= ARENA, at[0]
                if len(shape) == 2:
                    v = v.rearrange("p (a b) -> p a b", a=shape[0])
                if len(shape) == 3:
                    v = v.rearrange("p (a b c) -> p a b c", a=shape[0], b=shape[1])
                return v
            return take

        take = views(used=2 * HC * T)
        sq_, sf_, sg_ = take(T), take(T), take(T)
        vf, fg, key, qry, lf = take(T), take(T), take(T), take(T), take(T)
        sgl, bcum = take(T), take(T)
        dec = take(LEVELS + 2, T)
        vT = take(NCH, C)
        kT = take(NCH, C)
        sc_mat = take(T)
        st = take(NCH, P)
        chd = take(NCH)
        osq, ors, otmp = take(T), take(T), take(T)
        L_END, L_STATE = LEVELS, LEVELS + 1

        take = views(used=2 * HC * T)
        sgate, gtmp = take(2, T), take(2, T)
        nsq, utmp = take(4, T), take(4, T)

        omlb, lb = lbt[:, 6], lbt[:, 5]
        take = views()
        aO = take(GROUPS * HPG, T)
        aV = take(GROUPS, TT * T).rearrange("p g (b n) -> p g b n", b=TT)
        QK = [take(2 * GROUPS, T) for _ in range(2)]
        raw, tcos, tsin = take(2, T), take(2, T), take(2, T)
        scm = take(4 * T)
        PTs = take(4 * T)
        lrow = take(GROUPS, T)
        dgl = take(GROUPS * TT, P)
        mxw, sum_, rec = [dgl.rearrange("p a n -> p (a n)")[:, n * T:(n + 1) * T] for n in range(3)]
        mx, nmx, lsum, lrec, lsev = [take(GROUPS, TT) for _ in range(5)]
        SC = [scm[:, 0:1024].rearrange("p (b n) -> p b n", b=4), scm[:, 1024:1536].rearrange("p (b n) -> p b n", b=4),
              scm[:, 1536:2048].rearrange("p (b n) -> p b n", b=4)]
        SC_BANKS = [ps[:, 4:6].rearrange("p a (b n) -> p (a b) n", b=2), ps[:, 6].rearrange("p (b n) -> p b n", b=4),
                    ps[:, 7].rearrange("p (b n) -> p b n", b=4)]

        take = views()
        NSA_OWN = 21300
        take = views(used=NSA_OWN)
        oaT = take(4, T)
        assert NSA_OWN + 4 * T <= H_AT
        qg, kg = take(2, T), take(2, T)
        vG = take(TT, HEADS_G * P)
        la = take(2, T)
        take = views()
        qraw, qrot = take(4, T), take(4, T)
        kvraw, kraw, kr = take(2, T), take(2, T), take(2, T)
        vsw = take(TT, 2 * P)
        ngate = take(TT, 3 * HEADS_N)
        lrS = take(T)
        zab = take(T)
        hidv, hsig = take(4 * 2 * NB), take(2, 2 * NB)
        hidk = take(2 * NB)
        kc = take(NB)
        vbd = take(2, 4 * HD)
        over = take(4 * T)
        ncos, nsin = [over[:, k * 2 * T:(k + 1) * 2 * T].rearrange("p (a n) -> p a n", a=2) for k in range(2)]
        sC = over[:, 0:2 * T].rearrange("p (t h n) -> p t h n", t=TT, h=HEADS_N)
        PTc = over[:, 2 * T:4 * T].rearrange("p (k n) -> p k n", k=2 * TT)
        oa = take(TT, HEADS_N * HD)
        oscl = take(TT, HD)
        cmx, csum, crec, cw = [take(TT, HEADS_N) for _ in range(4)]
        nmax, nneg, nsum, nrec, nw = [take(2, TT) for _ in range(5)]
        w2k, w2v = take(3 * HD), take(HD)
        shared = take(6144)
        w1 = shared[:, 0:4096].rearrange("p (x l m) -> p x l m", x=2, l=16)
        kvp = shared[:, 4096:6144].rearrange("p (x l n) -> p x l n", x=2, l=16)
        prob, probT = [shared[:, k * 2560:(k + 1) * 2560].rearrange("p (a n) -> p a n", a=2) for k in range(2)]
        OFF = [0, P, 3 * P, 6 * P]
        BOFF = [0, P, 512, 1024]

        take = views()
        gcum = take(2, T)
        gdec = [take(LEVELS + 2, T) for _ in range(2)]
        gkT = take(2, 3 * P)
        gchd = take(2, NCH)
        gsc, gst = take(T), take(NCH, P)
        gsig = take(2, T)
        gsr = take(HEADS_G, T)
        GO_AT = (2 + 2 * (LEVELS + 2)) * T + 6 * P + 2 * NCH + T + NCH * P + 6 * T
        goT = take(HEADS_G, T)
        gosq, gors, gotmp = take(T), take(T), take(T)
        take = views(used=2 * HC * T)
        msig, mtmp = take(4, T), take(2, T)
        assert 2 * HC * T + 6 * T <= GO_AT

        def tokens(g, b):
            return slice(b * P, (b + 1) * P) if g == 0 else slice(b, T, RESIDUES)

        def natural(g, v):
            return v.rearrange("p (b m) -> p b m", b=TT) if g == 0 else v.rearrange("p (r m) -> p m r", r=RESIDUES)

        block = ctx.enter_context(nc.Block())

        constants = ((gains, "gains"), (ident, "ident"), (ones, "ones"), (lvl_mask, "lvl_mask"), (reset, "reset"),
                     (lbl, "lbl"), (hgain, "hgain"), (rot_a, "rot_a"), (cos_a, "cos_a"), (sin_a, "sin_a"),
                     (win_mask, "win_mask"), (res_mask, "res_mask"),
                     (gbias, "gbias"), (ggain, "ggain"))
        ALL_CONSTANTS = 16 * len(constants)

        @block.sync
        def _(sp):
            for c in range(DC):
                sp.dma_start(h[:, c], a["x"][:, c]).then_inc(s["x_loaded"], 16)
            for dst, name in constants:
                sp.dma_start(dst[:], a[name]).then_inc(s["consts_loaded"], 16)
            for name, units, width in SECTIONS:
                w, n0 = a["w_" + name], FIRST[name]
                k0 = 0
                if n0 == 0:
                    for k in range(RING):
                        sp.dma_start(ring[:, k, 0:width], w[k]).then_inc(w_ready[k], 16)
                    k0 = RING
                loops = (units - k0) // RING
                if loops > 1:
                    with sp.Fori(0, loops) as i:
                        for k in range(k0, k0 + RING):
                            r = (n0 + k) % RING
                            sp.wait_ge(s["w_used"], i * RING + (n0 + k - RING + 1))
                            sp.dma_start(ring[:, r, 0:width], w[bass.ds(i * RING + k, 1)].rearrange("a p n -> (a p) n")
                                         ).then_inc(w_ready[r], 16)
                    k0 += loops * RING
                for k in range(k0, units):
                    r = (n0 + k) % RING
                    sp.wait_ge(s["w_used"], n0 + k - RING + 1)
                    sp.dma_start(ring[:, r, 0:width], w[k]).then_inc(w_ready[r], 16)

        H_CREDIT = 2
        def h_done(k, n):
            return 8 * k + n + 1 + H_CREDIT

        NORM_AFTER = [None, 0, 2, 3, 5, 6, 7, 9]
        NORM_INPUT = [0, 1, 2, 3, None, 4, 5, None]

        @block.tensor
        def _(pe):
            def plain(section, k, rhs, bank, i=None, per=0, first=True, last=True, n=8):
                r, v = ring_use(section, k, i, per)
                pe.wait_ge(w_ready[r], v)
                for c in range(n):
                    m = nc.tensor.matmul(ps[:, bank], ring[:, r, c * P:(c + 1) * P], rhs(c),
                                         start=first and c == 0, stop=last and c == n - 1)
                return m

            def unit(section, k, act, bank, i=None, per=0, n=8, ready=None):
                r, v, _ = split_use(section, k, i, per)
                pe.wait_ge(s["w_lo"], v)
                for c in range(n):
                    if ready is not None:
                        ready(c)
                    w = slice(c * P, (c + 1) * P)
                    nc.tensor.matmul(ps[:, bank], ws[:, 0, r, w], act[:, 0, c], start=c == 0, stop=False)
                    nc.tensor.matmul(ps[:, bank], ws[:, 0, r, w], act[:, 1, c], start=False, stop=False)
                    m = nc.tensor.matmul(ps[:, bank], ws[:, 1, r, w], act[:, 0, c], start=False, stop=c == n - 1)
                return m

            def used(m):
                m.then_inc(s["w_used"], 1)

            def mean_square(n):
                for c in range(DC):
                    pe.wait_ge(s["sq_ready"], 8 * n + c + 1)
                    nc.tensor.matmul(ps[:, 6], ones[:], nsq[:, c % 4], start=c == 0, stop=c == DC - 1
                                     ).then_inc(s["ms_ready"], 1)

            def u_chunk(m):
                def ready(c):
                    pe.wait_ge(s["u_lo_odd"] if c % 2 else s["u_lo_even"], 4 * m + c // 2 + 1)
                return ready

            def project(section, k_upd, act):
                with pe.Fori(0, DC // RING) as i:
                    for j in range(RING):
                        pe.wait_ge(s["h_ready"], i * RING + (8 * k_upd + j + 1))
                        used(unit(section, j, act, j % 2, i, RING))

            def ffn(f, k_upd, m):
                for half in range(2):
                    gu, down, G = f"gu{f}{'ab'[half]}", f"down{f}{'ab'[half]}", HC * (2 * f + half)

                    def tile(j, i=None, ready=None):
                        at = G + j + 1 if i is None else i * 2 + (G + j + 1)
                        pe.wait_ge(s["g_full"], at)
                        used(unit(gu, 2 * j, us, 2 * (j % 2), i, 4, ready=ready))
                        used(unit(gu, 2 * j + 1, us, 2 * (j % 2) + 1, i, 4))

                    tile(0, ready=None if half else u_chunk(m))
                    tile(1)
                    with pe.Fori(0, (HC - 3) // 2) as i:
                        tile(2, i)
                        tile(3, i)
                    tile(HC - 1)

                    def hid_chunk(c):
                        pe.wait_ge(s["g_lo"], G + c + 1)

                    with pe.Fori(0, DC // 4) as i:
                        for j in range(4):
                            pe.wait_ge(s["h_ready"], i * 4 + (8 * (k_upd + half) + j + 1))
                            used(down_unit(down, j, i, hid_chunk if j == 0 else None))

            def down_unit(section, j, i, ready):
                return unit(section, j, hid, 4 + j % 2, i, 4, n=HC, ready=ready)

            def hgrn_project(i=None, k0=0, first=False):
                order = (("sig_f", 1), ("query", 0), ("silu_g", 2), ("vf_ready", 3))
                for k, (freed, bank) in enumerate(order):
                    if not first:
                        pe.wait_ge(s[freed], i + 1)
                    used(unit("hgrn", k0 + k, us, bank, i, 4, ready=u_chunk(0) if first and k == 0 else None))

            def chunk_scores(i, it, dv, k_, q_, rows, first_x=True):
                for n, l in enumerate(list(range(LEVELS - 1, -1, -1)) + [None]):
                    if l is not None and first_x:
                        pe.wait_ge(s["x_ready"], it * 9 + (n + 3))
                    if n >= 2:
                        pe.wait_ge(s["scores"], i * 8 + (n - 1))
                    for c in range(NCH):
                        t = slice(c * C, (c + 1) * C)
                        kk, qq = (k_[rows, t], q_[rows, t]) if l is None else (dv[rows, l, t], dv[rows, l, t])
                        m = nc.tensor.matmul(ps[:, 4 + n % 2, t], kk, qq, start=True, stop=True)
                    m.then_inc(s["score_ps"], 1)

            def chunk_states(i, keys, values):
                for c in range(NCH - 1):
                    m = nc.tensor.matmul(ps[:, 6, c * C:(c + 1) * C], keys(c), values(c), start=True, stop=True)
                m.then_inc(s["st_ps"], 1)

            def chunk_outputs(i, values, sc, stv, dv, rows, sq):
                pe.wait_ge(s["scores"], i * 8 + 8)
                pe.wait_ge(s["states"], i * 3 + 3)
                for c in range(NCH):
                    t = slice(c * C, (c + 1) * C)
                    m = nc.tensor.matmul(ps[:, 7, t], values(c), sc[:, t], start=True, stop=c == 0)
                    if c:
                        m = nc.tensor.matmul(ps[:, 7, t], stv[rows, c], dv[rows, L_STATE, t], start=False, stop=True)
                m.then_inc(s["o_ps"], 1)
                pe.wait_ge(s["o_sq"], i + 1)
                nc.tensor.matmul(ps[:, 6], ones[:], sq, start=True, stop=True).then_inc(s["o_ms"], 1)

            ALL = slice(0, P)

            def hgrn_core(i):
                pe.wait_ge(s["vf_ready"], i + 1)
                for c in range(NCH):
                    m = nc.tensor.transpose(ps[:, 6, c * C:(c + 1) * C], vf[:, c * C:(c + 1) * C], ident[:])
                m.then_inc(s["vt_ps"], 1)
                chunk_scores(i, i, dec, key, qry, ALL)
                pe.wait_ge(s["vt_ready"], i + 1)
                for c in range(NCH - 1):
                    m = nc.tensor.transpose(ps[:, 6, c * C:(c + 1) * C], dec[:, L_END, c * C:(c + 1) * C], ident[:])
                m.then_inc(s["kt_ps"], 1)
                pe.wait_ge(s["kt_ready"], i + 1)
                chunk_states(i, lambda c: kT[:, c], lambda c: vT[:, c])
                chunk_outputs(i, lambda c: vT[:, c], sc_mat, st, dec, ALL, osq)

            pe.wait_ge(s["consts_loaded"], ALL_CONSTANTS)
            mean_square(0)
            hgrn_project(0, first=True)
            with pe.Fori(0, HEADS_H - 1) as i:
                hgrn_project(i, k0=4)
                hgrn_core(i)
            hgrn_core(HEADS_H - 1)
            pe.wait_ge(s["o_lo"], HEADS_H)
            project("hgrn_out", 0, hid)
            mean_square(1)
            ffn(0, 1, 1)

            def by_tokens(o, rr, per, width, c0, toks, first, last):
                for cc in range(per):
                    w = slice(cc * width, (cc + 1) * width)
                    uh, ul = us[:, 0, c0 + cc, toks], us[:, 1, c0 + cc, toks]
                    nc.tensor.matmul(o, uh, ws[:, 0, rr, w], start=first and cc == 0, stop=False)
                    nc.tensor.matmul(o, uh, ws[:, 1, rr, w], start=False, stop=False)
                    m = nc.tensor.matmul(o, ul, ws[:, 0, rr, w], start=False, stop=last and cc == per - 1)
                return m

            mean_square(2)
            for g in range(GROUPS):
                base = 4 * (g % 2)
                for n in range(4):
                    rr, v, _ = split_use("attn_v", 4 * g + n)
                    pe.wait_ge(s["w_lo"], v)
                    if g == 0:
                        u_chunk(2)(2 * n)
                        u_chunk(2)(2 * n + 1)
                    for tt in range(TT):
                        if g == 2 and n == 0:
                            pe.wait_ge(s["av_ready"], tt + 1)
                        m = by_tokens(ps[:, base + tt], rr, 2, 512, 2 * n, tokens(g, tt), n == 0, n == 3)
                    used(m)

            def qk_tile(N):
                if N >= 2:
                    pe.wait_ge(s["raw_ready"], N - 1)
                elif N == 0:
                    pe.wait_ge(s["av_ready"], GROUPS * TT)
                used(unit("attn_qk", N, us, N % 2))

            def rotate(N):
                pe.wait_ge(s["raw_ready"], N + 1)
                if N >= 2:
                    pe.wait_ge(s["rope_sin"], N - 1)
                nc.tensor.matmul(ps[:, 2 + N % 2], rot_a[:], raw[:, N % 2], start=True, stop=True
                                 ).then_inc(s["rot_ps"], 1)

            def attn_scores(j):
                pe.wait_ge(s["qk_ready"], 6 * (j + 1))
                if j:
                    pe.wait_ge(s["ao_ready"], 3 * j)
                for g in range(GROUPS):
                    q, k = QK[j % 2][:, 2 * g], QK[j % 2][:, 2 * g + 1]
                    for b in range(TT):
                        if g:
                            m = nc.tensor.matmul(SC_BANKS[g][:, b], q[:, tokens(g, b)], k[:, tokens(g, b)],
                                                 start=True, stop=True)
                        elif b:
                            m = nc.tensor.matmul(SC_BANKS[0][:, b], q[:, tokens(0, b)], k[:, (b - 1) * P:(b + 1) * P],
                                                 start=True, stop=True)
                        else:
                            for half in range(2):
                                m = nc.tensor.matmul(SC_BANKS[0][:, 0, half * P:(half + 1) * P], q[:, 0:P], k[:, 0:P],
                                                     start=True, stop=True)
                    m.then_inc(s["sc_ps"], 1)

            def attn_core(j):
                for g in range(GROUPS):
                    pe.wait_ge(s["p_norm"], 2 * j + 1 + (g > 0))
                    for b in range(TT):
                        for half in range(2 if g == 0 else 1):
                            m = nc.tensor.transpose(SC_BANKS[g][:, b, half * P:(half + 1) * P],
                                                    SC[g][:, b, half * P:(half + 1) * P], ident[:])
                    m.then_inc(s["pt_ps"], 1)
                pe.wait_ge(s["lse_diag"], j + 1)
                pe.wait_ge(s["rope_sin"], min(6 * (j + 2), 24))
                for g, bank in enumerate((2, 3, 7)):
                    if g == 2:
                        pe.wait_ge(s["pt_ready"], 3 * j + 3)
                    for b in range(TT):
                        m = nc.tensor.matmul(ps[:, bank, b * P:(b + 1) * P], ones[:], dgl[:, g * TT + b],
                                             start=True, stop=True)
                    m.then_inc(s["lse_ps"], 1)
                for g in range(GROUPS):
                    hd = slice(j * P, (j + 1) * P)
                    for b in range(TT):
                        o = ps[:, 4 + g, b * P:(b + 1) * P]
                        if g:
                            m = nc.tensor.matmul(o, aV[:, g, b, hd], PTs[:, (g + 1) * T + b * P:(g + 1) * T + (b + 1) * P],
                                                 start=True, stop=True)
                        else:
                            m = nc.tensor.matmul(o, aV[:, 0, b, hd], PTs[:, b * 2 * P + P:(b + 1) * 2 * P],
                                                 start=True, stop=b == 0)
                            if b:
                                m = nc.tensor.matmul(o, aV[:, 0, b - 1, hd], PTs[:, b * 2 * P:b * 2 * P + P],
                                                     start=False, stop=True)
                    m.then_inc(s["ao_ps"], 1)

            for n in range(6):
                qk_tile(n)
                if n:
                    rotate(n - 1)
            rotate(5)
            for j in range(HPG):
                N = 6 * (j + 1)
                if j + 1 < HPG:
                    if j:
                        pe.wait_ge(s["lse_rows"], 3 * j)
                    qk_tile(N)
                    qk_tile(N + 1)
                    rotate(N)
                    qk_tile(N + 2)
                    rotate(N + 1)
                attn_scores(j)
                if j + 1 < HPG:
                    for n in range(3, 6):
                        qk_tile(N + n)
                        rotate(N + n - 1)
                    rotate(N + 5)
                attn_core(j)
            pe.wait_ge(s["ao_ready"], GROUPS * HPG)
            with pe.Fori(0, DC // 2) as i:
                for j in range(2):
                    pe.wait_ge(s["h_ready"], i * 2 + (8 * 3 + j + 1))
                    used(plain("attn_out", 2 * j, lambda c: aO[:, c], j, i, 4, last=False, n=6))
                    used(plain("attn_out", 2 * j + 1, lambda c: aO[:, 6 + c], j, i, 4, first=False, n=6))
            mean_square(3)
            ffn(1, 4, 3)

            mean_square(4)
            mean_square(5)
            ROT = {0: 0, 1: 1, 2: 2, 3: 3, 6: 4, 7: 5}

            def fm_tile(n):
                if n >= 2:
                    pe.wait_ge(s["nt_ready"], n - 1)
                used(unit("nsa_fm" if n < 8 else "gla_fm", n % 8, us, n % 2, ready=None if n else u_chunk(4)))

            def nsa_rotate(n):
                x = ROT[n]
                pe.wait_ge(s["nt_ready"], n + 1)
                if x == 0:
                    pe.wait_ge(s["nsa_consts"], 16 * 6)
                if x >= 2:
                    pe.wait_ge(s["nrope_sin"], x - 1)
                src = qraw[:, n] if n < 4 else kraw[:, n - 6]
                nc.tensor.matmul(ps[:, 2 + x % 2], rot_n[:], src, start=True, stop=True).then_inc(s["nrot_ps"], 1)

            def token_major(section, units, per, width, freed):
                for n in range(units):
                    rr, v, _ = split_use(section, n)
                    pe.wait_ge(s["w_lo"], v)
                    for tt in range(TT):
                        if n == 0 and freed:
                            pe.wait_ge(s[freed], tt + 1)
                        m = by_tokens(ps[:, 4 + tt, 0:width], rr, per, width, per * n, tokens(0, tt),
                                      n == 0, n == units - 1)
                    used(m)

            for n in range(8):
                fm_tile(n)
                if n - 1 in ROT:
                    nsa_rotate(n - 1)
            token_major("nsa_tm", 2, 4, TM_COLS, None)
            nsa_rotate(7)
            token_major("gla_v", 4, 2, 512, "ngate_ready")
            for n in range(8, 12):
                fm_tile(n)
            pe.wait_ge(s["nt_ready"], 11)
            used(unit("gla_lr", 0, us, 0))

            pe.wait_ge(s["cmp_loaded"], 48)
            for x in range(2):
                pe.wait_ge(s["kvpe"], 8 * (x + 1))
                pe.wait_ge(s["nt_ready"], 12 + x)
                bank = 1 - x
                for l in range(16):
                    m = nc.tensor.matmul(ps[:, bank, 0:2 * NB], w1[:, x, l], kvp[:, x, l], start=l == 0, stop=l == 15)
                m.then_inc(s["hid_ps"], 1)
            pe.wait_ge(s["nrope_sin"], 6)
            for p in range(2):
                m = nc.tensor.matmul(ps[:, 2 + p], gw2[0:RANK, p * P:(p + 1) * P], lrS[0:RANK], start=True, stop=True)
            m.then_inc(s["gz_ps"], 1)
            pe.wait_ge(s["gv_ready"], TT)
            pe.wait_ge(s["hid"], 2)
            nc.tensor.matmul(ps[:, 6, 0:NB], w2k[:, HD:3 * HD], hidk[:, 0:NB], start=True, stop=False)
            nc.tensor.matmul(ps[:, 6, 0:NB], w2k[:, 0:2 * HD], hidk[:, NB:2 * NB], start=False, stop=True
                             ).then_inc(s["kc_ps"], 1)
            for g in range(2):
                m = nc.tensor.matmul(ps[:, 7, g * HD:(g + 1) * HD], hidv[:, g * P:(g + 1) * P], w2v, start=True, stop=True)
            m.then_inc(s["vc_ps"], 1)

            pe.wait_ge(s["kc_ready"], 1)
            cs = ps[:, 4:6].rearrange("p g (t h n) -> p g t h n", t=TT, h=4)
            for tt in range(TT):
                for hh in range(HEADS_N):
                    rows = slice(hh // 4 * HD, hh // 4 * HD + HD)
                    m = nc.tensor.matmul(cs[:, hh // 4, tt, hh % 4], qraw[rows, hh % 4, tt * P:(tt + 1) * P], kc[rows],
                                         start=True, stop=True)
            m.then_inc(s["cs_ps"], 1)
            pe.wait_ge(s["vbd"], 8)
            pe.wait_ge(s["cs_w"], 1)
            for b in range(2):
                for k in range(4):
                    tt, g = divmod(b * 4 + k, 2)
                    m = nc.tensor.transpose(ps[:, 6 + b, k * P:(k + 1) * P],
                                            sC[:, tt, 4 * g:4 * g + 4].rearrange("p h n -> p (h n)"), ident[:])
                m.then_inc(s["ct_ps"], 1)
            pe.wait_ge(s["ct_ready"], 2)
            pe.wait_ge(s["z_b"], 2)
            for tt in range(TT):
                for g in range(2):
                    m = nc.tensor.matmul(ps[:, tt, g * 256:(g + 1) * 256], PTc[:, 2 * tt + g], vbd[:, g], start=True, stop=True)
                m.then_inc(s["co_ps"], 1)

            def nsa_scores(e):
                hh, x = divmod(e, 2)
                rows = slice(hh // 4 * HD, hh // 4 * HD + HD)
                if e == 0:
                    pe.wait_ge(s["oa_ready"], 3)
                elif e == 1:
                    pe.wait_ge(s["oa_ready"], 4)
                else:
                    pe.wait_ge(s["npt_ready"], 3 * (e - 1))
                base = ps[:, 3 * (e % 2):3 * (e % 2) + 3].rearrange("p a n -> p (a n)")
                for tt in range(TT):
                    m = nc.tensor.matmul(base[:, BOFF[tt]:BOFF[tt] + (tt + 1) * P], qrot[rows, hh % 4, tt * P:(tt + 1) * P],
                                         kr[rows, x, 0:(tt + 1) * P], start=True, stop=True)
                m.then_inc(s["ns_ps"], 1)

            def nsa_transposes(e):
                pe.wait_ge(s["ns_exp"], 4 * (e + 1))
                base = ps[:, 3 * (e % 2):3 * (e % 2) + 3].rearrange("p a n -> p (a n)")
                for k in range(10):
                    m = nc.tensor.transpose(base[:, k * P:(k + 1) * P], prob[:, e % 2, k * P:(k + 1) * P], ident[:])
                m.then_inc(s["nt_ps"], 1)

            def nsa_values(e):
                hh, x = divmod(e, 2)
                pe.wait_ge(s["npt_ready"], 3 * (e + 1))
                if e >= 2:
                    pe.wait_ge(s["n_scaled"], e - 1)
                vcols = slice(x * P + hh // 4 * HD, x * P + hh // 4 * HD + HD)
                for tt in range(TT):
                    for k in range(tt + 1):
                        at = OFF[tt] + k * P
                        m = nc.tensor.matmul(ps[:, 6 + e % 2, tt * HD:(tt + 1) * HD], probT[:, e % 2, at:at + P],
                                             vsw[:, k, vcols], start=k == 0, stop=k == tt)
                m.then_inc(s["no_ps"], 1)

            pe.wait_ge(s["nrope"], 6)
            E = 2 * HEADS_N
            nsa_scores(0)
            for e in range(E):
                if e + 1 < E:
                    nsa_scores(e + 1)
                nsa_transposes(e)
                if e:
                    nsa_values(e - 1)
            nsa_values(E - 1)
            pe.wait_ge(s["oa_acc"], E)
            for ft in range(4):
                for tt in range(TT):
                    m = nc.tensor.transpose(ps[:, ft, tt * P:(tt + 1) * P], oa[:, tt, ft * P:(ft + 1) * P], ident[:])
                m.then_inc(s["oat_ps"], 1)

            for n in range(HEADS_G):
                pe.wait_ge(s["oat_ready"], n + 1)
                used(unit("gla_r", n, us, n))
            for hh in range(HEADS_G):
                p, I = hh // 2, HEADS_H + hh
                rows = slice(hh % 2 * HD, hh % 2 * HD + HD)
                dv = gdec[p]
                vals = lambda c: vG[:, c, hh * P:(hh + 1) * P]
                chunk_scores(I, HEADS_H + p, dv, kg[:, p], qg[:, p], rows, first_x=hh % 2 == 0)
                if hh % 2 == 0:
                    if hh:
                        pe.wait_ge(s["o_rstd"], 2 * I)
                    for c in range(NCH - 1):
                        m = nc.tensor.transpose(ps[:, 6, c * C:(c + 1) * C], dv[:, L_END, c * C:(c + 1) * C], ident[:])
                    m.then_inc(s["kt_ps"], 1)
                    pe.wait_ge(s["kt_ready"], HEADS_H + p + 1)
                else:
                    pe.wait_ge(s["o_rstd"], 2 * I)
                chunk_states(I, lambda c: gkT[:, p, c * P:(c + 1) * P], vals)
                if hh:
                    pe.wait_ge(s["o_scaled"], I)
                chunk_outputs(I, vals, gsc, gst, dv, rows, gosq)

            pe.wait_ge(s["gb_ready"], HEADS_G)
            with pe.Fori(0, 2) as i:
                for j in range(4):
                    b = 4 * (j % 2)
                    pe.wait_ge(s["merged"], i * 4 + (j + 1))
                    used(unit("merge", 3 * j, us, b, i, 8))
                    used(unit("merge", 3 * j + 1, us, b + 1, i, 8))
                    rr, v = ring_use("merge", 3 * j + 2, i, 12)
                    pe.wait_ge(w_ready[rr], v)
                    for c in range(8):
                        src = oaT[:, c] if c < 4 else goT[:, c - 4]
                        m = nc.tensor.matmul(ps[:, b + 2 + c // 4], ring[:, rr, c * P:(c + 1) * P], src,
                                             start=c % 4 == 0, stop=c % 4 == 3)
                    used(m)
            pe.wait_ge(s["m_lo"], DC)
            project("mix_out", 7, hid)
            mean_square(6)
            ffn(2, 8, 5)
            mean_square(7)

        @block.scalar
        def _(act):
            def hi(section, k, i=None, per=0, used_per=None):
                r, v = ring_use(section, k, i, used_per or per)
                slot, _, free = split_use(section, k, i, used_per or per)
                w = WIDTH[section]
                if free is not None:
                    act.wait_ge(s["w_used"], free)
                act.wait_ge(w_ready[r], v)
                nc.scalar.copy(ws[:, 0, slot, 0:w], ring[:, r, 0:w]).then_inc(s["w_hi"], 1)

            def norm(n, nxt=None):
                m = NORM_INPUT[n]
                for c in range(DC):
                    if c == DC - 1 and nxt:
                        hi(nxt, 0)
                    if n == 0:
                        act.wait_ge(s["x_loaded"], 16 * 8)
                    else:
                        act.wait_ge(s["h_ready"], h_done(NORM_AFTER[n], c))
                    if c >= 4:
                        act.wait_ge(s["ms_ready"], 8 * n + c - 3)
                    nc.scalar.activation(nsq[:, c % 4], h[:, c], ACT.Square).then_inc(s["sq_ready"], 1)
                act.wait_ge(s["ms_ready"], 8 * (n + 1))
                nc.scalar.activation(rs[:], ps[:, 6], ACT.Ln, scale=1.0 / D, bias=eps[:, 0:1]).then_inc(s["rstd"], 1)
                act.wait_ge(s["rstd"], 2 * n + 1)
                nc.scalar.activation(rs[:], rs[:], ACT.Exp, scale=-0.5).then_inc(s["rstd"], 1)
                if m is None:
                    return
                for c in range(DC):
                    if c == 4:
                        hi(nxt, 1)
                    act.wait_ge(s["u_tmp"], 8 * m + c + 1)
                    nc.scalar.copy(us[:, 0, c], utmp[:, c % 4]).then_inc(s["u_hi"], 1)

            def ffn(f, nxt):
                for half in range(2):
                    gu, down, G = f"gu{f}{'ab'[half]}", f"down{f}{'ab'[half]}", HC * (2 * f + half)

                    def tile(j, i=None):
                        x = j % 2
                        at = lambda v, per: v if i is None else i * per + v
                        last = j == HC - 1
                        hi(down, 0) if last else hi(gu, 2 * j + 2, i, 4)
                        act.wait_ge(s["w_used"], at(FIRST[gu] + 2 * j + 1, 4))
                        nc.scalar.activation(sgate[:, x], ps[:, 2 * x], ACT.Sigmoid).then_inc(s["gate_sig"], 1)
                        hi(down, 1) if last else hi(gu, 2 * j + 3, i, 4)
                        act.wait_ge(s["g_full"], at(G + j + 3, 2))
                        dst = hid[:, 0, j] if i is None else hid[:, 0, bass.ds(i * 2 + j, 1)].rearrange("p a t -> p (a t)")
                        nc.scalar.copy(dst, gtmp[:, x]).then_inc(s["g_hi"], 1)

                    with act.Fori(0, (HC - 1) // 2) as i:
                        tile(0, i)
                        tile(1, i)
                    tile(HC - 1)
                    for j in range(2, DC):
                        hi(down, j)
                    if half == 0:
                        hi(f"gu{f}b", 0)
                        hi(f"gu{f}b", 1)

            def decay_exps(it, cum, dv, ends):
                act.wait_ge(s["cum"], it + 1)
                nc.scalar.activation(dv[:, L_STATE], cum, ACT.Exp).then_inc(s["dec_out"], 1)
                act.wait_ge(s["dec_out"], it * 4 + 1)
                nc.scalar.copy(ends, dv[:, L_STATE, C - 1::C]).then_inc(s["chunk_decay"], 1)
                for lo, hi, ready in ((6, 8, 2), (3, 6, 5), (0, 3, 8)):
                    act.wait_ge(s["dec_in"], it * 8 + ready)
                    nc.scalar.activation(dv[:, lo:hi], dv[:, lo:hi], ACT.Exp).then_inc(s["dec_out"], 1)

            def output_rstd(i, sq, r):
                act.wait_ge(s["o_ps"], i + 1)
                nc.scalar.activation(sq, ps[:, 7], ACT.Square).then_inc(s["o_sq"], 1)
                act.wait_ge(s["o_ms"], i + 1)
                nc.scalar.activation(r, ps[:, 6], ACT.Ln, scale=1.0 / P, bias=eps[:, 0:1]).then_inc(s["o_rstd"], 1)
                act.wait_ge(s["o_rstd"], i * 2 + 1)
                nc.scalar.activation(r, r, ACT.Exp, scale=-0.5).then_inc(s["o_rstd"], 1)

            act.wait_ge(s["credit"], 2)
            norm(0, "hgrn")
            hi("hgrn", 2)
            hi("hgrn", 3)
            act.wait_ge(s["lb_steps"], 5)
            nc.scalar.activation(lbt[:, 0:3], lbt[:, 0:3], ACT.Exp).then_inc(s["lb_steps"], 1)
            def hgrn_head(i, last=False):
                w0 = FIRST["hgrn"]
                nxt = (lambda k: hi("hgrn_out", k) if k < 2 else None) if last else (lambda k: hi("hgrn", 4 + k, i, 4))
                nxt(0)
                nxt(1)
                for k, (src, dst, done) in enumerate(((1, sf_, "sig_f"), (0, sq_, "sig_q"), (2, sg_, "sig_g"))):
                    act.wait_ge(s["w_used"], i * 4 + (w0 + k + 1))
                    nc.scalar.activation(dst, ps[:, src], ACT.Sigmoid).then_inc(s[done], 1)
                act.wait_ge(s["w_used"], i * 4 + (w0 + 4))
                nc.scalar.copy(vf, ps[:, 3]).then_inc(s["vf_ready"], 1)
                act.wait_ge(s["forget"], i + 1)
                nc.scalar.activation(lf, fg, ACT.Ln).then_inc(s["log_f"], 1)
                nxt(2)
                decay_exps(i, bcum, dec, chd)
                nxt(3)
                act.wait_ge(s["vt_ps"], i + 1)
                nc.scalar.copy(vT, ps[:, 6].rearrange("p (c t) -> p c t", c=NCH)).then_inc(s["vt_ready"], 1)
                act.wait_ge(s["kt_ps"], i + 1)
                nc.scalar.copy(kT[:, 0:3], ps[:, 6, 0:3 * C].rearrange("p (c t) -> p c t", c=3)).then_inc(s["kt_ready"], 1)
                output_rstd(i, osq, ors)
                act.wait_ge(s["o_full"], i + 1)
                dst = hid[:, 0, i] if last else hid[:, 0, bass.ds(i, 1)].rearrange("p a t -> p (a t)")
                nc.scalar.copy(dst, otmp).then_inc(s["o_hi"], 1)

            with act.Fori(0, HEADS_H - 1) as i:
                hgrn_head(i)
            hgrn_head(HEADS_H - 1, last=True)
            for k in range(2, DC):
                hi("hgrn_out", k)
            norm(1, "gu0a")
            ffn(0, "attn_v")

            norm(2, "attn_v")
            act.dma_start(a["h_spill"], h).then_inc(s["spilled"], 16)
            for g in range(GROUPS):
                for k in range(4 * g + 2, 4 * g + 6):
                    hi("attn_v", k) if k < 12 else hi("attn_qk", k - 12)
                for tt in range(TT):
                    act.wait_ge(s["w_used"], FIRST["attn_v"] + 4 * (g + 1))
                    nc.scalar.copy(aV[:, g, tt], ps[:, 4 * (g % 2) + tt]).then_inc(s["av_ready"], 1)

            def take_raw(N):
                if N + 2 < 24:
                    hi("attn_qk", N + 2)
                act.wait_ge(s["w_used"], FIRST["attn_qk"] + N + 1)
                if N >= 2:
                    act.wait_ge(s["rope_cos"], N - 1)
                    act.wait_ge(s["rot_ps"], N - 1)
                nc.scalar.copy(raw[:, N % 2], ps[:, N % 2]).then_inc(s["raw_ready"], 1)

            for n in range(6):
                take_raw(n)
            for j in range(HPG):
                N = 6 * (j + 1)
                if j + 1 < HPG:
                    for n in range(3):
                        take_raw(N + n)
                for g in range(GROUPS):
                    act.wait_ge(s["sc_negmax"], 3 * j + g + 1)
                    for b in range(TT):
                        nc.scalar.activation(SC[g][:, b], SC[g][:, b], ACT.Exp, bias=nmx[:, g, b:b + 1],
                                             accum_out=lsum[:, g, b:b + 1]).then_inc(s["p_exp"], 1)
                act.wait_ge(s["p_exp"], 12 * (j + 1))
                nc.scalar.activation(lsev, lsum, ACT.Ln).then_inc(s["p_logsum"], 1)
                if j + 1 < HPG:
                    for n in range(3, 6):
                        take_raw(N + n)
                for g in range(GROUPS):
                    act.wait_ge(s["pt_ps"], 3 * j + g + 1)
                    if g == 0:
                        nc.scalar.copy(PTs[:, 0:1024], ps[:, 4:6].rearrange("p a n -> p (a n)")).then_inc(s["pt_ready"], 1)
                    else:
                        nc.scalar.copy(PTs[:, (g + 1) * T:(g + 2) * T], ps[:, 5 + g]).then_inc(s["pt_ready"], 1)
                act.wait_ge(s["spilled"], 16)
                for g, bank in enumerate((2, 3, 7)):
                    act.wait_ge(s["lse_ps"], 3 * j + g + 1)
                    dst = lrow[:, g].rearrange("p (b m) -> p b m", b=TT if g == 0 else P)
                    nc.scalar.copy(dst, natural(g, ps[:, bank])).then_inc(s["lse_rows"], 1)
                act.wait_ge(s["mix_diff"], j + 1)
                nc.scalar.activation(lrow, lrow, ACT.Exp).then_inc(s["mix_exp"], 1)
            act.wait_ge(s["ao_ready"], GROUPS * HPG)
            act.dma_start(h, a["h_spill"]).then_inc(s["reloaded"], 16)
            for dst, name in ((rot_n, "rot_n"), (cos_n, "cos_n"), (sin_n, "sin_n"), (cmp_mask, "cmp_mask"),
                              (pos_kv, "pos_kv"), (gw2[0:RANK], "gw2")):
                act.dma_start(dst, a[name]).then_inc(s["nsa_consts"], 16)
            norm(3, "gu1a")
            ffn(1, None)

            norm(4)
            norm(5, "nsa_fm")
            act.dma_start(a["h_spill"], h).then_inc(s["spilled"], 16)
            fm_dst = [qraw[:, n] for n in range(4)] + [kvraw[:, 0], kvraw[:, 1], kraw[:, 0], kraw[:, 1],
                                                       qg[:, 0], qg[:, 1], kg[:, 0], kg[:, 1]]

            def take_fm(n):
                scale = float(HD) ** -0.5 if n < 4 or n in (8, 9) else 1.0
                if n < 8:
                    hi("nsa_fm", n + 2) if n < 6 else hi("nsa_tm", n - 6)
                elif n < 11:
                    hi("gla_fm", n - 6) if n < 10 else hi("gla_lr", 0)
                else:
                    hi("gla_r", 0)
                act.wait_ge(s["w_used"], (FIRST["nsa_fm"] + n if n < 8 else FIRST["gla_fm"] + n - 8) + 1)
                nc.scalar.activation(fm_dst[n], ps[:, n % 2], ACT.Copy, scale=scale).then_inc(s["nt_ready"], 1)

            take_fm(0)
            act.wait_ge(s["u_lo_even"], 20)
            act.wait_ge(s["u_lo_odd"], 20)
            for dst, name in ((w1, "cmp_w1"), (w2k, "cmp_w2k"), (w2v, "cmp_w2v")):
                act.dma_start(dst, a[name]).then_inc(s["cmp_loaded"], 16)
            for n in range(1, 8):
                take_fm(n)
            hi("gla_v", 0)
            hi("gla_v", 1)
            for tt in range(TT):
                act.wait_ge(s["w_used"], FIRST["nsa_tm"] + 2)
                nc.scalar.copy(vsw[:, tt], ps[:, 4 + tt, 0:2 * P]).then_inc(s["ntm_ready"], 1)
                nc.scalar.activation(ngate[:, tt], ps[:, 4 + tt, 2 * P:TM_COLS], ACT.Sigmoid).then_inc(s["ngate_ready"], 1)
            for k in range(4):
                hi("gla_v", 2 + k) if k < 2 else hi("gla_fm", k - 2)
            act.wait_ge(s["spilled"], 32)
            for tt in range(TT):
                act.wait_ge(s["w_used"], FIRST["gla_v"] + 4)
                nc.scalar.copy(vG[:, tt], ps[:, 4 + tt]).then_inc(s["gv_ready"], 1)
            for n in range(8, 12):
                take_fm(n)
            act.wait_ge(s["w_used"], FIRST["gla_lr"] + 1)
            nc.scalar.copy(lrS[0:RANK], ps[0:RANK, 0]).then_inc(s["nt_ready"], 1)
            hi("gla_r", 1)
            for x in range(2):
                act.wait_ge(s["hid_ps"], x + 1)
                nc.scalar.activation(hsig[:, x], ps[:, 1 - x, 0:2 * NB], ACT.Sigmoid).then_inc(s["hid_sig"], 1)
            act.wait_ge(s["kc_ps"], 1)
            nc.scalar.copy(kc, ps[:, 6, 0:NB]).then_inc(s["kc_ready"], 1)
            act.wait_ge(s["vc_ps"], 1)
            act.wait_ge(s["kvpe_zero"], 2)
            for g in range(2):
                for k in range(4):
                    rows = slice(32 * k, 32 * k + 32)
                    nc.scalar.copy(vbd[rows, g, k * HD:(k + 1) * HD], ps[rows, 7, g * HD:(g + 1) * HD]).then_inc(s["vbd"], 1)
            for p in range(2):
                act.wait_ge(s["z_b"], p + 1)
                if p:
                    act.wait_ge(s["z_min"], 1)
                nc.scalar.activation(zab, la[:, p], ACT.Abs).then_inc(s["z_abs"], 1)
                act.wait_ge(s["z_abs"], p + 1)
                nc.scalar.activation(zab, zab, ACT.Exp, scale=-1.0).then_inc(s["z_exp"], 1)
                act.wait_ge(s["z_exp"], p + 1)
                nc.scalar.activation(zab, zab, ACT.Ln, bias=ones[:, 0:1]).then_inc(s["z_ln"], 1)
            act.wait_ge(s["cs_sub"], 1)
            nc.scalar.activation(sC, sC, ACT.Exp).then_inc(s["cs_exp"], 1)
            for b in range(2):
                act.wait_ge(s["ct_ps"], b + 1)
                nc.scalar.copy(PTc[:, 4 * b:4 * b + 4], ps[:, 6 + b].rearrange("p (k n) -> p k n", k=4)).then_inc(s["ct_ready"], 1)
            for tt in range(TT):
                act.wait_ge(s["co_ps"], tt + 1)
                nc.scalar.copy(oa[:, tt], ps[:, tt]).then_inc(s["oa_ready"], 1)
            act.wait_ge(s["hid"], 2)
            def nsa_exps(i, x):
                base = ps[:, 3 * x:3 * x + 3].rearrange("p a n -> p (a n)")
                act.wait_ge(s["ns_neg"], i * 2 + (x + 1))
                for tt in range(TT):
                    nc.scalar.activation(prob[:, x, OFF[tt]:OFF[tt] + (tt + 1) * P], base[:, BOFF[tt]:BOFF[tt] + (tt + 1) * P],
                                         ACT.Exp, bias=nneg[:, x, tt:tt + 1], accum_out=nsum[:, x, tt:tt + 1]
                                         ).then_inc(s["ns_exp"], 1)

            def nsa_copies(i, x):
                base = ps[:, 3 * x:3 * x + 3].rearrange("p a n -> p (a n)")
                act.wait_ge(s["nt_ps"], i * 2 + (x + 1))
                for k in range(3):
                    lo, hi = 512 * k, min(512 * (k + 1), 1280)
                    nc.scalar.copy(probT[:, x, lo:hi], base[:, lo:hi]).then_inc(s["npt_ready"], 1)

            nsa_exps(0, 0)
            with act.Fori(0, HEADS_N - 1) as i:
                nsa_exps(i, 1)
                nsa_copies(i, 0)
                nsa_exps(i + 1, 0)
                nsa_copies(i, 1)
            nsa_exps(HEADS_N - 1, 1)
            nsa_copies(HEADS_N - 1, 0)
            nsa_copies(HEADS_N - 1, 1)
            for ft in range(4):
                act.wait_ge(s["oat_ps"], ft + 1)
                nc.scalar.copy(oaT[:, ft], ps[:, ft]).then_inc(s["oat_ready"], 1)
            for n in range(HEADS_G):
                hi("gla_r", n + 2) if n < 2 else hi("merge", n - 2)
                act.wait_ge(s["w_used"], FIRST["gla_r"] + n + 1)
                if n >= 2:
                    act.wait_ge(s["gr_silu"], n - 1)
                nc.scalar.activation(gsig[:, n % 2], ps[:, n], ACT.Sigmoid).then_inc(s["gr_sig"], 1)
            for p in range(2):
                decay_exps(HEADS_H + p, gcum[:, p], gdec[p], gchd[:, p])
            for hh in range(HEADS_G):
                if hh % 2 == 0:
                    act.wait_ge(s["kt_ps"], HEADS_H + hh // 2 + 1)
                    nc.scalar.copy(gkT[:, hh // 2], ps[:, 6, 0:3 * C]).then_inc(s["kt_ready"], 1)
                output_rstd(HEADS_H + hh, gosq, gors)
            act.wait_ge(s["gb_ready"], HEADS_G)
            act.dma_start(h, a["h_spill"]).then_inc(s["reloaded"], 16)
            for j in range(DC):
                for k in range(2):
                    hi("merge", 3 * (j + 1) + k) if j + 1 < DC else hi("mix_out", k)
                    act.wait_ge(s["w_used"], FIRST["merge"] + 3 * j + k + 1)
                    if j >= 2:
                        act.wait_ge(s["m_full"], j - 1)
                    nc.scalar.activation(msig[:, 2 * (j % 2) + k], ps[:, 4 * (j % 2) + k], ACT.Sigmoid
                                         ).then_inc(s["mg_sig"], 1)
                act.wait_ge(s["m_full"], j + 1)
                nc.scalar.copy(hid[:, 0, j], mtmp[:, j % 2]).then_inc(s["m_hi"], 1)
            for k in range(2, DC):
                hi("mix_out", k)
            norm(6, "gu2a")
            ffn(2, None)
            norm(7)
            for c in range(DC):
                act.wait_ge(s["credit"], 3 + c)
                act.dma_start(out[:, c], h[:, c]).then_inc(s["stored"], 16)
            act.wait_ge(s["stored"], 16 * DC)

        @block.gpsimd
        def _(pool):
            def lo(section, k, i=None, per=0):
                slot, done, _ = split_use(section, k, i, per)
                r, _ = ring_use(section, k)
                w = WIDTH[section]
                pool.wait_ge(s["w_hi"], done)
                nc.gpsimd.tensor_tensor(ws[:, 1, slot, 0:w], ring[:, r, 0:w], ws[:, 0, slot, 0:w].bitcast(F32),
                                        ALU.subtract).then_inc(s["w_lo"], 1)

            def norm(n, nxt):
                m = NORM_INPUT[n]
                for c in range(0, DC, 2):
                    if c == 4:
                        lo(nxt, 1)
                    pool.wait_ge(s["u_hi"], 8 * m + c + 1)
                    nc.gpsimd.tensor_tensor(us[:, 1, c], utmp[:, c % 4], us[:, 0, c].bitcast(F32), ALU.subtract
                                            ).then_inc(s["u_lo_even"], 1)

            def ffn(f):
                for half in range(2):
                    gu, down, G = f"gu{f}{'ab'[half]}", f"down{f}{'ab'[half]}", HC * (2 * f + half)

                    def tile(j, i=None):
                        for k in range(2):
                            lo(down, k) if j == HC - 1 else lo(gu, 2 * j + 2 + k, i, 4)
                        pool.wait_ge(s["g_hi"], G + j + 1 if i is None else i * 2 + (G + j + 1))
                        dst, src = ((hid[:, 1, j], hid[:, 0, j]) if i is None else
                                    [hid[:, x, bass.ds(i * 2 + j, 1)].rearrange("p a t -> p (a t)") for x in (1, 0)])
                        nc.gpsimd.tensor_tensor(dst, gtmp[:, j % 2], src.bitcast(F32), ALU.subtract).then_inc(s["g_lo"], 1)

                    with pool.Fori(0, (HC - 1) // 2) as i:
                        tile(0, i)
                        tile(1, i)
                    tile(HC - 1)
                    for j in range(2, DC):
                        lo(down, j)
                    if half == 0:
                        lo(f"gu{f}b", 0)
                        lo(f"gu{f}b", 1)

            def decayed(it, dv, k_, q_, operands, between={}):
                for n, l in enumerate((L_END, L_STATE, 6, 5, 4, 3, 2, 1, 0)):
                    if n in between:
                        between[n]()
                    if n == 0:
                        pool.wait_ge(s["dec_out"], it * 4 + 2)
                        for sem, v in operands:
                            pool.wait_ge(sem, v)
                        nc.gpsimd.tensor_tensor(dv[:, l], dv[:, l], k_, ALU.mult).then_inc(s["x_ready"], 1)
                        continue
                    if n == 1:
                        pool.wait_ge(s["chunk_decay"], it + 1)
                        nc.gpsimd.tensor_tensor(dv[:, l], dv[:, l], q_, ALU.mult).then_inc(s["x_ready"], 1)
                        continue
                    if n in (3, 6):
                        pool.wait_ge(s["dec_out"], it * 4 + n // 3 + 2)
                    m = 1 << l
                    x = dv[:, l].rearrange("p (b h m) -> p b h m", h=2, m=m)
                    kk = k_.rearrange("p (b h m) -> p b h m", h=2, m=m)
                    qq = q_.rearrange("p (b h m) -> p b h m", h=2, m=m)
                    nc.gpsimd.tensor_tensor(x[:, :, 0], x[:, :, 0], kk[:, :, 0], ALU.mult)
                    nc.gpsimd.tensor_tensor(x[:, :, 1], x[:, :, 1], qq[:, :, 1], ALU.mult).then_inc(s["x_ready"], 1)
                if 9 in between:
                    between[9]()

            lo("hgrn", 0)
            norm(0, "hgrn")
            lo("hgrn", 2)
            lo("hgrn", 3)

            def hgrn_head(i, last=False):
                nxt = (lambda k: lo("hgrn_out", k) if k < 2 else None) if last else (lambda k: lo("hgrn", 4 + k, i, 4))
                nxt(0)
                nxt(1)
                decayed(i, dec, key, qry, ((s["query"], i + 1), (s["key"], i + 1)), {2: lambda: nxt(2), 9: lambda: nxt(3)})
                pool.wait_ge(s["o_hi"], i + 1)
                dst, src = ((hid[:, 1, i], hid[:, 0, i]) if last else
                            [hid[:, x, bass.ds(i, 1)].rearrange("p a t -> p (a t)") for x in (1, 0)])
                nc.gpsimd.tensor_tensor(dst, otmp, src.bitcast(F32), ALU.subtract).then_inc(s["o_lo"], 1)

            with pool.Fori(0, HEADS_H - 1) as i:
                hgrn_head(i)
            hgrn_head(HEADS_H - 1, last=True)
            for k in range(2, DC):
                lo("hgrn_out", k)
            lo("gu0a", 0)
            norm(1, "gu0a")
            ffn(0)
            lo("attn_v", 0)
            norm(2, "attn_v")
            for k in range(2, 12):
                lo("attn_v", k)
            lo("attn_qk", 0)
            lo("attn_qk", 1)

            def times_cos(N):
                if N + 2 < 24:
                    lo("attn_qk", N + 2)
                pool.wait_ge(s["raw_ready"], N + 1)
                if N >= 2:
                    pool.wait_ge(s["qk_ready"], N - 1)
                nc.gpsimd.tensor_tensor(tcos[:, N % 2], raw[:, N % 2], cos_a[:], ALU.mult).then_inc(s["rope_cos"], 1)

            for n in range(6):
                times_cos(n)
            for j in range(HPG):
                N = 6 * (j + 1)
                if j + 1 < HPG:
                    for n in range(3):
                        times_cos(N + n)
                pool.wait_ge(s["p_recip"], j + 1)
                nc.gpsimd.tensor_tensor(SC[0], SC[0], lrec[:, 0, :, None].broadcast_to((P, TT, 2 * P)), ALU.mult
                                        ).then_inc(s["p_norm"], 1)
                both = scm[:, 1024:2048].rearrange("p (b n) -> p b n", b=2 * TT)
                r12 = lrec[:, 1:3].rearrange("p g b -> p (g b)")[:, :, None]
                nc.gpsimd.tensor_tensor(both, both, r12.broadcast_to((P, 2 * TT, P)), ALU.mult).then_inc(s["p_norm"], 1)
                pool.wait_ge(s["lse"], j + 1)
                pool.wait_ge(s["spilled"], 16)
                nc.gpsimd.tensor_tensor(dgl, ident[:, None, :].broadcast_to((P, GROUPS * TT, P)),
                                        lsev.rearrange("p g b -> p (g b)")[:, :, None].broadcast_to((P, GROUPS * TT, P)),
                                        ALU.mult).then_inc(s["lse_diag"], 1)
                if j + 1 < HPG:
                    for n in range(3, 6):
                        times_cos(N + n)
                pool.wait_ge(s["mix_max"], j + 1)
                nc.gpsimd.tensor_tensor(lrow, lrow, mxw[:, None, :].broadcast_to((P, GROUPS, T)), ALU.subtract
                                        ).then_inc(s["mix_diff"], 1)
                pool.wait_ge(s["mix_recip"], j + 1)
                nc.gpsimd.tensor_tensor(lrow, lrow, rec[:, None, :].broadcast_to((P, GROUPS, T)), ALU.mult
                                        ).then_inc(s["mix_weight"], 1)

            lo("gu1a", 0)
            norm(3, "gu1a")
            ffn(1)

            lo("nsa_fm", 0)
            norm(5, "nsa_fm")
            pool.wait_ge(s["u_lo_odd"], 20)
            pool.wait_ge(s["u_lo_even"], 20)
            nc.gpsimd.memset(kvp, 0.0).then_inc(s["kvpe_zero"], 1)
            nc.gpsimd.memset(vbd, 0.0).then_inc(s["kvpe_zero"], 1)
            for n in range(8):
                lo("nsa_fm", n + 2) if n < 6 else lo("nsa_tm", n - 6)
                if n in (4, 5):
                    continue
                x = n if n < 4 else n - 2
                pool.wait_ge(s["nt_ready"], n + 1)
                if n == 0:
                    pool.wait_ge(s["nsa_consts"], 16 * 6)
                if x >= 2:
                    pool.wait_ge(s["nrope"], x - 1)
                src = qraw[:, n] if n < 4 else kraw[:, n - 6]
                nc.gpsimd.tensor_tensor(ncos[:, x % 2], src, cos_n[:], ALU.mult).then_inc(s["nrope_cos"], 1)
            for section, units in (("gla_v", 4), ("gla_fm", 4), ("gla_lr", 1), ("gla_r", 4)):
                for k in range(units):
                    lo(section, k)
            lo("merge", 0)
            lo("merge", 1)
            for p in range(2):
                decayed(HEADS_H + p, gdec[p], kg[:, p], qg[:, p], ())
            for j in range(DC):
                for k in range(2):
                    lo("merge", 3 * (j + 1) + k) if j + 1 < DC else lo("mix_out", k)
                pool.wait_ge(s["m_hi"], j + 1)
                nc.gpsimd.tensor_tensor(hid[:, 1, j], mtmp[:, j % 2], hid[:, 0, j].bitcast(F32), ALU.subtract
                                        ).then_inc(s["m_lo"], 1)
            for k in range(2, DC):
                lo("mix_out", k)
            lo("gu2a", 0)
            norm(6, "gu2a")
            ffn(2)

        @block.vector
        def _(dve):
            def norm(n, done=None):
                m = NORM_INPUT[n]
                dve.wait_ge(s["rstd"], 2 * n + 2)

                def odd_lo(c):
                    dve.wait_ge(s["u_hi"], 8 * m + c + 1)
                    nc.vector.tensor_tensor(us[:, 1, c], utmp[:, c % 4], us[:, 0, c].bitcast(F32), ALU.subtract
                                            ).then_inc(s["u_lo_odd"], 1)

                for c in range(DC):
                    if m is not None and c >= 4:
                        dve.wait_ge(s["u_lo_odd"] if c % 2 else s["u_lo_even"], 4 * m + (c - 4) // 2 + 1)
                    nc.vector.scalar_tensor_tensor(out=h[:, c] if m is None else utmp[:, c % 4], in0=h[:, c],
                                                   scalar=gains[:, n, c:c + 1], in1=rs[:], op0=ALU.mult, op1=ALU.mult
                                                   ).then_inc(done if m is None else s["u_tmp"], 1)
                    if m is not None and c % 2 == 0 and c:
                        odd_lo(c - 1)
                if m is not None:
                    odd_lo(DC - 1)

            def residual(section, k_upd, units, base, body):
                n = body
                with dve.Fori(0, DC // n) as i:
                    for j in range(n):
                        dve.wait_ge(s["w_used"], i * (n * units) + (FIRST[section] + units * (j + 1)))
                        hj = h[:, bass.ds(i * n + j, 1)].rearrange("p a t -> p (a t)")
                        nc.vector.tensor_tensor(hj, hj, ps[:, base + j % 2], ALU.add).then_inc(s["h_ready"], 1)

            def ffn(f, k_upd):
                for half in range(2):
                    gu, down, G = f"gu{f}{'ab'[half]}", f"down{f}{'ab'[half]}", HC * (2 * f + half)

                    def tile(j, i=None, first=False):
                        x = j % 2
                        at = lambda v, per: v if i is None else i * per + v
                        dve.wait_ge(s["gate_sig"], at(G + j + 1, 2))
                        nc.vector.tensor_tensor(sgate[:, x], sgate[:, x], ps[:, 2 * x], ALU.mult).then_inc(s["gate_silu"], 1)
                        dve.wait_ge(s["w_used"], at(FIRST[gu] + 2 * j + 2, 4))
                        dve.wait_ge(s["gate_silu"], at(G + j + 1, 2))
                        if not first:
                            dve.wait_ge(s["g_lo"], at(G + j - 1, 2))
                        nc.vector.tensor_tensor(gtmp[:, x], sgate[:, x], ps[:, 2 * x + 1], ALU.mult
                                                ).then_inc(s["g_full"], 1)

                    tile(0, first=True)
                    tile(1, first=True)
                    with dve.Fori(0, (HC - 3) // 2) as i:
                        tile(2, i)
                        tile(3, i)
                    tile(HC - 1)
                    residual(down, k_upd + half, 1, 4, 4)

            nc.vector.memset(eps[:], EPS).then_inc(s["credit"], 1)
            nc.vector.memset(chd, 0.0).then_inc(s["credit"], 1)
            nc.vector.memset(start[:, 0:1], 0.0).then_inc(s["g_full"], 2)
            nc.vector.memset(start[:, 1:2], 0.0).then_inc(s["h_ready"], 2)
            nc.vector.memset(start[:, 3:4], 0.0).then_inc(s["merged"], 2)
            dve.wait_ge(s["consts_loaded"], ALL_CONSTANTS)

            def exponents(it, b, log_decay, dv):
                nc.vector.tensor_tensor_scan(b, reset[:], log_decay, 0.0, ALU.mult, ALU.add).then_inc(s["cum"], 1)
                dve.wait_ge(s["cum"], it + 1)
                b2 = b.rearrange("p (c t) -> p c t", c=NCH)
                nc.vector.tensor_tensor(dv[:, L_END].rearrange("p (c t) -> p c t", c=NCH),
                                        b2[:, :, C - 1:C].broadcast_to((P, NCH, C)), b2, ALU.subtract
                                        ).then_inc(s["dec_in"], 1)
                for l in range(LEVELS - 1, -1, -1):
                    m = 1 << l
                    bb = b.rearrange("p (b h m) -> p b h m", h=2, m=m)
                    x = dv[:, l].rearrange("p (b h m) -> p b h m", h=2, m=m)
                    ref = bb[:, :, 0, m - 1:m].broadcast_to((P, T // (2 * m), m))
                    nc.vector.tensor_tensor(x[:, :, 0], ref, bb[:, :, 0], ALU.subtract)
                    nc.vector.tensor_tensor(x[:, :, 1], bb[:, :, 1], ref, ALU.subtract).then_inc(s["dec_in"], 1)

            def gather_scores(i, sc):
                for n, l in enumerate(list(range(LEVELS - 1, -1, -1)) + [LEVELS]):
                    dve.wait_ge(s["score_ps"], i * 8 + (n + 1))
                    if n:
                        dve.wait_ge(s["scores"], i * 8 + n)
                    mk = lvl_mask[:, l:l + 1].broadcast_to((P, NCH, P))
                    sv = sc.rearrange("p (c t) -> p c t", c=NCH)
                    pv = ps[:, 4 + n % 2].rearrange("p (c t) -> p c t", c=NCH)
                    if n == 0:
                        nc.vector.tensor_tensor(sv, pv, mk, ALU.mult).then_inc(s["scores"], 1)
                    else:
                        nc.vector.memset(waited[:], 0.0)
                        nc.vector.copy_predicated(sv, mk.bitcast(U32), pv).then_inc(s["scores"], 1)

            def chain_states(i, it, stv, ends):
                dve.wait_ge(s["st_ps"], i + 1)
                nc.vector.tensor_copy(stv[:, 1], ps[:, 6, 0:C]).then_inc(s["states"], 1)
                for c in (1, 2):
                    dve.wait_ge(s["states"], i * 3 + c)
                    dve.wait_ge(s["chunk_decay"], it + 1)
                    nc.vector.scalar_tensor_tensor(out=stv[:, c + 1], in0=stv[:, c], scalar=ends[:, c:c + 1],
                                                   in1=ps[:, 6, c * C:(c + 1) * C], op0=ALU.mult, op1=ALU.add
                                                   ).then_inc(s["states"], 1)

            def head_output(i, gain, r, tmp, gate, dst, done):
                dve.wait_ge(s["o_rstd"], i * 2 + 2)
                nc.vector.scalar_tensor_tensor(out=tmp, in0=ps[:, 7], scalar=gain[:, 0:1], in1=r,
                                               op0=ALU.mult, op1=ALU.mult).then_inc(s["o_scaled"], 1)
                dve.wait_ge(s["o_scaled"], i + 1)
                nc.vector.tensor_tensor(dst, tmp, gate, ALU.mult).then_inc(done, 1)

            norm(0)
            lbs = s["lb_steps"]
            nc.vector.tensor_tensor(lbt[:, 3], lbl[:, 0], lbl[:, 1], ALU.max).then_inc(lbs, 1)
            dve.wait_ge(lbs, 1)
            nc.vector.tensor_tensor(lbt[:, 3], lbt[:, 3], lbl[:, 2], ALU.max).then_inc(lbs, 1)
            dve.wait_ge(lbs, 2)
            for r in range(3):
                nc.vector.tensor_tensor(lbt[:, r], lbl[:, r], lbt[:, 3], ALU.subtract).then_inc(lbs, 1)
            dve.wait_ge(lbs, 6)
            nc.vector.tensor_tensor(lbt[:, 3], lbt[:, 0], lbt[:, 1], ALU.add).then_inc(lbs, 1)
            dve.wait_ge(lbs, 7)
            nc.vector.tensor_tensor(lbt[:, 3], lbt[:, 3], lbt[:, 2], ALU.add).then_inc(lbs, 1)
            dve.wait_ge(lbs, 8)
            nc.vector.reciprocal(lbt[:, 4], lbt[:, 3]).then_inc(lbs, 1)
            dve.wait_ge(lbs, 9)
            nc.vector.tensor_tensor(lb, lbt[:, 0], lbt[:, 4], ALU.mult).then_inc(lbs, 1)
            dve.wait_ge(lbs, 10)
            nc.vector.tensor_scalar(omlb, lb, -1.0, 1.0, ALU.mult, ALU.add).then_inc(lbs, 1)
            dve.wait_ge(lbs, 11)
            with dve.Fori(0, HEADS_H) as i:
                dve.wait_ge(s["sig_f"], i + 1)
                nc.vector.tensor_scalar(fg, sf_, omlb[:, bass.ds(i, 1)], lb[:, bass.ds(i, 1)], ALU.mult, ALU.add
                                        ).then_inc(s["forget"], 1)
                dve.wait_ge(s["forget"], i + 1)
                nc.vector.tensor_scalar(key, fg, -1.0, 1.0, ALU.mult, ALU.add).then_inc(s["key"], 1)
                dve.wait_ge(s["sig_q"], i + 1)
                nc.vector.tensor_tensor(qry, sq_, ps[:, 0], ALU.mult).then_inc(s["query"], 1)
                dve.wait_ge(s["sig_g"], i + 1)
                nc.vector.tensor_tensor(sgl, sg_, ps[:, 2], ALU.mult).then_inc(s["silu_g"], 1)
                dve.wait_ge(s["log_f"], i + 1)
                exponents(i, bcum, lf, dec)
                gather_scores(i, sc_mat)
                chain_states(i, i, st, chd)
                head_output(i, hgain, ors, otmp, sgl, otmp, s["o_full"])
                dve.wait_ge(s["o_lo"], i + 1)
            residual("hgrn_out", 0, 1, 0, RING)
            norm(1)
            ffn(0, 1)

            norm(2)

            def rope(N):
                dve.wait_ge(s["rot_ps"], N + 1)
                nc.vector.tensor_tensor(tsin[:, N % 2], ps[:, 2 + N % 2], sin_a[:], ALU.mult).then_inc(s["rope_sin"], 1)
                dve.wait_ge(s["rope_sin"], N + 1)
                dve.wait_ge(s["rope_cos"], N + 1)
                nc.vector.tensor_tensor(QK[N // 6 % 2][:, N % 6], tcos[:, N % 2], tsin[:, N % 2], ALU.add
                                        ).then_inc(s["qk_ready"], 1)

            dve.wait_ge(s["spilled"], 16)
            for n in range(6):
                rope(n)
            for j in range(HPG):
                N = 6 * (j + 1)
                if j + 1 < HPG:
                    rope(N)
                    rope(N + 1)
                for g in range(GROUPS):
                    dve.wait_ge(s["sc_ps"], 3 * j + g + 1)
                    if g == 0:
                        nc.vector.scalar_tensor_tensor(out=SC[0], in0=SC_BANKS[0], scalar=float(P) ** -0.5,
                                                       in1=win_mask[:], op0=ALU.mult, op1=ALU.add
                                                       ).then_inc(s["sc_masked"], 1)
                    else:
                        nc.vector.scalar_tensor_tensor(out=SC[g], in0=SC_BANKS[g], scalar=float(P) ** -0.5,
                                                       in1=res_mask[:, g - 1:g].broadcast_to((P, TT, P)),
                                                       op0=ALU.mult, op1=ALU.add).then_inc(s["sc_masked"], 1)
                    dve.wait_ge(s["sc_masked"], 3 * j + g + 1)
                    nc.vector.tensor_reduce(mx[:, g], SC[g], AX.X, ALU.max).then_inc(s["sc_max"], 1)
                    dve.wait_ge(s["sc_max"], 3 * j + g + 1)
                    nc.vector.tensor_scalar(nmx[:, g], mx[:, g], -1.0, None, ALU.mult).then_inc(s["sc_negmax"], 1)
                dve.wait_ge(s["p_exp"], 12 * (j + 1))
                nc.vector.reciprocal(lrec, lsum).then_inc(s["p_recip"], 1)
                dve.wait_ge(s["p_logsum"], j + 1)
                nc.vector.tensor_tensor(lsev, lsev, mx, ALU.add).then_inc(s["lse"], 1)
                if j + 1 < HPG:
                    for n in range(2, 6):
                        rope(N + n)
                dve.wait_ge(s["lse_rows"], 3 * j + 3)
                nc.vector.tensor_tensor(mxw, lrow[:, 0], lrow[:, 1], ALU.max).then_inc(s["mix_max1"], 1)
                dve.wait_ge(s["mix_max1"], j + 1)
                nc.vector.tensor_tensor(mxw, mxw, lrow[:, 2], ALU.max).then_inc(s["mix_max"], 1)
                dve.wait_ge(s["mix_exp"], j + 1)
                nc.vector.tensor_tensor(sum_, lrow[:, 0], lrow[:, 1], ALU.add).then_inc(s["mix_sum1"], 1)
                dve.wait_ge(s["mix_sum1"], j + 1)
                nc.vector.tensor_tensor(sum_, sum_, lrow[:, 2], ALU.add).then_inc(s["mix_sum"], 1)
                dve.wait_ge(s["mix_sum"], j + 1)
                nc.vector.reciprocal(rec, sum_).then_inc(s["mix_recip"], 1)
                dve.wait_ge(s["mix_weight"], j + 1)
                for g in range(GROUPS):
                    dve.wait_ge(s["ao_ps"], 3 * j + g + 1)
                    n = TT if g == 0 else P
                    nc.vector.tensor_tensor(aO[:, g * HPG + j].rearrange("p (b m) -> p b m", b=n), natural(g, ps[:, 4 + g]),
                                            lrow[:, g].rearrange("p (b m) -> p b m", b=n), ALU.mult
                                            ).then_inc(s["ao_ready"], 1)
            dve.wait_ge(s["reloaded"], 16)
            residual("attn_out", 3, 2, 0, 2)
            norm(3)
            ffn(1, 4)

            norm(4, s["h_ready"])
            norm(5)
            dve.wait_ge(s["nsa_consts"], 16 * 6)

            def nsa_rope(x):
                n = (0, 1, 2, 3, 6, 7)[x]
                dve.wait_ge(s["nrot_ps"], x + 1)
                nc.vector.tensor_tensor(nsin[:, x % 2], ps[:, 2 + x % 2], sin_n[:], ALU.mult).then_inc(s["nrope_sin"], 1)
                dve.wait_ge(s["nrope_sin"], x + 1)
                dve.wait_ge(s["nrope_cos"], x + 1)
                dst = qrot[:, n] if n < 4 else kr[:, n - 6]
                nc.vector.tensor_tensor(dst, ncos[:, x % 2], nsin[:, x % 2], ALU.add).then_inc(s["nrope"], 1)

            for x in range(4):
                nsa_rope(x)
            dve.wait_ge(s["kvpe_zero"], 2)
            for x in range(2):
                dve.wait_ge(s["nt_ready"], 5 + x)
                for g in range(2):
                    src = slice(g * HD, (g + 1) * HD)
                    kv = kvraw[src, x].rearrange("p (n l o) -> p o l n", l=8, o=2)
                    pos = pos_kv[src, x].rearrange("p (l o) -> p o l", o=2)
                    for odd in range(2):
                        for hi in range(2):
                            dst = kvp[odd * HD:(odd + 1) * HD, x, 8 * hi:8 * hi + 8, g * NB:g * NB + 31]
                            nc.vector.tensor_tensor(dst, kv[:, odd, :, hi:hi + 31],
                                                    pos[:, odd, 8 * hi:8 * hi + 8, None].broadcast_to((HD, 8, 31)),
                                                    ALU.add).then_inc(s["kvpe"], 1)
            for x in (4, 5):
                nsa_rope(x)
            for x in range(2):
                dve.wait_ge(s["hid_sig"], x + 1)
                if x == 0:
                    nc.vector.tensor_tensor(hidk, hsig[:, 0], ps[:, 1, 0:2 * NB], ALU.mult).then_inc(s["hid"], 1)
                else:
                    for g in range(2):
                        src = slice(g * NB, (g + 1) * NB)
                        m = nc.vector.tensor_tensor(hidv[:, g * P:(g + 1) * P].rearrange("p (k n) -> p k n", k=4),
                                                    hsig[:, 1, None, src].broadcast_to((P, 4, NB)),
                                                    ps[:, 0, src][:, None, :].broadcast_to((P, 4, NB)), ALU.mult)
                    m.then_inc(s["hid"], 1)
            dve.wait_ge(s["gz_ps"], 1)
            dve.wait_ge(s["spilled"], 32)
            for p in range(2):
                nc.vector.tensor_scalar(la[:, p], ps[:, 2 + p], gbias[:, p:p + 1], None, ALU.add).then_inc(s["z_b"], 1)
            for p in range(2):
                dve.wait_ge(s["z_ln"], p + 1)
                nc.vector.scalar_tensor_tensor(out=la[:, p], in0=la[:, p], scalar=0.0, in1=zab, op0=ALU.min,
                                               op1=ALU.subtract).then_inc(s["z_min"], 1)
                dve.wait_ge(s["z_min"], p + 1)
                nc.vector.tensor_scalar(la[:, p], la[:, p], 1.0 / TAU, None, ALU.mult).then_inc(s["log_a"], 1)
            SH = (P, TT, HEADS_N, NB)
            cs = ps[:, 4:6].rearrange("p g (t h n) -> p g t h n", t=TT, h=4)
            mk = cmp_mask[:].rearrange("p k (t n) -> p k t n", t=TT)
            dve.wait_ge(s["cs_ps"], 1)
            for g in range(2):
                nc.vector.tensor_tensor(sC[:, :, 4 * g:4 * g + 4], cs[:, g], mk[:, 0, :, None, :].broadcast_to((P, TT, 4, NB)),
                                        ALU.add).then_inc(s["cs_masked"], 1)
            dve.wait_ge(s["cs_masked"], 2)
            nc.vector.tensor_reduce(cmx, sC, AX.X, ALU.max).then_inc(s["cs_max"], 1)
            dve.wait_ge(s["cs_max"], 1)
            nc.vector.tensor_tensor(sC, sC, cmx[:, :, :, None].broadcast_to(SH), ALU.subtract).then_inc(s["cs_sub"], 1)
            dve.wait_ge(s["cs_exp"], 1)
            nc.vector.tensor_reduce(csum, sC, AX.X, ALU.add).then_inc(s["cs_sum"], 1)
            dve.wait_ge(s["cs_sum"], 1)
            nc.vector.reciprocal(crec, csum).then_inc(s["cs_rec"], 1)
            nc.vector.tensor_tensor(sC, sC, mk[:, 1, :, None, :].broadcast_to(SH), ALU.mult).then_inc(s["cs_valid"], 1)
            dve.wait_ge(s["cs_rec"], 1)
            dve.wait_ge(s["ngate_ready"], TT)
            nc.vector.tensor_tensor(cw, crec, ngate.rearrange("p t (h b) -> p t h b", b=3)[:, :, :, 0], ALU.mult
                                    ).then_inc(s["cs_gate"], 1)
            dve.wait_ge(s["cs_gate"], 1)
            dve.wait_ge(s["cs_valid"], 1)
            nc.vector.tensor_tensor(sC, sC, cw[:, :, :, None].broadcast_to(SH), ALU.mult).then_inc(s["cs_w"], 1)

            def nsa_stats(i, x):
                base = ps[:, 3 * x:3 * x + 3].rearrange("p a n -> p (a n)")
                dve.wait_ge(s["ns_ps"], i * 2 + (x + 1))
                for tt in range(TT):
                    diag = base[:, BOFF[tt] + tt * P:BOFF[tt] + (tt + 1) * P]
                    nc.vector.tensor_tensor(diag, diag, res_mask[:, 0], ALU.add).then_inc(s["ns_masked"], 1)
                for tt in range(TT):
                    dve.wait_ge(s["ns_masked"], i * 8 + (4 * x + tt + 1))
                    nc.vector.tensor_reduce(nmax[:, x, tt:tt + 1], base[:, BOFF[tt]:BOFF[tt] + (tt + 1) * P], AX.X, ALU.max
                                            ).then_inc(s["ns_max"], 1)
                dve.wait_ge(s["ns_max"], i * 8 + (4 * x + 4))
                nc.vector.tensor_scalar(nneg[:, x], nmax[:, x], -1.0, None, ALU.mult).then_inc(s["ns_neg"], 1)

            def nsa_weight(i, x):
                dve.wait_ge(s["ns_exp"], i * 8 + (4 * x + 4))
                nc.vector.reciprocal(nrec[:, x], nsum[:, x]).then_inc(s["n_rec"], 1)
                dve.wait_ge(s["n_rec"], i * 2 + (x + 1))
                nc.vector.tensor_tensor(nw[:, x, :, None], nrec[:, x, :, None], ngate[:, :, bass.ds(i * 3 + (1 + x), 1)],
                                        ALU.mult).then_inc(s["n_w"], 1)

            def nsa_add(i, x):
                dve.wait_ge(s["n_w"], i * 2 + (x + 1))
                dve.wait_ge(s["no_ps"], i * 2 + (x + 1))
                nc.vector.tensor_tensor(oscl, ps[:, 6 + x, 0:TT * HD].rearrange("p (t d) -> p t d", t=TT),
                                        nw[:, x, :, None].broadcast_to((P, TT, HD)), ALU.mult).then_inc(s["n_scaled"], 1)
                dve.wait_ge(s["n_scaled"], i * 2 + (x + 1))
                o = oa[:, :, bass.ds(i * HD, HD)]
                nc.vector.tensor_tensor(o, o, oscl, ALU.add).then_inc(s["oa_acc"], 1)

            dve.wait_ge(s["oa_ready"], TT)
            nsa_stats(0, 0)
            nsa_stats(0, 1)
            with dve.Fori(0, HEADS_N - 1) as i:
                for x in range(2):
                    nsa_weight(i, x)
                    nsa_stats(i + 1, x)
                    nsa_add(i, x)
            for x in range(2):
                nsa_weight(HEADS_N - 1, x)
                nsa_add(HEADS_N - 1, x)

            dve.wait_ge(s["oat_ready"], 4)
            for p in range(2):
                dve.wait_ge(s["log_a"], p + 1)
                exponents(HEADS_H + p, gcum[:, p], la[:, p], gdec[p])
            for n in range(HEADS_G):
                dve.wait_ge(s["gr_sig"], n + 1)
                nc.vector.tensor_tensor(gsr[:, n], gsig[:, n % 2], ps[:, n], ALU.mult).then_inc(s["gr_silu"], 1)
            dve.wait_ge(s["gr_silu"], HEADS_G)
            for hh in range(HEADS_G):
                gather_scores(HEADS_H + hh, gsc)
                chain_states(HEADS_H + hh, HEADS_H + hh // 2, gst, gchd[:, hh // 2])
                head_output(HEADS_H + hh, ggain, gors, gotmp, gsr[:, hh], goT[:, hh], s["gb_ready"])

            for j in range(DC):
                b, x = 4 * (j % 2), 2 * (j % 2)
                dve.wait_ge(s["w_used"], FIRST["merge"] + 3 * j + 3)
                dve.wait_ge(s["mg_sig"], 2 * j + 2)
                nc.vector.tensor_tensor(msig[:, x], msig[:, x], ps[:, b + 2], ALU.mult).then_inc(s["mg_a"], 1)
                nc.vector.tensor_tensor(msig[:, x + 1], msig[:, x + 1], ps[:, b + 3], ALU.mult).then_inc(s["merged"], 1)
                dve.wait_ge(s["mg_a"], j + 1)
                dve.wait_ge(s["merged"], j + 3)
                if j >= 2:
                    dve.wait_ge(s["m_lo"], j - 1)
                nc.vector.tensor_tensor(mtmp[:, j % 2], msig[:, x], msig[:, x + 1], ALU.add).then_inc(s["m_full"], 1)
            dve.wait_ge(s["reloaded"], 32)
            residual("mix_out", 7, 1, 0, RING)
            norm(6)
            ffn(2, 8)
            norm(7, s["credit"])


def kernel(**inputs):
    import numpy as np
    from concourse import bacc
    from concourse.bass_utils import run_bass_kernel_spmd

    g = {n: np.asarray(v) for n, v in inputs.items()}

    def fm(w):
        K, N = w.shape
        return np.ascontiguousarray(w.reshape(K // P, P, N // P, P).transpose(2, 1, 0, 3).reshape(N // P, P, K))

    def down(w):
        return np.ascontiguousarray(w.reshape(HC, P, DC, P).transpose(2, 1, 0, 3).reshape(DC, P, HC * P))

    def cols(v):
        return v.reshape(-1, P).T

    arrays = {"x": np.ascontiguousarray(g["x"][0].reshape(T, DC, P).transpose(2, 1, 0))}
    w = fm(g["hgrn_w_in"][0]).reshape(4, 8, P, D)
    arrays["w_hgrn"] = np.ascontiguousarray(w[[1, 0, 3, 2]].transpose(1, 0, 2, 3).reshape(32, P, D))
    arrays["w_hgrn_out"] = fm(g["hgrn_w_out"][0])
    ffns = [(g["ffn_w_in"][n][:, :FF], g["ffn_w_in"][n][:, FF:], g["ffn_w_down"][n]) for n in range(2)]
    ffns.append((g["w_ffn_gate_2"][0], g["w_ffn_up_2"][0], g["w_ffn_down_2"][0]))
    for n, (gate, up, w_down) in enumerate(ffns):
        both = np.stack([fm(gate), fm(up)], 1).reshape(2, 2 * HC, P, D)
        for half in range(2):
            arrays[f"w_gu{n}{'ab'[half]}"] = np.ascontiguousarray(both[half])
            arrays[f"w_down{n}{'ab'[half]}"] = down(w_down[half * HC * P:(half + 1) * HC * P])

    def tm(w):
        return np.ascontiguousarray(w.reshape(4, 2, P, -1).transpose(0, 2, 1, 3).reshape(4, P, -1))

    AW = GROUPS * HPG * P
    qkv = g["attn_w_qkv"][0]
    arrays["w_attn_v"] = np.concatenate([tm(qkv[:, 2 * AW + n * 512:2 * AW + (n + 1) * 512]) for n in range(GROUPS)])
    w = fm(qkv[:, :2 * AW]).reshape(2, GROUPS, HPG, P, D)
    arrays["w_attn_qk"] = np.ascontiguousarray(w.transpose(2, 1, 0, 3, 4).reshape(24, P, D))
    arrays["w_attn_out"] = np.ascontiguousarray(
        fm(g["attn_w_out"][0]).reshape(DC, P, 2, 6 * P).transpose(0, 2, 1, 3).reshape(2 * DC, P, 6 * P))
    arrays["gains"] = np.ascontiguousarray(np.stack([cols(v) for v in (
        g["norm_mix"][0], g["norm_ffn"][0], g["norm_mix"][1], g["norm_ffn"][1], g["final_norm"],
        g["norm_mix_2"][0], g["norm_ffn_2"][0], g["norm_final_2"])], 1))
    arrays["lbl"] = np.ascontiguousarray(g["hgrn_lb_logits"].reshape(3, DC, P).transpose(2, 0, 1))
    arrays["hgain"] = np.ascontiguousarray(g["hgrn_out_norm"].reshape(P, 1))
    arrays["ident"] = np.eye(P, dtype=np.float32)
    arrays["ones"] = np.ones((P, P), np.float32)
    si, ti = np.arange(P)[:, None], np.arange(P)[None, :]
    masks = [(si // (2 << l) == ti // (2 << l)) & (si // (1 << l) % 2 == 0) & (ti // (1 << l) % 2 == 1)
             for l in range(LEVELS)] + [si == ti]
    arrays["lvl_mask"] = np.ascontiguousarray(np.stack(masks, 1).astype(np.float32))
    arrays["reset"] = np.ascontiguousarray(np.broadcast_to((np.arange(T) % C != 0).astype(np.float32), (P, T)))

    w = g["w_in_2"][0]
    cuts = np.cumsum([0, HEADS_N * HD, 12 * HD, 3 * HEADS_N, HEADS_G * HD, HEADS_G * HD, HEADS_G * P, RANK,
                      HEADS_G * P, 2 * D])
    wq, wkv, wgate, wgq, wgk, wgv, wlr, wr, wmerge = [w[:, lo:hi] for lo, hi in zip(cuts[:-1], cuts[1:])]
    wq = wq.reshape(D, 2, 4, HD).transpose(0, 2, 1, 3).reshape(D, 512)
    kv = [wkv[:, n * P:(n + 1) * P] for n in range(6)]
    arrays["w_nsa_fm"] = fm(np.concatenate([wq, kv[0], kv[1], kv[2], kv[4]], 1))
    w = np.concatenate([kv[3], kv[5], wgate], 1)
    arrays["w_nsa_tm"] = np.ascontiguousarray(w.reshape(2, 4, P, TM_COLS).transpose(0, 2, 1, 3).reshape(2, P, -1))
    arrays["w_gla_v"] = tm(wgv)
    arrays["w_gla_fm"] = fm(np.concatenate([wgq, wgk], 1))
    arrays["w_gla_lr"] = fm(np.concatenate([wlr, np.zeros((D, P - RANK), np.float32)], 1))
    arrays["w_gla_r"] = fm(wr)
    up = np.concatenate([g["w_up_nsa_2"][0], g["w_up_gla_2"][0]], 0)
    arrays["w_merge"] = np.ascontiguousarray(
        np.stack([fm(wmerge[:, :D]), fm(wmerge[:, D:]), fm(up)], 1).reshape(3 * DC, P, D))
    arrays["w_mix_out"] = fm(g["w_out_2"][0])
    arrays["cmp_w1"] = np.ascontiguousarray(np.stack(
        [g[n][0].reshape(16, P, P).transpose(1, 0, 2) for n in ("cmp_k_w1_2", "cmp_v_w1_2")], 1))
    zero = np.zeros((P, HD), np.float32)
    arrays["cmp_w2k"] = np.ascontiguousarray(np.concatenate([zero, g["cmp_k_w2_2"][0], zero], 1))
    arrays["cmp_w2v"] = np.ascontiguousarray(g["cmp_v_w2_2"][0])
    arrays["pos_kv"] = np.ascontiguousarray(np.stack(
        [np.concatenate([g[n][0].T] * 2) for n in ("cmp_pe_k_2", "cmp_pe_v_2")], 1))
    arrays["gw2"] = np.ascontiguousarray(g["gla_gate_w2_2"][0])
    arrays["gbias"] = np.ascontiguousarray(g["gla_gate_b_2"][0].reshape(2, P).T)
    arrays["ggain"] = np.ascontiguousarray(g["gla_norm_2"].reshape(P, 1))
    half = 8
    rot = np.zeros((P, P), np.float32)
    for base in (0, HD):
        for m in range(half):
            rot[base + m + half, base + m], rot[base + m, base + m + half] = -1.0, 1.0
    arrays["rot_n"] = rot
    inv = (np.float32(500000.0) ** (-np.arange(half, dtype=np.float32) / np.float32(half))).astype(np.float32)
    ang = (np.arange(T, dtype=np.float32)[None, :] * inv[:, None]).astype(np.float32)
    one, nil = np.ones((HD - 2 * half, T), np.float32), np.zeros((HD - 2 * half, T), np.float32)
    arrays["cos_n"] = np.concatenate([np.cos(ang), np.cos(ang), one] * 2).astype(np.float32)
    arrays["sin_n"] = np.concatenate([np.sin(ang), np.sin(ang), nil] * 2).astype(np.float32)
    blk = np.arange(NB)
    seen = (blk * 16 + 31 <= np.arange(T)[:, None]) & (blk < NB - 1)
    seen = seen.reshape(TT, P, NB).transpose(1, 0, 2).reshape(P, TT * NB)
    arrays["cmp_mask"] = np.ascontiguousarray(np.stack([np.where(seen, 0.0, NEG), seen], 1).astype(np.float32))
    rot = np.zeros((P, P), np.float32)
    for m in range(64):
        rot[m + 64, m], rot[m, m + 64] = -1.0, 1.0
    arrays["rot_a"] = rot
    inv = (1.0 / (np.float32(10000.0) ** (np.arange(0, P, 2, dtype=np.float32) / np.float32(P)))).astype(np.float32)
    ang = (np.arange(T, dtype=np.float32)[None, :] * inv[:, None]).astype(np.float32)
    arrays["cos_a"] = np.concatenate([np.cos(ang)] * 2).astype(np.float32)
    arrays["sin_a"] = np.concatenate([np.sin(ang)] * 2).astype(np.float32)
    cur, prev = si >= ti, si <= ti
    first = np.concatenate([np.zeros((P, P), bool), cur], 1)
    later = np.concatenate([prev, cur], 1)
    arrays["win_mask"] = np.ascontiguousarray(
        np.where(np.stack([first, later, later, later], 1), 0.0, NEG).astype(np.float32))
    arrays["res_mask"] = np.ascontiguousarray(
        np.where(np.stack([cur, cur & (si % 4 == ti % 4)], 1), 0.0, NEG).astype(np.float32))

    nc = bacc.Bacc("TRN2", target_bir_lowering=False, num_devices=1)
    aps = {n: nc.dram_tensor("in_" + n, v.shape, F32, kind="ExternalInput").ap() for n, v in arrays.items()}
    aps["h_spill"] = nc.dram_tensor("h_spill", (P, DC, T), F32, kind="Internal").ap()
    out = nc.dram_tensor("out_h", (P, DC, T), F32, kind="ExternalOutput").ap()
    program(nc, aps, out)
    r = run_bass_kernel_spmd(nc, [{"in_" + n: v for n, v in arrays.items()}], core_ids=[0])
    y = r.results[0]["out_h"]
    return np.ascontiguousarray(y.transpose(2, 1, 0).reshape(1, T, D))
```

```python
import concourse.bass as bass
from concourse import mybir
from contextlib import ExitStack

F32 = mybir.dt.float32
R32 = mybir.dt.float32r
U32 = mybir.dt.uint32
ALU = mybir.AluOpType
ACT = mybir.ActivationFunctionType
AX = mybir.AxisListType

P = 128
T = 512
D = 1024
DC = D // P
TT = T // P
FF = 2816
FC = FF // P
HEADS_H = 8
C = 128
NCH = T // C
LEVELS = 7
NORMS = 8
GROUPS = 3
HPG = 4
RESIDUES = 4
NEG = -1e30
HEADS_N = 8
HD = 64
NB = 32
TM_COLS = 2 * P + 3 * HEADS_N
HEADS_G = 4
RANK = 16
TAU = 16.0
EPS = 1e-6
RING = 4
SLOT = 11 * P
HC = FC // 2
ARENA = 28832
H_AT = ARENA - DC * T

SECTIONS = [
    ("hgrn", 4 * HEADS_H, 8 * P), ("hgrn_out", DC, 8 * P),
    ("gu0a", 2 * HC, 8 * P), ("down0a", DC, HC * P), ("gu0b", 2 * HC, 8 * P), ("down0b", DC, HC * P),
    ("attn_v", 4 * GROUPS, 8 * P), ("attn_qk", 2 * GROUPS * HPG, 8 * P), ("attn_out", 2 * DC, 6 * P),
    ("gu1a", 2 * HC, 8 * P), ("down1a", DC, HC * P), ("gu1b", 2 * HC, 8 * P), ("down1b", DC, HC * P),
    ("nsa_fm", 8, 8 * P), ("nsa_tm", 2, 4 * TM_COLS), ("gla_v", 4, 8 * P), ("gla_fm", 4, 8 * P),
    ("gla_lr", 1, 8 * P), ("gla_r", HEADS_G, 8 * P), ("merge", 3 * DC, 8 * P), ("mix_out", DC, 8 * P),
    ("gu2a", 2 * HC, 8 * P), ("down2a", DC, HC * P), ("gu2b", 2 * HC, 8 * P), ("down2b", DC, HC * P),
]
WIDTH = {name: width for name, _, width in SECTIONS}
FIRST = {}
_n = 0
for _name, _units, _ in SECTIONS:
    FIRST[_name] = _n
    _n += _units


SPLIT = [(name, k) for name, units, _ in SECTIONS for k in range(units)
         if name != "attn_out" and not (name == "merge" and k % 3 == 2)]
SPLIT_AT = {unit: n for n, unit in enumerate(SPLIT)}


def split_use(section, k, i=None, per=0):
    n = SPLIT_AT[(section, k)]
    done = n + 1 if i is None else i * per + (n + 1)
    if n < 2:
        return n % 2, done, None
    last, lk = SPLIT[n - 2]
    free = FIRST[last] + lk + 1
    return n % 2, done, free if i is None else i * per + free


def ring_use(section, k, i=None, per=0):
    n = FIRST[section] + k
    count = 16 * (n // RING + 1)
    return n % RING, count if i is None else i * (16 * per // RING) + count


def program(nc, a, out):
    names = """x_loaded norm_consts consts_loaded w_hi w_lo u_tmp u_hi u_lo_even u_lo_odd g_full g_hi g_lo o_full o_hi o_lo
        m_full m_hi m_lo spilled reloaded nsa_consts w_used h_ready sq_ready sq_sum ms_ready rstd lb_steps 
        sig_f sig_q sig_g vf_ready forget key query silu_g log_f cum dec_in dec_out chunk_decay
        x_ready vt_ps vt_ready kt_ps kt_ready score_ps scores st_ps states o_ps o_sq o_ms o_rstd o_scaled 
        gate_norm up_norm gate_sig gate_silu stored credit
        av_ready raw_ready rope_cos rope_sin qk_ready sc_ps sc_masked sc_max sc_negmax p_exp p_logsum
        p_recip lse lse_diag p_norm pt_ps pt_ready lse_ps lse_rows ao_ps mix_max1 mix_max mix_diff mix_exp mix_sum1
        mix_sum mix_recip mix_weight ao_raw ao_ready
        nt_ready nrot_ps nrope_cos nrope_sin nrope ntm_ready ngate_ready gv_ready cmp_loaded kvpe_zero kvpe hid_ps
        hid_sig hid kc_ps kc_ready vc_ps vbd cs_ps cs_masked cs_max cs_sub cs_exp cs_sum cs_rec cs_gate cs_valid cs_w
        ct_ps ct_ready co_ps oa_ready ns_ps ns_masked ns_max ns_neg ns_exp nt_ps npt_ready no_ps n_rec n_w ns_scaled
        oa_acc gz_ps z_b z_abs z_exp z_ln z_min log_a gr_sig gr_silu gb_ready mg_sig mg_a 
        merged""".split()
    with ExitStack() as ctx:
        def sb(name, *shape):
            return ctx.enter_context(nc.sbuf_tensor(name, [P, *shape], F32))

        s = {n: ctx.enter_context(nc.semaphore(n)) for n in names}
        w_ready = [ctx.enter_context(nc.semaphore(f"w_ready{r}")) for r in range(RING)]

        arena_at = (nc.sbuf_base + 31) // 32 * 32
        arena = sb("arena", ARENA)
        h = arena[:, H_AT:ARENA].rearrange("p (c t) -> p c t", c=DC)
        hid = nc.alloc_sbuf_tensor_at("hid", [P, 2, HC, T], R32, offset=arena_at)
        us = ctx.enter_context(nc.sbuf_tensor("u_split", [P, 2, DC, T], R32))
        ws = ctx.enter_context(nc.sbuf_tensor("w_split", [P, 2, 2, SLOT], R32))
        ring = sb("ring", RING, SLOT)
        rs = sb("rs_norm", T)
        gains = sb("gains_sb", NORMS, DC)
        ident = sb("ident_sb", P)
        ones = sb("ones_sb", P)
        lvl_mask = sb("lvl_mask_sb", LEVELS + 1, P)
        reset = sb("reset_sb", T)
        lbl = sb("lbl_sb", 3, DC)
        lbt = sb("lbt", 8, DC)
        small = sb("small", 16)
        hgain, ggain, eps, waited = [small[:, n:n + 1] for n in range(4)]
        gbias, start = small[:, 4:6], small[:, 8:12]
        mixer_consts = sb("mixer_consts", 2 * T + 9 * P)
        cos_a = mixer_consts[:, P:P + T]
        sin_a = mixer_consts[:, P + T:P + 2 * T]
        win_mask = mixer_consts[:, P + 2 * T:P + 4 * T].rearrange("p (b n) -> p b n", b=TT)
        res_mask = sb("res_mask_sb", 2, P)
        rot_n, cos_n, sin_n = mixer_consts[:, 0:P], cos_a, sin_a
        at = P + 2 * T
        cmp_mask = mixer_consts[:, at:at + 2 * TT * NB].rearrange("p (k n) -> p k n", k=2)
        pos_kv = mixer_consts[:, at + 256:at + 320].rearrange("p (k n) -> p k n", k=2)
        gw2 = mixer_consts[:, at + 320:at + 576]
        ps = ctx.enter_context(nc.psum_tensor("ps", [P, 8, 512], F32))

        def views(used=0):
            at = [used]

            def take(*shape):
                n = 1
                for x in shape:
                    n *= x
                v = arena[:, at[0]:at[0] + n]
                at[0] += n
                assert at[0] <= ARENA, at[0]
                if len(shape) == 2:
                    v = v.rearrange("p (a b) -> p a b", a=shape[0])
                if len(shape) == 3:
                    v = v.rearrange("p (a b c) -> p a b c", a=shape[0], b=shape[1])
                return v
            return take

        take = views(used=2 * HC * T)
        sq_, sf_, sg_ = take(T), take(T), take(T)
        vf, fg, key0, qry0, lf = take(T), take(T), take(T), take(T), take(T)
        key = [key0, arena[:, 8 * T:9 * T]]
        qry = [qry0, arena[:, 9 * T:10 * T]]
        sgl, bcum = take(T), take(T)
        dec = take(LEVELS + 2, T)
        vT = take(NCH, C)
        kT = take(NCH, C)
        sc_mat = take(T)
        st = take(NCH, P)
        chd = take(NCH)
        osq, ors, otmp = take(T), take(T), take(T)
        L_END, L_STATE = LEVELS, LEVELS + 1

        take = views(used=2 * HC * T)
        sgate, gtmp = take(2, T), take(2, T)
        nsq, utmp, nacc, gnorm = take(4, T), take(4, T), take(T), take(2, T)

        omlb, lb = lbt[:, 6], lbt[:, 5]
        take = views()
        aO = take(GROUPS * HPG, T)
        aV = take(GROUPS, TT * T).rearrange("p g (b n) -> p g b n", b=TT)
        QK = [take(2 * GROUPS, T) for _ in range(2)]
        raw, tcos, tsin = take(2, T), take(2, T), take(2, T)
        scm = take(4 * T)
        PTs = take(4 * T)
        lrow = take(GROUPS, T)
        dgl = take(GROUPS * TT, P)
        mxw, sum_, rec = [dgl.rearrange("p a n -> p (a n)")[:, n * T:(n + 1) * T] for n in range(3)]
        mx, nmx, lsum, lrec, lsev = [take(GROUPS, TT) for _ in range(5)]
        SC = [scm[:, 0:1024].rearrange("p (b n) -> p b n", b=4), scm[:, 1024:1536].rearrange("p (b n) -> p b n", b=4),
              scm[:, 1536:2048].rearrange("p (b n) -> p b n", b=4)]
        SC_BANKS = [ps[:, 4:6].rearrange("p a (b n) -> p (a b) n", b=2), ps[:, 6].rearrange("p (b n) -> p b n", b=4),
                    ps[:, 7].rearrange("p (b n) -> p b n", b=4)]

        take = views()
        NSA_OWN = 21300
        take = views(used=NSA_OWN)
        oaT = take(4, T)
        assert NSA_OWN + 4 * T <= H_AT
        qg, kg = take(2, T), take(2, T)
        vG = take(TT, HEADS_G * P)
        la = take(2, T)
        take = views()
        qraw, qrot = take(4, T), take(4, T)
        kvraw, kraw, kr = take(2, T), take(2, T), take(2, T)
        vsw = take(TT, 2 * P)
        ngate = take(TT, 3 * HEADS_N)
        lrS = take(T)
        zab = take(T)
        hidv, hsig = take(4 * 2 * NB), take(2, 2 * NB)
        hidk = take(2 * NB)
        kc = take(NB)
        vbd = take(2, 4 * HD)
        over = take(4 * T)
        ncos, nsin = [over[:, k * 2 * T:(k + 1) * 2 * T].rearrange("p (a n) -> p a n", a=2) for k in range(2)]
        sC = over[:, 0:2 * T].rearrange("p (t h n) -> p t h n", t=TT, h=HEADS_N)
        PTc = over[:, 2 * T:4 * T].rearrange("p (k n) -> p k n", k=2 * TT)
        cmx, csum, crec, cw = [take(TT, HEADS_N) for _ in range(4)]
        nmax, nneg, nsum, nrec, nw = [take(2, TT) for _ in range(5)]
        w2k, w2v = take(3 * HD), take(HD)
        shared = take(6144)
        w1 = shared[:, 0:4096].rearrange("p (x l m) -> p x l m", x=2, l=16)
        kvp = shared[:, 4096:6144].rearrange("p (x l n) -> p x l n", x=2, l=16)
        prob, probT = [shared[:, k * 2560:(k + 1) * 2560].rearrange("p (a n) -> p a n", a=2) for k in range(2)]
        OFF = [0, P, 3 * P, 6 * P]
        KOFF = [0, 4 * P, 7 * P, 9 * P]
        BOFF = [0, P, 512, 1024]

        take = views()
        gcum = take(2, T)
        gdec = [take(LEVELS + 2, T) for _ in range(2)]
        gkT = take(2, 3 * P)
        gchd = take(2, NCH)
        gsc, gst = take(T), take(NCH, P)
        gsig = take(2, T)
        gsr = take(HEADS_G, T)
        GO_AT = (2 + 2 * (LEVELS + 2)) * T + 6 * P + 2 * NCH + T + NCH * P + 6 * T
        goT = take(HEADS_G, T)
        gosq, gors, gotmp = take(T), take(T), take(T)
        take = views(used=2 * HC * T)
        msig, mtmp = take(4, T), take(2, T)
        assert 2 * HC * T + 6 * T <= GO_AT

        def tokens(g, b):
            return slice(b * P, (b + 1) * P) if g == 0 else slice(b, T, RESIDUES)

        def natural(g, v):
            return v.rearrange("p (b m) -> p b m", b=TT) if g == 0 else v.rearrange("p (r m) -> p m r", r=RESIDUES)

        block = ctx.enter_context(nc.Block())

        constants = ((gains, "gains"), (ones, "ones"), (ident, "ident"), (lvl_mask, "lvl_mask"), (reset, "reset"),
                     (lbl, "lbl"), (hgain, "hgain"), (cos_a, "cos_a"), (sin_a, "sin_a"),
                     (win_mask, "win_mask"), (res_mask, "res_mask"),
                     (gbias, "gbias"), (ggain, "ggain"))
        ALL_CONSTANTS = 16 * (len(constants) - 2)

        @block.sync
        def _(sp):
            for c in range(DC):
                sp.dma_start(h[:, c], a["x"][:, c]).then_inc(s["x_loaded"], 16)
            for dst, name in constants[:2]:
                sp.dma_start(dst[:], a[name]).then_inc(s["norm_consts"], 16)
            for name, units, width in SECTIONS:
                w, n0 = a["w_" + name], FIRST[name]
                k0 = 0
                if n0 == 0:
                    for k in range(RING):
                        sp.dma_start(ring[:, k, 0:width], w[k]).then_inc(w_ready[k], 16)
                    for dst, const in constants[2:]:
                        sp.dma_start(dst[:], a[const]).then_inc(s["consts_loaded"], 16)
                    k0 = RING
                loops = (units - k0) // RING
                if loops > 1:
                    with sp.Fori(0, loops) as i:
                        for k in range(k0, k0 + RING):
                            r = (n0 + k) % RING
                            sp.wait_ge(s["w_used"], i * RING + (n0 + k - RING + 1))
                            sp.dma_start(ring[:, r, 0:width], w[bass.ds(i * RING + k, 1)].rearrange("a p n -> (a p) n")
                                         ).then_inc(w_ready[r], 16)
                    k0 += loops * RING
                for k in range(k0, units):
                    r = (n0 + k) % RING
                    sp.wait_ge(s["w_used"], n0 + k - RING + 1)
                    sp.dma_start(ring[:, r, 0:width], w[k]).then_inc(w_ready[r], 16)

        def cnt(head, per, n):
            return per * head + n if isinstance(head, int) else head[0] * (2 * per) + (per * head[1] + n)

        def later(head, n):
            return head + n if isinstance(head, int) else (head[0], head[1] + n)

        def hgrn_unit(head, k):
            return ("hgrn", 4 * head + k) if isinstance(head, int) else ("hgrn", 4 * head[1] + k, head[0], 8)

        def over_heads(engine, body):
            with engine.Fori(0, (HEADS_H - 2) // 2) as i:
                body((i, 0))
                body((i, 1))
            body(HEADS_H - 2)
            body(HEADS_H - 1)

        H_CREDIT = 2
        def h_done(k, n):
            return 8 * k + n + 1 + H_CREDIT

        NORM_AFTER = [None, 0, 2, 3, 5, 6, 7, 9]
        NORM_INPUT = [0, 1, 2, 3, None, 4, 5, None]

        @block.tensor
        def _(pe):
            def plain(section, k, rhs, bank, i=None, per=0, first=True, last=True, n=8):
                r, v = ring_use(section, k, i, per)
                pe.wait_ge(w_ready[r], v)
                for c in range(n):
                    m = nc.tensor.matmul(ps[:, bank], ring[:, r, c * P:(c + 1) * P], rhs(c),
                                         start=first and c == 0, stop=last and c == n - 1)
                return m

            def unit(section, k, act, bank, i=None, per=0, n=8, ready=None):
                r, v, _ = split_use(section, k, i, per)
                pe.wait_ge(s["w_lo"], v)
                for c in range(n):
                    if ready is not None:
                        ready(c)
                    w = slice(c * P, (c + 1) * P)
                    nc.tensor.matmul(ps[:, bank], ws[:, 0, r, w], act[:, 0, c], start=c == 0, stop=False)
                    nc.tensor.matmul(ps[:, bank], ws[:, 0, r, w], act[:, 1, c], start=False, stop=False)
                    m = nc.tensor.matmul(ps[:, bank], ws[:, 1, r, w], act[:, 0, c], start=False, stop=c == n - 1)
                return m

            def used(m):
                m.then_inc(s["w_used"], 1)

            def mean_square(n):
                pe.wait_ge(s["sq_sum"], 6 * (n + 1))
                nc.tensor.matmul(ps[:, 6], ones[:], nacc, start=True, stop=False)
                pe.wait_ge(s["sq_ready"], 8 * (n + 1))
                nc.tensor.matmul(ps[:, 6], ones[:], nsq[:, 3], start=False, stop=True).then_inc(s["ms_ready"], 1)

            def u_chunk(m):
                def ready(c):
                    pe.wait_ge(s["u_lo_odd"] if c % 2 else s["u_lo_even"], 4 * m + c // 2 + 1)
                return ready

            def project(section, k_upd, act, sem, credit=0):
                def chunk(c):
                    pe.wait_ge(sem, c + 1 + credit)

                with pe.Fori(0, DC // RING) as i:
                    for j in range(RING):
                        pe.wait_ge(s["h_ready"], i * RING + (8 * k_upd + j + 1))
                        used(unit(section, j, act, j % 2, i, RING, ready=None if j else chunk))

            def ffn(f, k_upd, m):
                for half in range(2):
                    gu, down, G = f"gu{f}{'ab'[half]}", f"down{f}{'ab'[half]}", HC * (2 * f + half)

                    def tile(j, i=None, ready=None):
                        at = G + j + 1 if i is None else i * 2 + (G + j + 1)
                        pe.wait_ge(s["g_full"], at)
                        if ready is not None:
                            pe.wait_ge(s["h_ready"], h_done(k_upd - 1, DC - 2))
                        used(unit(gu, 2 * j, us, 2 * (j % 2), i, 4, ready=ready))
                        if ready is not None:
                            mean_square((1, 3, 6)[f])
                            pe.wait_ge(s["h_ready"], h_done(k_upd - 1, DC - 1))
                        used(unit(gu, 2 * j + 1, us, 2 * (j % 2) + 1, i, 4))

                    tile(0, ready=None if half else u_chunk(m))
                    tile(1)
                    with pe.Fori(0, (HC - 3) // 2) as i:
                        tile(2, i)
                        tile(3, i)
                    tile(HC - 1)

                    def hid_chunk(c):
                        pe.wait_ge(s["g_lo"], G + c + 1)

                    with pe.Fori(0, DC // 4) as i:
                        for j in range(4):
                            pe.wait_ge(s["h_ready"], i * 4 + (8 * (k_upd + half) + j + 1))
                            used(unit(down, j, hid, 4 + j % 2, i, 4, n=HC, ready=hid_chunk if j == 0 else None))

            BANK = (1, 0, 2, 3)
            FREED = ("sig_f", "query", "silu_g", "vf_ready")

            def hgrn_project(head, k, ready=None):
                name, first, *loop = hgrn_unit(head, k)
                if head != 0:
                    pe.wait_ge(s[FREED[k]], cnt(later(head, -1), 1, 1))
                used(unit(name, first, us, BANK[k], *loop, ready=ready))

            def chunk_scores(head, it, dv, k_, q_, rows, first_x=True):
                for n, l in enumerate(list(range(LEVELS - 1, -1, -1)) + [None]):
                    if l is not None and first_x:
                        pe.wait_ge(s["x_ready"], cnt(it, 9, n + 1))
                    if n >= 2:
                        pe.wait_ge(s["scores"], cnt(head, 8, n - 1))
                    for c in range(NCH):
                        t = slice(c * C, (c + 1) * C)
                        kk, qq = (k_[rows, t], q_[rows, t]) if l is None else (dv[rows, l, t], dv[rows, l, t])
                        m = nc.tensor.matmul(ps[:, 4 + n % 2, t], kk, qq, start=True, stop=True)
                    m.then_inc(s["score_ps"], 1)

            def chunk_states(keys, values):
                for c in range(NCH - 1):
                    m = nc.tensor.matmul(ps[:, 6, c * C:(c + 1) * C], keys(c), values(c), start=True, stop=True)
                m.then_inc(s["st_ps"], 1)

            def chunk_outputs(head, it, values, sc, stv, dv, rows):
                pe.wait_ge(s["scores"], cnt(head, 8, 8))
                pe.wait_ge(s["states"], cnt(head, 3, 3))
                pe.wait_ge(s["x_ready"], cnt(it, 9, 9))
                for c in range(NCH):
                    t = slice(c * C, (c + 1) * C)
                    m = nc.tensor.matmul(ps[:, 7, t], values(c), sc[:, t], start=True, stop=c == 0)
                    if c:
                        m = nc.tensor.matmul(ps[:, 7, t], stv[rows, c], dv[rows, L_STATE, t], start=False, stop=True)
                m.then_inc(s["o_ps"], 1)

            def output_mean_square(head, sq):
                pe.wait_ge(s["o_sq"], cnt(head, 1, 1))
                nc.tensor.matmul(ps[:, 6], ones[:], sq, start=True, stop=True).then_inc(s["o_ms"], 1)

            ALL = slice(0, P)

            def hgrn_head(head):
                nxt, nxt2 = later(head, 1), later(head, 2)
                pe.wait_ge(s["vf_ready"], cnt(head, 1, 1))
                pe.wait_ge(s["o_rstd"], cnt(head, 2, 2))
                for c in range(NCH):
                    m = nc.tensor.transpose(ps[:, 6, c * C:(c + 1) * C], vf[:, c * C:(c + 1) * C], ident[:])
                m.then_inc(s["vt_ps"], 1)
                x = (head if isinstance(head, int) else head[1]) % 2
                chunk_scores(head, head, dec, key[x], qry[x], ALL)
                pe.wait_ge(s["vt_ready"], cnt(head, 1, 1))
                pe.wait_ge(s["x_ready"], cnt(head, 9, 8))
                for c in range(NCH - 1):
                    m = nc.tensor.transpose(ps[:, 6, c * C:(c + 1) * C], dec[:, L_END, c * C:(c + 1) * C], ident[:])
                m.then_inc(s["kt_ps"], 1)
                if head != HEADS_H - 1:
                    hgrn_project(nxt, 2)
                pe.wait_ge(s["kt_ready"], cnt(head, 1, 1))
                chunk_states(lambda c: kT[:, c], lambda c: vT[:, c])
                if head != HEADS_H - 1:
                    hgrn_project(nxt, 3)
                chunk_outputs(head, head, lambda c: vT[:, c], sc_mat, st, dec, ALL)
                if not isinstance(head, int):
                    hgrn_project(nxt2, 0)
                output_mean_square(head, osq)
                if not isinstance(head, int):
                    hgrn_project(nxt2, 1)

            pe.wait_ge(s["norm_consts"], 32)
            mean_square(0)
            for k in range(4):
                hgrn_project(0, k, ready=None if k else u_chunk(0))
            for k in range(2):
                hgrn_project(1, k)
            pe.wait_ge(s["consts_loaded"], ALL_CONSTANTS)
            over_heads(pe, hgrn_head)
            project("hgrn_out", 0, hid, s["o_lo"], credit=1)
            ffn(0, 1, 1)

            def by_tokens(o, rr, per, width, c0, toks, first, last):
                for cc in range(per):
                    w = slice(cc * width, (cc + 1) * width)
                    uh, ul = us[:, 0, c0 + cc, toks], us[:, 1, c0 + cc, toks]
                    nc.tensor.matmul(o, uh, ws[:, 0, rr, w], start=first and cc == 0, stop=False)
                    nc.tensor.matmul(o, uh, ws[:, 1, rr, w], start=False, stop=False)
                    m = nc.tensor.matmul(o, ul, ws[:, 0, rr, w], start=False, stop=last and cc == per - 1)
                return m

            mean_square(2)
            for g in range(GROUPS):
                base = 4 * (g % 2)
                for n in range(4):
                    rr, v, _ = split_use("attn_v", 4 * g + n)
                    pe.wait_ge(s["w_lo"], v)
                    if g == 0:
                        u_chunk(2)(2 * n)
                        u_chunk(2)(2 * n + 1)
                    for tt in range(TT):
                        if g == 2 and n == 0:
                            pe.wait_ge(s["av_ready"], tt + 1)
                        m = by_tokens(ps[:, base + tt], rr, 2, 512, 2 * n, tokens(g, tt), n == 0, n == 3)
                    used(m)

            def qk_tile(N):
                if N >= 2:
                    pe.wait_ge(s["raw_ready"], N - 1)
                elif N == 0:
                    pe.wait_ge(s["av_ready"], GROUPS * TT)
                used(unit("attn_qk", N, us, N % 2))

            def attn_scores(j):
                pe.wait_ge(s["qk_ready"], 6 * (j + 1))
                if j:
                    pe.wait_ge(s["ao_raw"], 3 * j)
                    pe.wait_ge(s["lse_rows"], 3 * j)
                for g in range(GROUPS):
                    q, k = QK[j % 2][:, 2 * g], QK[j % 2][:, 2 * g + 1]
                    for b in range(TT):
                        if g:
                            m = nc.tensor.matmul(SC_BANKS[g][:, b], q[:, tokens(g, b)], k[:, tokens(g, b)],
                                                 start=True, stop=True)
                        elif b:
                            m = nc.tensor.matmul(SC_BANKS[0][:, b], q[:, tokens(0, b)], k[:, (b - 1) * P:(b + 1) * P],
                                                 start=True, stop=True)
                        else:
                            for half in range(2):
                                m = nc.tensor.matmul(SC_BANKS[0][:, 0, half * P:(half + 1) * P], q[:, 0:P], k[:, 0:P],
                                                     start=True, stop=True)
                    m.then_inc(s["sc_ps"], 1)

            OUT_BANK = (0, 1, 4, 5)

            def attn_out(k):
                n, second = k // 8 * 4 + k % 4, k % 8 // 4
                if k >= 8 and not second:
                    pe.wait_ge(s["h_ready"], h_done(3, n - 4))
                used(plain("attn_out", k, lambda c: aO[:, c % 3 * HPG + 2 * second + c // 3], OUT_BANK[n % 4],
                           first=not second, last=second == 1, n=6))

            def attn_core(j):
                for g in range(GROUPS):
                    pe.wait_ge(s["p_norm"], 2 * j + 1 + (g > 0))
                    for b in range(TT):
                        for half in range(2 if g == 0 else 1):
                            m = nc.tensor.transpose(SC_BANKS[g][:, b, half * P:(half + 1) * P],
                                                    SC[g][:, b, half * P:(half + 1) * P], ident[:])
                    m.then_inc(s["pt_ps"], 1)
                for g in range(GROUPS):
                    hd = slice(j * P, (j + 1) * P)
                    pe.wait_ge(s["pt_ready"], 3 * j + g + 1)
                    for b in range(TT):
                        o = ps[:, 4 + g, b * P:(b + 1) * P]
                        if g:
                            m = nc.tensor.matmul(o, aV[:, g, b, hd], PTs[:, (g + 1) * T + b * P:(g + 1) * T + (b + 1) * P],
                                                 start=True, stop=True)
                        else:
                            m = nc.tensor.matmul(o, aV[:, 0, b, hd], PTs[:, b * 2 * P + P:(b + 1) * 2 * P],
                                                 start=True, stop=b == 0)
                            if b:
                                m = nc.tensor.matmul(o, aV[:, 0, b - 1, hd], PTs[:, b * 2 * P:b * 2 * P + P],
                                                     start=False, stop=True)
                    m.then_inc(s["ao_ps"], 1)
                pe.wait_ge(s["lse_diag"], j + 1)
                for g, bank in enumerate((2, 3, 7)):
                    for b in range(TT):
                        m = nc.tensor.matmul(ps[:, bank, b * P:(b + 1) * P], ones[:], dgl[:, g * TT + b],
                                             start=True, stop=True)
                    m.then_inc(s["lse_ps"], 1)

            for n in range(6):
                qk_tile(n)
            for j in range(HPG):
                N = 6 * (j + 1)
                if j + 1 < HPG:
                    for n in range(3):
                        qk_tile(N + n)
                attn_scores(j)
                if j + 1 < HPG:
                    for n in range(3, 6):
                        qk_tile(N + n)
                else:
                    pe.wait_ge(s["ao_ready"], GROUPS * 2)
                    attn_out(0)
                    attn_out(1)
                attn_core(j)
            pe.wait_ge(s["ao_raw"], GROUPS * HPG)
            attn_out(2)
            attn_out(3)
            pe.wait_ge(s["ao_ready"], GROUPS * HPG)
            for k in range(4, 2 * DC):
                attn_out(k)
            ffn(1, 4, 3)

            mean_square(4)
            mean_square(5)
            ROT = {0: 0, 1: 1, 2: 2, 3: 3, 6: 4, 7: 5}

            def fm_tile(n):
                if n >= 2:
                    pe.wait_ge(s["nt_ready"], n - 1)
                used(unit("nsa_fm" if n < 8 else "gla_fm", n % 8, us, n % 2, ready=None if n else u_chunk(4)))

            def nsa_rotate(n):
                x = ROT[n]
                pe.wait_ge(s["nt_ready"], n + 1)
                if x == 0:
                    pe.wait_ge(s["nsa_consts"], 16 * 6)
                if x >= 2:
                    pe.wait_ge(s["nrope_sin"], x - 1)
                src = qraw[:, n] if n < 4 else kraw[:, n - 6]
                nc.tensor.matmul(ps[:, 2 + x % 2], rot_n[:], src, start=True, stop=True).then_inc(s["nrot_ps"], 1)

            def token_major(section, units, per, width, freed):
                for n in range(units):
                    rr, v, _ = split_use(section, n)
                    pe.wait_ge(s["w_lo"], v)
                    for tt in range(TT):
                        if n == 0 and freed:
                            pe.wait_ge(s[freed], tt + 1)
                        m = by_tokens(ps[:, 4 + tt, 0:width], rr, per, width, per * n, tokens(0, tt),
                                      n == 0, n == units - 1)
                    used(m)

            for n in range(8):
                fm_tile(n)
                if n - 1 in ROT:
                    nsa_rotate(n - 1)
            token_major("nsa_tm", 2, 4, TM_COLS, None)
            nsa_rotate(7)
            token_major("gla_v", 4, 2, 512, "ngate_ready")
            for n in range(8, 12):
                fm_tile(n)
            pe.wait_ge(s["nt_ready"], 11)
            used(unit("gla_lr", 0, us, 0))

            pe.wait_ge(s["cmp_loaded"], 48)
            for x in range(2):
                pe.wait_ge(s["kvpe"], 8 * (x + 1))
                pe.wait_ge(s["nt_ready"], 12 + x)
                bank = 1 - x
                for l in range(16):
                    m = nc.tensor.matmul(ps[:, bank, 0:2 * NB], w1[:, x, l], kvp[:, x, l], start=l == 0, stop=l == 15)
                m.then_inc(s["hid_ps"], 1)
            pe.wait_ge(s["nrope_sin"], 6)
            for p in range(2):
                m = nc.tensor.matmul(ps[:, 2 + p], gw2[0:RANK, p * P:(p + 1) * P], lrS[0:RANK], start=True, stop=True)
            m.then_inc(s["gz_ps"], 1)
            pe.wait_ge(s["gv_ready"], TT)
            pe.wait_ge(s["hid"], 2)
            nc.tensor.matmul(ps[:, 6, 0:NB], w2k[:, HD:3 * HD], hidk[:, 0:NB], start=True, stop=False)
            nc.tensor.matmul(ps[:, 6, 0:NB], w2k[:, 0:2 * HD], hidk[:, NB:2 * NB], start=False, stop=True
                             ).then_inc(s["kc_ps"], 1)
            for g in range(2):
                m = nc.tensor.matmul(ps[:, 7, g * HD:(g + 1) * HD], hidv[:, g * P:(g + 1) * P], w2v, start=True, stop=True)
            m.then_inc(s["vc_ps"], 1)

            pe.wait_ge(s["kc_ready"], 1)
            cs = ps[:, 4:6].rearrange("p g (t h n) -> p g t h n", t=TT, h=4)
            for tt in range(TT):
                for hh in range(HEADS_N):
                    rows = slice(hh // 4 * HD, hh // 4 * HD + HD)
                    m = nc.tensor.matmul(cs[:, hh // 4, tt, hh % 4], qraw[rows, hh % 4, tt * P:(tt + 1) * P], kc[rows],
                                         start=True, stop=True)
            m.then_inc(s["cs_ps"], 1)
            pe.wait_ge(s["vbd"], 8)
            pe.wait_ge(s["cs_w"], 1)
            for b in range(2):
                for k in range(4):
                    tt, g = divmod(b * 4 + k, 2)
                    m = nc.tensor.transpose(ps[:, 6 + b, k * P:(k + 1) * P],
                                            sC[:, tt, 4 * g:4 * g + 4].rearrange("p h n -> p (h n)"), ident[:])
                m.then_inc(s["ct_ps"], 1)
            pe.wait_ge(s["ct_ready"], 2)
            pe.wait_ge(s["z_b"], 2)
            for ft in range(4):
                g, pair = divmod(ft, 2)
                for tt in range(TT):
                    m = nc.tensor.matmul(ps[:, ft, tt * P:(tt + 1) * P], vbd[:, g, pair * P:(pair + 1) * P],
                                         PTc[:, 2 * tt + g], start=True, stop=True)
                m.then_inc(s["co_ps"], 1)

            def nsa_scores(e):
                hh, x = divmod(e, 2)
                rows = slice(hh // 4 * HD, hh // 4 * HD + HD)
                if e == 0:
                    pe.wait_ge(s["oa_ready"], 3)
                elif e == 1:
                    pe.wait_ge(s["oa_ready"], 4)
                else:
                    pe.wait_ge(s["npt_ready"], 3 * (e - 1))
                base = ps[:, 3 * (e % 2):3 * (e % 2) + 3].rearrange("p a n -> p (a n)")
                for tt in range(TT):
                    m = nc.tensor.matmul(base[:, BOFF[tt]:BOFF[tt] + (tt + 1) * P], qrot[rows, hh % 4, tt * P:(tt + 1) * P],
                                         kr[rows, x, 0:(tt + 1) * P], start=True, stop=True)
                m.then_inc(s["ns_ps"], 1)

            def nsa_transposes(e):
                base = ps[:, 3 * (e % 2):3 * (e % 2) + 3].rearrange("p a n -> p (a n)")
                for tt in range(TT):
                    pe.wait_ge(s["ns_scaled"], 4 * e + tt + 1)
                    for k in range(tt + 1):
                        at = KOFF[k] + (tt - k) * P
                        m = nc.tensor.transpose(base[:, at:at + P], prob[:, e % 2, OFF[tt] + k * P:OFF[tt] + (k + 1) * P],
                                                ident[:])
                m.then_inc(s["nt_ps"], 1)

            def nsa_values(e):
                hh, x = divmod(e, 2)
                pe.wait_ge(s["npt_ready"], 3 * (e + 1))
                if x == 0 and hh >= 2:
                    pe.wait_ge(s["oa_acc"], hh - 1)
                vcols = slice(x * P + hh // 4 * HD, x * P + hh // 4 * HD + HD)
                rows = slice(hh % 2 * HD, hh % 2 * HD + HD)
                for k in range(TT):
                    m = nc.tensor.matmul(ps[rows, 6 + hh % 2, k * P:T], vsw[:, k, vcols],
                                         probT[:, e % 2, KOFF[k]:KOFF[k] + (TT - k) * P],
                                         start=x == 0 and k == 0, stop=x == 1 and k == TT - 1)
                m.then_inc(s["no_ps"], 1)

            pe.wait_ge(s["nrope"], 6)
            E = 2 * HEADS_N
            nsa_scores(0)
            for e in range(E):
                if e + 1 < E:
                    nsa_scores(e + 1)
                nsa_transposes(e)
                if e:
                    nsa_values(e - 1)
            nsa_values(E - 1)

            pe.wait_ge(s["npt_ready"], 3 * E)
            for n in range(2):
                used(unit("gla_r", n, us, n))
            for hh in range(HEADS_G):
                p, I = hh // 2, HEADS_H + hh
                rows = slice(hh % 2 * HD, hh % 2 * HD + HD)
                dv = gdec[p]
                vals = lambda c: vG[:, c, hh * P:(hh + 1) * P]
                chunk_scores(I, HEADS_H + p, dv, kg[:, p], qg[:, p], rows, first_x=hh % 2 == 0)
                if hh % 2 == 0:
                    if hh:
                        pe.wait_ge(s["o_rstd"], 2 * I + 2)
                    pe.wait_ge(s["x_ready"], 9 * (HEADS_H + p) + 8)
                    for c in range(NCH - 1):
                        m = nc.tensor.transpose(ps[:, 6, c * C:(c + 1) * C], dv[:, L_END, c * C:(c + 1) * C], ident[:])
                    m.then_inc(s["kt_ps"], 1)
                    pe.wait_ge(s["kt_ready"], HEADS_H + p + 1)
                else:
                    pe.wait_ge(s["o_rstd"], 2 * I + 2)
                chunk_states(lambda c: gkT[:, p, c * P:(c + 1) * P], vals)
                if hh < 2:
                    used(unit("gla_r", 2 + hh, us, 2 + hh))
                if hh:
                    pe.wait_ge(s["o_scaled"], I)
                chunk_outputs(I, HEADS_H + p, vals, gsc, gst, dv, rows)
                output_mean_square(I, gosq)

            for j in range(DC):
                b = 4 * (j % 2)
                pe.wait_ge(s["merged"], j + 1)
                if j == 0:
                    pe.wait_ge(s["gr_silu"], HEADS_G)
                if j == 1:
                    pe.wait_ge(s["gb_ready"], HEADS_G)
                used(unit("merge", 3 * j, us, b))
                used(unit("merge", 3 * j + 1, us, b + 1))
                if j == 0:
                    pe.wait_ge(s["gb_ready"], HEADS_G)
                rr, v = ring_use("merge", 3 * j + 2)
                pe.wait_ge(w_ready[rr], v)
                for c in range(8):
                    src = oaT[:, c] if c < 4 else goT[:, c - 4]
                    m = nc.tensor.matmul(ps[:, b + 2 + c // 4], ring[:, rr, c * P:(c + 1) * P], src,
                                         start=c % 4 == 0, stop=c % 4 == 3)
                used(m)
            project("mix_out", 7, hid, s["m_lo"])
            ffn(2, 8, 5)
            mean_square(7)

        @block.scalar
        def _(act):
            def hi(section, k, i=None, per=0):
                r, v = ring_use(section, k, i, per)
                slot, _, free = split_use(section, k, i, per)
                w = WIDTH[section]
                if free is not None:
                    act.wait_ge(s["w_used"], free)
                act.wait_ge(w_ready[r], v)
                nc.scalar.copy(ws[:, 0, slot, 0:w], ring[:, r, 0:w]).then_inc(s["w_hi"], 1)

            def norm(n, nxt=None):
                m = NORM_INPUT[n]
                for c in range(DC):
                    if n == 0:
                        act.wait_ge(s["x_loaded"], 16 * 8)
                    else:
                        act.wait_ge(s["h_ready"], h_done(NORM_AFTER[n], c))
                    if c >= 4:
                        act.wait_ge(s["sq_sum"], 6 * n + max(c - 4, 1))
                    nc.scalar.activation(nsq[:, c % 4], h[:, c], ACT.Square).then_inc(s["sq_ready"], 1)
                if nxt:
                    hi(nxt, 0)
                rms(n)
                if m is None:
                    return
                for c in range(DC):
                    if c == 4:
                        hi(nxt, 1)
                    act.wait_ge(s["u_tmp"], 8 * m + c + 1)
                    nc.scalar.copy(us[:, 0, c], utmp[:, c % 4]).then_inc(s["u_hi"], 1)

            def early_norm(n, section, nxt):
                m = NORM_INPUT[n]
                for c in range(DC):
                    if section and c + 2 < DC:
                        hi(section, c + 2)
                    if c == DC - 2:
                        hi(nxt, 0)
                    act.wait_ge(s["h_ready"], h_done(NORM_AFTER[n], c))
                    if c >= 4:
                        act.wait_ge(s["sq_sum"], 6 * n + max(c - 4, 1))
                    nc.scalar.activation(nsq[:, c % 4], h[:, c], ACT.Square).then_inc(s["sq_ready"], 1)
                    act.wait_ge(s["u_tmp"], 8 * m + c + 1)
                    nc.scalar.copy(us[:, 0, c], utmp[:, c % 4]).then_inc(s["u_hi"], 1)
                hi(nxt, 1)
                rms(n)

            def rms(n):
                act.wait_ge(s["ms_ready"], n + 1)
                nc.scalar.activation(rs[:], ps[:, 6], ACT.Ln, scale=1.0 / D, bias=eps[:, 0:1]).then_inc(s["rstd"], 1)
                act.wait_ge(s["rstd"], 2 * n + 1)
                nc.scalar.activation(rs[:], rs[:], ACT.Exp, scale=-0.5).then_inc(s["rstd"], 1)

            def ffn(f, nxt):
                for half in range(2):
                    gu, down, G = f"gu{f}{'ab'[half]}", f"down{f}{'ab'[half]}", HC * (2 * f + half)

                    def tile(j, i=None):
                        x = j % 2
                        at = lambda v, per: v if i is None else i * per + v
                        last = j == HC - 1
                        hi(down, 0) if last else hi(gu, 2 * j + 2, i, 4)
                        act.wait_ge(s["gate_norm"], at(G + j + 1, 2))
                        nc.scalar.activation(sgate[:, x], gnorm[:, x], ACT.Sigmoid).then_inc(s["gate_sig"], 1)
                        hi(down, 1) if last else hi(gu, 2 * j + 3, i, 4)
                        act.wait_ge(s["g_full"], at(G + j + 3, 2))
                        dst = hid[:, 0, j] if i is None else hid[:, 0, bass.ds(i * 2 + j, 1)].rearrange("p a t -> p (a t)")
                        nc.scalar.copy(dst, gtmp[:, x]).then_inc(s["g_hi"], 1)

                    with act.Fori(0, (HC - 1) // 2) as i:
                        tile(0, i)
                        tile(1, i)
                    tile(HC - 1)
                    for j in range(2, DC):
                        hi(down, j)
                    if half == 0:
                        hi(f"gu{f}b", 0)
                        hi(f"gu{f}b", 1)

            def decay_exps(it, dv, part):
                lo, hi, ready = ((5, 7, 2), (3, 5, 4), (0, 3, 7), (7, 8, 8))[part]
                act.wait_ge(s["dec_in"], cnt(it, 8, ready))
                nc.scalar.activation(dv[:, lo:hi], dv[:, lo:hi], ACT.Exp).then_inc(s["dec_out"], 1)

            def state_exps(it, cum, dv, ends):
                act.wait_ge(s["cum"], cnt(it, 1, 1))
                nc.scalar.activation(dv[:, L_STATE], cum, ACT.Exp).then_inc(s["dec_out"], 1)
                act.wait_ge(s["dec_out"], cnt(it, 5, 5))
                nc.scalar.copy(ends, dv[:, L_STATE, C - 1::C]).then_inc(s["chunk_decay"], 1)

            def output_square(head, sq):
                act.wait_ge(s["o_ps"], cnt(head, 1, 1))
                nc.scalar.activation(sq, ps[:, 7], ACT.Square).then_inc(s["o_sq"], 1)

            def output_rstd(head, r):
                act.wait_ge(s["o_ms"], cnt(head, 1, 1))
                nc.scalar.activation(r, ps[:, 6], ACT.Ln, scale=1.0 / P, bias=eps[:, 0:1]).then_inc(s["o_rstd"], 1)
                act.wait_ge(s["o_rstd"], cnt(head, 2, 3))
                nc.scalar.activation(r, r, ACT.Exp, scale=-0.5).then_inc(s["o_rstd"], 1)

            act.wait_ge(s["credit"], 2)
            norm(0, "hgrn")

            def hgrn_sigmoid(head, k, dst, done):
                src = (1, 0, 2)[k]
                act.wait_ge(s["w_used"], cnt(head, 4, FIRST["hgrn"] + k + 1))
                if head != 0 and k:
                    act.wait_ge(s[("", "query", "silu_g")[k]], cnt(later(head, -1), 1, 1))
                nc.scalar.activation(dst, ps[:, src], ACT.Sigmoid).then_inc(s[done], 1)

            def hgrn_log(head):
                act.wait_ge(s["forget"], cnt(head, 1, 1))
                nc.scalar.activation(lf, fg, ACT.Ln).then_inc(s["log_f"], 1)

            def hgrn_value(head):
                act.wait_ge(s["w_used"], cnt(head, 4, FIRST["hgrn"] + 4))
                nc.scalar.copy(vf, ps[:, 3]).then_inc(s["vf_ready"], 1)

            hgrn_sigmoid(0, 0, sf_, "sig_f")
            hi("hgrn", 2)
            hgrn_sigmoid(0, 1, sq_, "sig_q")
            act.wait_ge(s["lb_steps"], 5)
            nc.scalar.activation(lbt[:, 0:3], lbt[:, 0:3], ACT.Exp).then_inc(s["lb_steps"], 1)
            hgrn_log(0)
            hi("hgrn", 3)
            decay_exps(0, dec, 0)
            decay_exps(0, dec, 1)
            hi("hgrn", 4)
            decay_exps(0, dec, 2)
            decay_exps(0, dec, 3)
            state_exps(0, bcum, dec, chd)
            hi("hgrn", 5)
            hgrn_value(0)
            hgrn_sigmoid(0, 2, sg_, "sig_g")
            hi("hgrn", 6)
            hi("hgrn", 7)

            def hgrn_head(head):
                nxt, nxt2 = later(head, 1), later(head, 2)
                more = head != HEADS_H - 1
                if more:
                    hgrn_sigmoid(nxt, 0, sf_, "sig_f")
                    hgrn_sigmoid(nxt, 1, sq_, "sig_q")
                act.wait_ge(s["vt_ps"], cnt(head, 1, 1))
                nc.scalar.copy(vT, ps[:, 6].rearrange("p (c t) -> p c t", c=NCH)).then_inc(s["vt_ready"], 1)
                if more:
                    hgrn_log(nxt)
                    decay_exps(nxt, dec, 0)
                    decay_exps(nxt, dec, 1)
                act.wait_ge(s["kt_ps"], cnt(head, 1, 1))
                nc.scalar.copy(kT[:, 0:3], ps[:, 6, 0:3 * C].rearrange("p (c t) -> p c t", c=3)).then_inc(s["kt_ready"], 1)
                if more:
                    decay_exps(nxt, dec, 2)
                    hi(*hgrn_unit(nxt2, 0)) if not isinstance(head, int) else hi("hgrn_out", 0)
                    decay_exps(nxt, dec, 3)
                    hgrn_value(nxt)
                    hi(*hgrn_unit(nxt2, 1)) if not isinstance(head, int) else hi("hgrn_out", 1)
                output_square(head, osq)
                if more:
                    state_exps(nxt, bcum, dec, chd)
                if not isinstance(head, int):
                    hi(*hgrn_unit(nxt2, 2))
                output_rstd(head, ors)
                act.wait_ge(s["o_full"], cnt(head, 1, 1))
                dst = (hid[:, 0, head] if isinstance(head, int) else
                       hid[:, 0, bass.ds(head[0] * 2 + head[1], 1)].rearrange("p a t -> p (a t)"))
                nc.scalar.copy(dst, otmp).then_inc(s["o_hi"], 1)
                if more:
                    hgrn_sigmoid(nxt, 2, sg_, "sig_g")
                if not isinstance(head, int):
                    hi(*hgrn_unit(nxt2, 3))

            over_heads(act, hgrn_head)
            early_norm(1, "hgrn_out", "gu0a")
            ffn(0, "attn_v")

            norm(2, "attn_v")
            act.dma_start(a["h_spill"], h).then_inc(s["spilled"], 16)
            for g in range(GROUPS):
                for k in range(4 * g + 2, 4 * g + 6):
                    hi("attn_v", k) if k < 12 else hi("attn_qk", k - 12)
                for tt in range(TT):
                    act.wait_ge(s["w_used"], FIRST["attn_v"] + 4 * (g + 1))
                    nc.scalar.copy(aV[:, g, tt], ps[:, 4 * (g % 2) + tt]).then_inc(s["av_ready"], 1)

            def mix_exp(j):
                act.wait_ge(s["mix_diff"], j + 1)
                nc.scalar.activation(lrow, lrow, ACT.Exp).then_inc(s["mix_exp"], 1)

            def take_raw(N):
                if N + 2 < 24:
                    hi("attn_qk", N + 2)
                act.wait_ge(s["w_used"], FIRST["attn_qk"] + N + 1)
                if N >= 2:
                    act.wait_ge(s["rope_cos"], N - 1)
                    act.wait_ge(s["rope_sin"], 2 * N - 2)
                nc.scalar.copy(raw[:, N % 2], ps[:, N % 2]).then_inc(s["raw_ready"], 1)

            for n in range(6):
                take_raw(n)
            for j in range(HPG):
                N = 6 * (j + 1)
                if j + 1 < HPG:
                    for n in range(3):
                        take_raw(N + n)
                for g in range(GROUPS):
                    act.wait_ge(s["sc_negmax"], 3 * j + g + 1)
                    for b in range(TT):
                        nc.scalar.activation(SC[g][:, b], SC[g][:, b], ACT.Exp, bias=nmx[:, g, b:b + 1],
                                             accum_out=lsum[:, g, b:b + 1]).then_inc(s["p_exp"], 1)
                if j + 1 < HPG:
                    take_raw(N + 3)
                act.wait_ge(s["p_exp"], 12 * (j + 1))
                nc.scalar.activation(lsev, lsum, ACT.Ln).then_inc(s["p_logsum"], 1)
                if j:
                    mix_exp(j - 1)
                if j + 1 < HPG:
                    take_raw(N + 4)
                for g in range(GROUPS):
                    act.wait_ge(s["pt_ps"], 3 * j + g + 1)
                    if g == 0:
                        nc.scalar.copy(PTs[:, 0:1024], ps[:, 4:6].rearrange("p a n -> p (a n)")).then_inc(s["pt_ready"], 1)
                    else:
                        nc.scalar.copy(PTs[:, (g + 1) * T:(g + 2) * T], ps[:, 5 + g]).then_inc(s["pt_ready"], 1)
                if j + 1 < HPG:
                    take_raw(N + 5)
                for g in range(GROUPS):
                    act.wait_ge(s["ao_ps"], 3 * j + g + 1)
                    dst = aO[:, g * HPG + j].rearrange("p (b m) -> p b m", b=TT if g == 0 else P)
                    nc.scalar.copy(dst, natural(g, ps[:, 4 + g])).then_inc(s["ao_raw"], 1)
                act.wait_ge(s["spilled"], 16)
                for g, bank in enumerate((2, 3, 7)):
                    act.wait_ge(s["lse_ps"], 3 * j + g + 1)
                    dst = lrow[:, g].rearrange("p (b m) -> p b m", b=TT if g == 0 else P)
                    nc.scalar.copy(dst, natural(g, ps[:, bank])).then_inc(s["lse_rows"], 1)
            mix_exp(HPG - 1)
            act.wait_ge(s["ao_ready"], GROUPS * HPG)
            act.dma_start(h, a["h_spill"]).then_inc(s["reloaded"], 16)
            for dst, name in ((rot_n, "rot_n"), (cos_n, "cos_n"), (sin_n, "sin_n"), (cmp_mask, "cmp_mask"),
                              (pos_kv, "pos_kv"), (gw2[0:RANK], "gw2")):
                act.dma_start(dst, a[name]).then_inc(s["nsa_consts"], 16)
            early_norm(3, None, "gu1a")
            ffn(1, None)

            norm(4)
            norm(5, "nsa_fm")
            act.dma_start(a["h_spill"], h).then_inc(s["spilled"], 16)
            fm_dst = [qraw[:, n] for n in range(4)] + [kvraw[:, 0], kvraw[:, 1], kraw[:, 0], kraw[:, 1],
                                                       qg[:, 0], qg[:, 1], kg[:, 0], kg[:, 1]]

            def take_fm(n):
                scale = float(HD) ** -0.5 if n < 4 or n in (8, 9) else 1.0
                if n < 8:
                    hi("nsa_fm", n + 2) if n < 6 else hi("nsa_tm", n - 6)
                elif n < 11:
                    hi("gla_fm", n - 6) if n < 10 else hi("gla_lr", 0)
                else:
                    hi("gla_r", 0)
                act.wait_ge(s["w_used"], (FIRST["nsa_fm"] + n if n < 8 else FIRST["gla_fm"] + n - 8) + 1)
                nc.scalar.activation(fm_dst[n], ps[:, n % 2], ACT.Copy, scale=scale).then_inc(s["nt_ready"], 1)

            take_fm(0)
            act.wait_ge(s["u_lo_even"], 20)
            act.wait_ge(s["u_lo_odd"], 20)
            for dst, name in ((w1, "cmp_w1"), (w2k, "cmp_w2k"), (w2v, "cmp_w2v")):
                act.dma_start(dst, a[name]).then_inc(s["cmp_loaded"], 16)
            for n in range(1, 8):
                take_fm(n)
            hi("gla_v", 0)
            hi("gla_v", 1)
            for tt in range(TT):
                act.wait_ge(s["w_used"], FIRST["nsa_tm"] + 2)
                nc.scalar.copy(vsw[:, tt], ps[:, 4 + tt, 0:2 * P]).then_inc(s["ntm_ready"], 1)
                nc.scalar.activation(ngate[:, tt], ps[:, 4 + tt, 2 * P:TM_COLS], ACT.Sigmoid).then_inc(s["ngate_ready"], 1)
            for k in range(4):
                hi("gla_v", 2 + k) if k < 2 else hi("gla_fm", k - 2)
            act.wait_ge(s["spilled"], 32)
            for tt in range(TT):
                act.wait_ge(s["w_used"], FIRST["gla_v"] + 4)
                nc.scalar.copy(vG[:, tt], ps[:, 4 + tt]).then_inc(s["gv_ready"], 1)
            for n in range(8, 12):
                take_fm(n)
            act.wait_ge(s["w_used"], FIRST["gla_lr"] + 1)
            nc.scalar.copy(lrS[0:RANK], ps[0:RANK, 0]).then_inc(s["nt_ready"], 1)
            hi("gla_r", 1)
            for x in range(2):
                act.wait_ge(s["hid_ps"], x + 1)
                nc.scalar.activation(hsig[:, x], ps[:, 1 - x, 0:2 * NB], ACT.Sigmoid).then_inc(s["hid_sig"], 1)
            act.wait_ge(s["kc_ps"], 1)
            nc.scalar.copy(kc, ps[:, 6, 0:NB]).then_inc(s["kc_ready"], 1)
            act.wait_ge(s["vc_ps"], 1)
            act.wait_ge(s["kvpe_zero"], 2)
            for g in range(2):
                for k in range(4):
                    rows = slice(32 * k, 32 * k + 32)
                    nc.scalar.copy(vbd[rows, g, k * HD:(k + 1) * HD], ps[rows, 7, g * HD:(g + 1) * HD]).then_inc(s["vbd"], 1)
            for p in range(2):
                act.wait_ge(s["z_b"], p + 1)
                if p:
                    act.wait_ge(s["z_min"], 1)
                nc.scalar.activation(zab, la[:, p], ACT.Abs).then_inc(s["z_abs"], 1)
                act.wait_ge(s["z_abs"], p + 1)
                nc.scalar.activation(zab, zab, ACT.Exp, scale=-1.0).then_inc(s["z_exp"], 1)
                act.wait_ge(s["z_exp"], p + 1)
                nc.scalar.activation(zab, zab, ACT.Ln, bias=ones[:, 0:1]).then_inc(s["z_ln"], 1)
            act.wait_ge(s["cs_sub"], 1)
            nc.scalar.activation(sC, sC, ACT.Exp).then_inc(s["cs_exp"], 1)
            for b in range(2):
                act.wait_ge(s["ct_ps"], b + 1)
                nc.scalar.copy(PTc[:, 4 * b:4 * b + 4], ps[:, 6 + b].rearrange("p (k n) -> p k n", k=4)).then_inc(s["ct_ready"], 1)
            for tt in range(TT):
                act.wait_ge(s["co_ps"], tt + 1)
                nc.scalar.copy(oaT[:, tt], ps[:, tt]).then_inc(s["oa_ready"], 1)
            act.wait_ge(s["hid"], 2)
            def nsa_exps(i, x):
                base = ps[:, 3 * x:3 * x + 3].rearrange("p a n -> p (a n)")
                for tt in range(TT):
                    act.wait_ge(s["ns_neg"], i * 8 + (4 * x + max(tt, 1) + 1))
                    nc.scalar.activation(prob[:, x, OFF[tt]:OFF[tt] + (tt + 1) * P], base[:, BOFF[tt]:BOFF[tt] + (tt + 1) * P],
                                         ACT.Exp, bias=nneg[:, x, tt:tt + 1], accum_out=nsum[:, x, tt:tt + 1]
                                         ).then_inc(s["ns_exp"], 1)

            def nsa_copies(i, x):
                base = ps[:, 3 * x:3 * x + 3].rearrange("p a n -> p (a n)")
                act.wait_ge(s["nt_ps"], i * 2 + (x + 1))
                for k in range(3):
                    lo, hi = 512 * k, min(512 * (k + 1), 1280)
                    nc.scalar.copy(probT[:, x, lo:hi], base[:, lo:hi]).then_inc(s["npt_ready"], 1)

            nsa_exps(0, 0)
            with act.Fori(0, HEADS_N - 1) as i:
                nsa_copies(i, 0)
                nsa_exps(i, 1)
                nsa_copies(i, 1)
                nsa_exps(i + 1, 0)
            nsa_copies(HEADS_N - 1, 0)
            nsa_exps(HEADS_N - 1, 1)
            nsa_copies(HEADS_N - 1, 1)
            def output_gate(n):
                hi("gla_r", n + 2) if n < 2 else hi("merge", n - 2)
                act.wait_ge(s["w_used"], FIRST["gla_r"] + n + 1)
                if n >= 2:
                    act.wait_ge(s["gr_silu"], n - 1)
                nc.scalar.activation(gsig[:, n % 2], ps[:, n], ACT.Sigmoid).then_inc(s["gr_sig"], 1)

            output_gate(0)
            output_gate(1)
            for p in range(2):
                for part in range(4):
                    decay_exps(HEADS_H + p, gdec[p], part)
                state_exps(HEADS_H + p, gcum[:, p], gdec[p], gchd[:, p])
            for hh in range(HEADS_G):
                if hh % 2 == 0:
                    act.wait_ge(s["kt_ps"], HEADS_H + hh // 2 + 1)
                    nc.scalar.copy(gkT[:, hh // 2], ps[:, 6, 0:3 * C]).then_inc(s["kt_ready"], 1)
                if hh < 2:
                    output_gate(2 + hh)
                output_square(HEADS_H + hh, gosq)
                output_rstd(HEADS_H + hh, gors)
            act.wait_ge(s["gb_ready"], HEADS_G)
            act.dma_start(h, a["h_spill"]).then_inc(s["reloaded"], 16)
            for j in range(DC):
                for k in range(2):
                    hi("merge", 3 * (j + 1) + k) if j + 1 < DC else hi("mix_out", k)
                    act.wait_ge(s["w_used"], FIRST["merge"] + 3 * j + k + 1)
                    if j >= 2:
                        act.wait_ge(s["m_full"], j - 1)
                    nc.scalar.activation(msig[:, 2 * (j % 2) + k], ps[:, 4 * (j % 2) + k], ACT.Sigmoid
                                         ).then_inc(s["mg_sig"], 1)
                act.wait_ge(s["m_full"], j + 1)
                nc.scalar.copy(hid[:, 0, j], mtmp[:, j % 2]).then_inc(s["m_hi"], 1)
            early_norm(6, "mix_out", "gu2a")
            ffn(2, None)
            norm(7)
            for c in range(DC):
                act.wait_ge(s["credit"], 3 + c)
                act.dma_start(out[:, c], h[:, c]).then_inc(s["stored"], 16)
            act.wait_ge(s["stored"], 16 * DC)

        @block.gpsimd
        def _(pool):
            def lo(section, k, i=None, per=0):
                slot, done, _ = split_use(section, k, i, per)
                r, _ = ring_use(section, k)
                w = WIDTH[section]
                pool.wait_ge(s["w_hi"], done)
                nc.gpsimd.tensor_tensor(ws[:, 1, slot, 0:w], ring[:, r, 0:w], ws[:, 0, slot, 0:w].bitcast(F32),
                                        ALU.subtract).then_inc(s["w_lo"], 1)

            def norm(n, nxt):
                m = NORM_INPUT[n]
                for c in range(0, DC, 2):
                    if c == 4:
                        lo(nxt, 1)
                    pool.wait_ge(s["u_hi"], 8 * m + c + 1)
                    nc.gpsimd.tensor_tensor(us[:, 1, c], utmp[:, c % 4], us[:, 0, c].bitcast(F32), ALU.subtract
                                            ).then_inc(s["u_lo_even"], 1)

            def early_norm(n, section, nxt):
                m = NORM_INPUT[n]
                for c in range(DC):
                    if section and c + 2 < DC:
                        lo(section, c + 2)
                    if c == DC - 2:
                        lo(nxt, 0)
                    if c % 2 == 0:
                        pool.wait_ge(s["u_hi"], 8 * m + c + 1)
                        nc.gpsimd.tensor_tensor(us[:, 1, c], utmp[:, c % 4], us[:, 0, c].bitcast(F32), ALU.subtract
                                                ).then_inc(s["u_lo_even"], 1)
                lo(nxt, 1)

            def ffn(f):
                for half in range(2):
                    gu, down, G = f"gu{f}{'ab'[half]}", f"down{f}{'ab'[half]}", HC * (2 * f + half)

                    def tile(j, i=None):
                        for k in range(2):
                            lo(down, k) if j == HC - 1 else lo(gu, 2 * j + 2 + k, i, 4)
                        pool.wait_ge(s["g_hi"], G + j + 1 if i is None else i * 2 + (G + j + 1))
                        dst, src = ((hid[:, 1, j], hid[:, 0, j]) if i is None else
                                    [hid[:, x, bass.ds(i * 2 + j, 1)].rearrange("p a t -> p (a t)") for x in (1, 0)])
                        nc.gpsimd.tensor_tensor(dst, gtmp[:, j % 2], src.bitcast(F32), ALU.subtract).then_inc(s["g_lo"], 1)

                    with pool.Fori(0, (HC - 1) // 2) as i:
                        tile(0, i)
                        tile(1, i)
                    tile(HC - 1)
                    for j in range(2, DC):
                        lo(down, j)
                    if half == 0:
                        lo(f"gu{f}b", 0)
                        lo(f"gu{f}b", 1)

            def decayed(it, dv, k_, q_, operands=(), between={}):
                for sem, v in operands:
                    pool.wait_ge(sem, v)
                for n, l in enumerate((6, 5, 4, 3, 2, 1, 0, L_END, L_STATE)):
                    if n in between:
                        between[n]()
                    if n in (0, 2, 4, 7, 8):
                        pool.wait_ge(s["dec_out"], cnt(it, 5, {0: 1, 2: 2, 4: 3, 7: 4, 8: 5}[n]))
                    if n >= 7:
                        if n == 8:
                            pool.wait_ge(s["chunk_decay"], cnt(it, 1, 1))
                        nc.gpsimd.tensor_tensor(dv[:, l], dv[:, l], (k_, q_)[n - 7], ALU.mult).then_inc(s["x_ready"], 1)
                        continue
                    m = 1 << l
                    x = dv[:, l].rearrange("p (b h m) -> p b h m", h=2, m=m)
                    kk = k_.rearrange("p (b h m) -> p b h m", h=2, m=m)
                    qq = q_.rearrange("p (b h m) -> p b h m", h=2, m=m)
                    nc.gpsimd.tensor_tensor(x[:, :, 0], x[:, :, 0], kk[:, :, 0], ALU.mult)
                    nc.gpsimd.tensor_tensor(x[:, :, 1], x[:, :, 1], qq[:, :, 1], ALU.mult).then_inc(s["x_ready"], 1)

            def hgrn_decayed(head, between):
                x = (head if isinstance(head, int) else head[1]) % 2
                decayed(head, dec, key[x], qry[x], ((s["query"], cnt(head, 1, 1)), (s["key"], cnt(head, 1, 1))), between)

            lo("hgrn", 0)
            norm(0, "hgrn")
            lo("hgrn", 2)
            lo("hgrn", 3)
            hgrn_decayed(0, {4: lambda: lo("hgrn", 4), 8: lambda: lo("hgrn", 5)})
            lo("hgrn", 6)
            lo("hgrn", 7)

            def hgrn_head(head):
                nxt, nxt2 = later(head, 1), later(head, 2)
                if not isinstance(head, int):
                    hgrn_decayed(nxt, {4: lambda: lo(*hgrn_unit(nxt2, 0)), 8: lambda: lo(*hgrn_unit(nxt2, 1))})
                    lo(*hgrn_unit(nxt2, 2))
                elif head == HEADS_H - 2:
                    hgrn_decayed(nxt, {7: lambda: lo("hgrn_out", 0), 8: lambda: lo("hgrn_out", 1)})
                pool.wait_ge(s["o_hi"], cnt(head, 1, 1))
                dst, src = ((hid[:, 1, head], hid[:, 0, head]) if isinstance(head, int) else
                            [hid[:, x, bass.ds(head[0] * 2 + head[1], 1)].rearrange("p a t -> p (a t)") for x in (1, 0)])
                nc.gpsimd.tensor_tensor(dst, otmp, src.bitcast(F32), ALU.subtract).then_inc(s["o_lo"], 1)
                if not isinstance(head, int):
                    lo(*hgrn_unit(nxt2, 3))

            over_heads(pool, hgrn_head)
            early_norm(1, "hgrn_out", "gu0a")
            ffn(0)
            lo("attn_v", 0)
            norm(2, "attn_v")
            for k in range(2, 12):
                lo("attn_v", k)
            lo("attn_qk", 0)
            lo("attn_qk", 1)

            def times_cos(N):
                if N + 2 < 24:
                    lo("attn_qk", N + 2)
                pool.wait_ge(s["raw_ready"], N + 1)
                if N >= 2:
                    pool.wait_ge(s["qk_ready"], N - 1)
                nc.gpsimd.tensor_tensor(tcos[:, N % 2], raw[:, N % 2], cos_a[:], ALU.mult).then_inc(s["rope_cos"], 1)

            for n in range(6):
                times_cos(n)
            for j in range(HPG):
                N = 6 * (j + 1)
                if j + 1 < HPG:
                    for n in range(5):
                        times_cos(N + n)
                pool.wait_ge(s["lse"], j + 1)
                if j:
                    pool.wait_ge(s["ao_ready"], 3 * j)
                else:
                    pool.wait_ge(s["spilled"], 16)
                nc.gpsimd.tensor_tensor(dgl, ident[:, None, :].broadcast_to((P, GROUPS * TT, P)),
                                        lsev.rearrange("p g b -> p (g b)")[:, :, None].broadcast_to((P, GROUPS * TT, P)),
                                        ALU.mult).then_inc(s["lse_diag"], 1)
                if j + 1 < HPG:
                    times_cos(N + 5)

            early_norm(3, None, "gu1a")
            ffn(1)

            lo("nsa_fm", 0)
            norm(5, "nsa_fm")
            pool.wait_ge(s["u_lo_odd"], 20)
            pool.wait_ge(s["u_lo_even"], 20)
            nc.gpsimd.memset(kvp, 0.0).then_inc(s["kvpe_zero"], 1)
            nc.gpsimd.memset(vbd, 0.0).then_inc(s["kvpe_zero"], 1)
            for n in range(8):
                lo("nsa_fm", n + 2) if n < 6 else lo("nsa_tm", n - 6)
                if n in (4, 5):
                    continue
                x = n if n < 4 else n - 2
                pool.wait_ge(s["nt_ready"], n + 1)
                if n == 0:
                    pool.wait_ge(s["nsa_consts"], 16 * 6)
                if x >= 2:
                    pool.wait_ge(s["nrope"], x - 1)
                src = qraw[:, n] if n < 4 else kraw[:, n - 6]
                nc.gpsimd.tensor_tensor(ncos[:, x % 2], src, cos_n[:], ALU.mult).then_inc(s["nrope_cos"], 1)
            for section, units in (("gla_v", 4), ("gla_fm", 4), ("gla_lr", 1), ("gla_r", 4)):
                for k in range(units):
                    lo(section, k)
            for p in range(2):
                decayed(HEADS_H + p, gdec[p], kg[:, p], qg[:, p])
            lo("merge", 0)
            lo("merge", 1)
            for j in range(DC):
                for k in range(2):
                    lo("merge", 3 * (j + 1) + k) if j + 1 < DC else lo("mix_out", k)
                pool.wait_ge(s["m_hi"], j + 1)
                nc.gpsimd.tensor_tensor(hid[:, 1, j], mtmp[:, j % 2], hid[:, 0, j].bitcast(F32), ALU.subtract
                                        ).then_inc(s["m_lo"], 1)
            early_norm(6, "mix_out", "gu2a")
            ffn(2)

        @block.vector
        def _(dve):
            def norm(n, done=None):
                m = NORM_INPUT[n]
                dve.wait_ge(s["rstd"], 2 * n + 2)

                def odd_lo(c):
                    dve.wait_ge(s["u_hi"], 8 * m + c + 1)
                    nc.vector.tensor_tensor(us[:, 1, c], utmp[:, c % 4], us[:, 0, c].bitcast(F32), ALU.subtract
                                            ).then_inc(s["u_lo_odd"], 1)

                for c in range(DC):
                    if m is not None and c >= 4:
                        dve.wait_ge(s["u_lo_odd"] if c % 2 else s["u_lo_even"], 4 * m + (c - 4) // 2 + 1)
                    nc.vector.scalar_tensor_tensor(out=h[:, c] if m is None else utmp[:, c % 4], in0=h[:, c],
                                                   scalar=gains[:, n, c:c + 1], in1=rs[:], op0=ALU.mult, op1=ALU.mult
                                                   ).then_inc(done if m is None else s["u_tmp"], 1)
                    if m is not None and c % 2 == 0 and c:
                        odd_lo(c - 1)
                    if m is None and n == 4 and c >= 2:
                        add_square(5, c - 1)
                if m is not None:
                    odd_lo(DC - 1)

            def add_square(n, c):
                dve.wait_ge(s["sq_ready"], 8 * n + c + 1)
                if c > 1:
                    dve.wait_ge(s["sq_sum"], 6 * n + c - 1)
                nc.vector.tensor_tensor(nacc, nsq[:, 0] if c == 1 else nacc, nsq[:, c % 4], ALU.add
                                        ).then_inc(s["sq_sum"], 1)

            def early_input(n, c):
                m = NORM_INPUT[n]
                if c >= 4:
                    dve.wait_ge(s["u_lo_odd"] if c % 2 else s["u_lo_even"], 4 * m + (c - 4) // 2 + 1)
                dve.wait_ge(s["h_ready"], h_done(NORM_AFTER[n], c))
                nc.vector.tensor_scalar(utmp[:, c % 4], h[:, c], gains[:, n, c:c + 1], None, ALU.mult
                                        ).then_inc(s["u_tmp"], 1)
                if c >= 2:
                    add_square(n, c - 1)
                if c % 2:
                    dve.wait_ge(s["u_hi"], 8 * m + c + 1)
                    nc.vector.tensor_tensor(us[:, 1, c], utmp[:, c % 4], us[:, 0, c].bitcast(F32), ALU.subtract
                                            ).then_inc(s["u_lo_odd"], 1)

            def residual_and_input(section, norm):
                for c in range(DC):
                    dve.wait_ge(s["w_used"], FIRST[section] + c + 1)
                    nc.vector.tensor_tensor(h[:, c], h[:, c], ps[:, c % 2], ALU.add).then_inc(s["h_ready"], 1)
                    early_input(norm, c)

            def residual(section, base, norm=None):
                loops = DC if norm is None else DC // 2
                with dve.Fori(0, loops // 2) as i:
                    for j in range(2):
                        dve.wait_ge(s["w_used"], i * 2 + (FIRST[section] + j + 1))
                        hj = h[:, bass.ds(i * 2 + j, 1)].rearrange("p a t -> p (a t)")
                        nc.vector.tensor_tensor(hj, hj, ps[:, base + j], ALU.add).then_inc(s["h_ready"], 1)
                for j in range(loops, DC):
                    dve.wait_ge(s["w_used"], FIRST[section] + j + 1)
                    nc.vector.tensor_tensor(h[:, j], h[:, j], ps[:, base + j % 2], ALU.add).then_inc(s["h_ready"], 1)
                    for c in {5: (1, 2, 3), 6: (4, 5), 7: (6,)}.get(j, ()):
                        add_square(norm, c)

            def ffn(f, norm):
                for half in range(2):
                    gu, down, G = f"gu{f}{'ab'[half]}", f"down{f}{'ab'[half]}", HC * (2 * f + half)

                    def tile(j, i=None, first=False):
                        x = j % 2
                        at = lambda v, per: v if i is None else i * per + v
                        if first and j == 0:
                            dve.wait_ge(s["rstd"], 2 * (1, 3, 6)[f] + 2)
                        dve.wait_ge(s["w_used"], at(FIRST[gu] + 2 * j + 1, 4))
                        nc.vector.tensor_tensor(gnorm[:, x], ps[:, 2 * x], rs[:], ALU.mult).then_inc(s["gate_norm"], 1)
                        dve.wait_ge(s["gate_sig"], at(G + j + 1, 2))
                        nc.vector.tensor_tensor(sgate[:, x], sgate[:, x], gnorm[:, x], ALU.mult).then_inc(s["gate_silu"], 1)
                        dve.wait_ge(s["w_used"], at(FIRST[gu] + 2 * j + 2, 4))
                        if not first:
                            dve.wait_ge(s["g_lo"], at(G + j - 1, 2))
                        nc.vector.tensor_tensor(gtmp[:, x], ps[:, 2 * x + 1], rs[:], ALU.mult).then_inc(s["up_norm"], 1)
                        dve.wait_ge(s["gate_silu"], at(G + j + 1, 2))
                        dve.wait_ge(s["up_norm"], at(G + j + 1, 2))
                        nc.vector.tensor_tensor(gtmp[:, x], sgate[:, x], gtmp[:, x], ALU.mult).then_inc(s["g_full"], 1)

                    tile(0, first=True)
                    tile(1, first=True)
                    with dve.Fori(0, (HC - 3) // 2) as i:
                        tile(2, i)
                        tile(3, i)
                    tile(HC - 1)
                    residual(down, 4, norm if half else None)

            nc.vector.memset(eps[:], EPS).then_inc(s["credit"], 1)
            nc.vector.memset(chd, 0.0).then_inc(s["credit"], 1)
            nc.vector.memset(start[:, 0:1], 0.0).then_inc(s["g_full"], 2)
            nc.vector.memset(start[:, 1:2], 0.0).then_inc(s["h_ready"], 2)
            nc.vector.memset(start[:, 3:4], 0.0).then_inc(s["merged"], 2)
            nc.vector.memset(lbt[:, 7, 0:1], 0.0).then_inc(s["o_lo"], 1)
            nc.vector.memset(start[:, 2:3], 0.0).then_inc(s["o_rstd"], 2)
            for c in range(1, DC - 1):
                add_square(0, c)
            dve.wait_ge(s["norm_consts"], 32)

            def cumulate(it, b, log_decay):
                nc.vector.tensor_tensor_scan(b, reset[:], log_decay, 0.0, ALU.mult, ALU.add).then_inc(s["cum"], 1)
                dve.wait_ge(s["cum"], cnt(it, 1, 1))

            def level_exponents(b, dv, l):
                m = 1 << l
                bb = b.rearrange("p (b h m) -> p b h m", h=2, m=m)
                x = dv[:, l].rearrange("p (b h m) -> p b h m", h=2, m=m)
                ref = bb[:, :, 0, m - 1:m].broadcast_to((P, T // (2 * m), m))
                nc.vector.tensor_tensor(x[:, :, 0], ref, bb[:, :, 0], ALU.subtract)
                nc.vector.tensor_tensor(x[:, :, 1], bb[:, :, 1], ref, ALU.subtract).then_inc(s["dec_in"], 1)

            def end_exponents(b, dv):
                b2 = b.rearrange("p (c t) -> p c t", c=NCH)
                nc.vector.tensor_tensor(dv[:, L_END].rearrange("p (c t) -> p c t", c=NCH),
                                        b2[:, :, C - 1:C].broadcast_to((P, NCH, C)), b2, ALU.subtract
                                        ).then_inc(s["dec_in"], 1)

            def exponents(it, b, log_decay, dv):
                cumulate(it, b, log_decay)
                for l in range(LEVELS - 1, -1, -1):
                    level_exponents(b, dv, l)
                end_exponents(b, dv)

            def gather_scores(head, sc, after=lambda n: None):
                for n, l in enumerate(list(range(LEVELS - 1, -1, -1)) + [LEVELS]):
                    dve.wait_ge(s["score_ps"], cnt(head, 8, n + 1))
                    if n:
                        dve.wait_ge(s["scores"], cnt(head, 8, n))
                    mk = lvl_mask[:, l:l + 1].broadcast_to((P, NCH, P))
                    sv = sc.rearrange("p (c t) -> p c t", c=NCH)
                    pv = ps[:, 4 + n % 2].rearrange("p (c t) -> p c t", c=NCH)
                    if n == 0:
                        nc.vector.tensor_tensor(sv, pv, mk, ALU.mult).then_inc(s["scores"], 1)
                    else:
                        nc.vector.memset(waited[:], 0.0)
                        nc.vector.copy_predicated(sv, mk.bitcast(U32), pv).then_inc(s["scores"], 1)
                    after(n)

            def chain_states(head, it, stv, ends):
                dve.wait_ge(s["st_ps"], cnt(head, 1, 1))
                nc.vector.tensor_copy(stv[:, 1], ps[:, 6, 0:C]).then_inc(s["states"], 1)
                for c in (1, 2):
                    dve.wait_ge(s["states"], cnt(head, 3, c))
                    dve.wait_ge(s["chunk_decay"], cnt(it, 1, 1))
                    nc.vector.scalar_tensor_tensor(out=stv[:, c + 1], in0=stv[:, c], scalar=ends[:, c:c + 1],
                                                   in1=ps[:, 6, c * C:(c + 1) * C], op0=ALU.mult, op1=ALU.add
                                                   ).then_inc(s["states"], 1)

            def head_output(head, gain, r, tmp, gate, dst, done):
                dve.wait_ge(s["o_rstd"], cnt(head, 2, 4))
                nc.vector.scalar_tensor_tensor(out=tmp, in0=ps[:, 7], scalar=gain[:, 0:1], in1=r,
                                               op0=ALU.mult, op1=ALU.mult).then_inc(s["o_scaled"], 1)
                dve.wait_ge(s["o_scaled"], cnt(head, 1, 1))
                nc.vector.tensor_tensor(dst, tmp, gate, ALU.mult).then_inc(done, 1)

            norm(0)
            dve.wait_ge(s["consts_loaded"], ALL_CONSTANTS)
            lbs = s["lb_steps"]
            nc.vector.tensor_tensor(lbt[:, 3], lbl[:, 0], lbl[:, 1], ALU.max).then_inc(lbs, 1)
            dve.wait_ge(lbs, 1)
            nc.vector.tensor_tensor(lbt[:, 3], lbt[:, 3], lbl[:, 2], ALU.max).then_inc(lbs, 1)
            dve.wait_ge(lbs, 2)
            for r in range(3):
                nc.vector.tensor_tensor(lbt[:, r], lbl[:, r], lbt[:, 3], ALU.subtract).then_inc(lbs, 1)
            dve.wait_ge(lbs, 6)
            nc.vector.tensor_tensor(lbt[:, 3], lbt[:, 0], lbt[:, 1], ALU.add).then_inc(lbs, 1)
            dve.wait_ge(lbs, 7)
            nc.vector.tensor_tensor(lbt[:, 3], lbt[:, 3], lbt[:, 2], ALU.add).then_inc(lbs, 1)
            dve.wait_ge(lbs, 8)
            nc.vector.reciprocal(lbt[:, 4], lbt[:, 3]).then_inc(lbs, 1)
            dve.wait_ge(lbs, 9)
            nc.vector.tensor_tensor(lb, lbt[:, 0], lbt[:, 4], ALU.mult).then_inc(lbs, 1)
            dve.wait_ge(lbs, 10)
            nc.vector.tensor_scalar(omlb, lb, -1.0, 1.0, ALU.mult, ALU.add).then_inc(lbs, 1)
            dve.wait_ge(lbs, 11)

            def hgrn_gates(head):
                x = (head if isinstance(head, int) else head[1]) % 2
                col = bass.ds(head[0] * 2 + head[1], 1) if not isinstance(head, int) else slice(head, head + 1)
                dve.wait_ge(s["sig_f"], cnt(head, 1, 1))
                nc.vector.tensor_scalar(fg, sf_, omlb[:, col], lb[:, col], ALU.mult, ALU.add).then_inc(s["forget"], 1)
                dve.wait_ge(s["forget"], cnt(head, 1, 1))
                nc.vector.tensor_scalar(key[x], fg, -1.0, 1.0, ALU.mult, ALU.add).then_inc(s["key"], 1)
                dve.wait_ge(s["sig_q"], cnt(head, 1, 1))
                nc.vector.tensor_tensor(qry[x], sq_, ps[:, 0], ALU.mult).then_inc(s["query"], 1)

            def hgrn_silu(head):
                dve.wait_ge(s["sig_g"], cnt(head, 1, 1))
                nc.vector.tensor_tensor(sgl, sg_, ps[:, 2], ALU.mult).then_inc(s["silu_g"], 1)

            hgrn_gates(0)
            dve.wait_ge(s["log_f"], 1)
            exponents(0, bcum, lf, dec)

            def hgrn_head(head):
                nxt = later(head, 1)
                more = head != HEADS_H - 1

                def prepare(n):
                    if n == 2:
                        hgrn_silu(head)
                    if not more:
                        return
                    if n == 3:
                        hgrn_gates(nxt)
                    if n == 4:
                        dve.wait_ge(s["log_f"], cnt(nxt, 1, 1))
                        dve.wait_ge(s["dec_out"], cnt(head, 5, 5))
                        cumulate(nxt, bcum, lf)
                    for l in {5: (6, 5, 4), 6: (3, 2), 7: (1, 0)}.get(n, ()):
                        level_exponents(bcum, dec, l)

                gather_scores(head, sc_mat, prepare)
                chain_states(head, head, st, chd)
                if more:
                    end_exponents(bcum, dec)
                dve.wait_ge(s["o_lo"], cnt(head, 1, 1))
                head_output(head, hgain, ors, otmp, sgl, otmp, s["o_full"])

            over_heads(dve, hgrn_head)
            residual_and_input("hgrn_out", 1)
            ffn(0, 2)

            norm(2)

            def rope(N):
                dve.wait_ge(s["raw_ready"], N + 1)
                for lower in (0, 64):
                    src, dst = slice(lower, lower + 64), slice(64 - lower, 128 - lower)
                    nc.vector.tensor_tensor(tsin[dst, N % 2], raw[src, N % 2], sin_a[src], ALU.mult
                                            ).then_inc(s["rope_sin"], 1)
                dve.wait_ge(s["rope_sin"], 2 * N + 2)
                dve.wait_ge(s["rope_cos"], N + 1)
                nc.vector.tensor_tensor(QK[N // 6 % 2][:, N % 6], tcos[:, N % 2], tsin[:, N % 2], ALU.add
                                        ).then_inc(s["qk_ready"], 1)

            def mix_max(j):
                dve.wait_ge(s["lse_rows"], 3 * j + 3)
                nc.vector.tensor_tensor(mxw, lrow[:, 0], lrow[:, 1], ALU.max).then_inc(s["mix_max1"], 1)
                dve.wait_ge(s["mix_max1"], j + 1)
                nc.vector.tensor_tensor(mxw, mxw, lrow[:, 2], ALU.max).then_inc(s["mix_max"], 1)
                dve.wait_ge(s["mix_max"], j + 1)
                nc.vector.tensor_tensor(lrow, lrow, mxw[:, None, :].broadcast_to((P, GROUPS, T)), ALU.subtract
                                        ).then_inc(s["mix_diff"], 1)

            def mix_apply(j):
                dve.wait_ge(s["mix_exp"], j + 1)
                nc.vector.tensor_tensor(sum_, lrow[:, 0], lrow[:, 1], ALU.add).then_inc(s["mix_sum1"], 1)
                dve.wait_ge(s["mix_sum1"], j + 1)
                nc.vector.tensor_tensor(sum_, sum_, lrow[:, 2], ALU.add).then_inc(s["mix_sum"], 1)
                dve.wait_ge(s["mix_sum"], j + 1)
                nc.vector.reciprocal(rec, sum_).then_inc(s["mix_recip"], 1)
                dve.wait_ge(s["mix_recip"], j + 1)
                nc.vector.tensor_tensor(lrow, lrow, rec[:, None, :].broadcast_to((P, GROUPS, T)), ALU.mult
                                        ).then_inc(s["mix_weight"], 1)
                dve.wait_ge(s["mix_weight"], j + 1)
                dve.wait_ge(s["ao_raw"], 3 * j + 3)
                for g in range(GROUPS):
                    nc.vector.tensor_tensor(aO[:, g * HPG + j], aO[:, g * HPG + j], lrow[:, g], ALU.mult
                                            ).then_inc(s["ao_ready"], 1)

            dve.wait_ge(s["spilled"], 16)
            for n in range(6):
                rope(n)
            for j in range(HPG):
                N = 6 * (j + 1)
                if j + 1 < HPG:
                    rope(N)
                    rope(N + 1)
                for g in range(GROUPS):
                    dve.wait_ge(s["sc_ps"], 3 * j + g + 1)
                    if g == 0:
                        nc.vector.scalar_tensor_tensor(out=SC[0], in0=SC_BANKS[0], scalar=float(P) ** -0.5,
                                                       in1=win_mask[:], op0=ALU.mult, op1=ALU.add
                                                       ).then_inc(s["sc_masked"], 1)
                    else:
                        nc.vector.scalar_tensor_tensor(out=SC[g], in0=SC_BANKS[g], scalar=float(P) ** -0.5,
                                                       in1=res_mask[:, g - 1:g].broadcast_to((P, TT, P)),
                                                       op0=ALU.mult, op1=ALU.add).then_inc(s["sc_masked"], 1)
                    dve.wait_ge(s["sc_masked"], 3 * j + g + 1)
                    nc.vector.tensor_reduce(mx[:, g], SC[g], AX.X, ALU.max).then_inc(s["sc_max"], 1)
                    dve.wait_ge(s["sc_max"], 3 * j + g + 1)
                    nc.vector.tensor_scalar(nmx[:, g], mx[:, g], -1.0, None, ALU.mult).then_inc(s["sc_negmax"], 1)
                if j:
                    mix_max(j - 1)
                dve.wait_ge(s["p_exp"], 12 * (j + 1))
                nc.vector.reciprocal(lrec, lsum).then_inc(s["p_recip"], 1)
                dve.wait_ge(s["p_recip"], j + 1)
                nc.vector.tensor_tensor(SC[0], SC[0], lrec[:, 0, :, None].broadcast_to((P, TT, 2 * P)), ALU.mult
                                        ).then_inc(s["p_norm"], 1)
                both = scm[:, 1024:2048].rearrange("p (b n) -> p b n", b=2 * TT)
                r12 = lrec[:, 1:3].rearrange("p g b -> p (g b)")[:, :, None]
                nc.vector.tensor_tensor(both, both, r12.broadcast_to((P, 2 * TT, P)), ALU.mult).then_inc(s["p_norm"], 1)
                dve.wait_ge(s["p_logsum"], j + 1)
                nc.vector.tensor_tensor(lsev, lsev, mx, ALU.add).then_inc(s["lse"], 1)
                if j + 1 < HPG:
                    rope(N + 2)
                if j:
                    mix_apply(j - 1)
                if j + 1 < HPG:
                    for n in range(3, 6):
                        rope(N + n)
            mix_max(HPG - 1)
            mix_apply(HPG - 1)
            dve.wait_ge(s["reloaded"], 16)
            for n in range(DC):
                dve.wait_ge(s["w_used"], FIRST["attn_out"] + n // 4 * 8 + 4 + n % 4 + 1)
                nc.vector.tensor_tensor(h[:, n], h[:, n], ps[:, (0, 1, 4, 5)[n % 4]], ALU.add).then_inc(s["h_ready"], 1)
                early_input(3, n)
            ffn(1, 4)

            norm(4, s["h_ready"])
            norm(5)
            dve.wait_ge(s["nsa_consts"], 16 * 6)

            def nsa_rope(x):
                n = (0, 1, 2, 3, 6, 7)[x]
                dve.wait_ge(s["nrot_ps"], x + 1)
                nc.vector.tensor_tensor(nsin[:, x % 2], ps[:, 2 + x % 2], sin_n[:], ALU.mult).then_inc(s["nrope_sin"], 1)
                dve.wait_ge(s["nrope_sin"], x + 1)
                dve.wait_ge(s["nrope_cos"], x + 1)
                dst = qrot[:, n] if n < 4 else kr[:, n - 6]
                nc.vector.tensor_tensor(dst, ncos[:, x % 2], nsin[:, x % 2], ALU.add).then_inc(s["nrope"], 1)

            for x in range(4):
                nsa_rope(x)
            dve.wait_ge(s["kvpe_zero"], 2)
            for x in range(2):
                dve.wait_ge(s["nt_ready"], 5 + x)
                for g in range(2):
                    src = slice(g * HD, (g + 1) * HD)
                    kv = kvraw[src, x].rearrange("p (n l o) -> p o l n", l=8, o=2)
                    pos = pos_kv[src, x].rearrange("p (l o) -> p o l", o=2)
                    for odd in range(2):
                        for hi in range(2):
                            dst = kvp[odd * HD:(odd + 1) * HD, x, 8 * hi:8 * hi + 8, g * NB:g * NB + 31]
                            nc.vector.tensor_tensor(dst, kv[:, odd, :, hi:hi + 31],
                                                    pos[:, odd, 8 * hi:8 * hi + 8, None].broadcast_to((HD, 8, 31)),
                                                    ALU.add).then_inc(s["kvpe"], 1)
            for x in (4, 5):
                nsa_rope(x)
            for x in range(2):
                dve.wait_ge(s["hid_sig"], x + 1)
                if x == 0:
                    nc.vector.tensor_tensor(hidk, hsig[:, 0], ps[:, 1, 0:2 * NB], ALU.mult).then_inc(s["hid"], 1)
                else:
                    for g in range(2):
                        src = slice(g * NB, (g + 1) * NB)
                        m = nc.vector.tensor_tensor(hidv[:, g * P:(g + 1) * P].rearrange("p (k n) -> p k n", k=4),
                                                    hsig[:, 1, None, src].broadcast_to((P, 4, NB)),
                                                    ps[:, 0, src][:, None, :].broadcast_to((P, 4, NB)), ALU.mult)
                    m.then_inc(s["hid"], 1)
            dve.wait_ge(s["gz_ps"], 1)
            dve.wait_ge(s["spilled"], 32)
            for p in range(2):
                nc.vector.tensor_scalar(la[:, p], ps[:, 2 + p], gbias[:, p:p + 1], None, ALU.add).then_inc(s["z_b"], 1)
            for p in range(2):
                dve.wait_ge(s["z_ln"], p + 1)
                nc.vector.scalar_tensor_tensor(out=la[:, p], in0=la[:, p], scalar=0.0, in1=zab, op0=ALU.min,
                                               op1=ALU.subtract).then_inc(s["z_min"], 1)
                dve.wait_ge(s["z_min"], p + 1)
                nc.vector.tensor_scalar(la[:, p], la[:, p], 1.0 / TAU, None, ALU.mult).then_inc(s["log_a"], 1)
            SH = (P, TT, HEADS_N, NB)
            cs = ps[:, 4:6].rearrange("p g (t h n) -> p g t h n", t=TT, h=4)
            mk = cmp_mask[:].rearrange("p k (t n) -> p k t n", t=TT)
            dve.wait_ge(s["cs_ps"], 1)
            for g in range(2):
                nc.vector.tensor_tensor(sC[:, :, 4 * g:4 * g + 4], cs[:, g], mk[:, 0, :, None, :].broadcast_to((P, TT, 4, NB)),
                                        ALU.add).then_inc(s["cs_masked"], 1)
            dve.wait_ge(s["cs_masked"], 2)
            nc.vector.tensor_reduce(cmx, sC, AX.X, ALU.max).then_inc(s["cs_max"], 1)
            dve.wait_ge(s["cs_max"], 1)
            nc.vector.tensor_tensor(sC, sC, cmx[:, :, :, None].broadcast_to(SH), ALU.subtract).then_inc(s["cs_sub"], 1)
            dve.wait_ge(s["cs_exp"], 1)
            nc.vector.tensor_reduce(csum, sC, AX.X, ALU.add).then_inc(s["cs_sum"], 1)
            dve.wait_ge(s["cs_sum"], 1)
            nc.vector.reciprocal(crec, csum).then_inc(s["cs_rec"], 1)
            nc.vector.tensor_tensor(sC, sC, mk[:, 1, :, None, :].broadcast_to(SH), ALU.mult).then_inc(s["cs_valid"], 1)
            dve.wait_ge(s["cs_rec"], 1)
            dve.wait_ge(s["ngate_ready"], TT)
            nc.vector.tensor_tensor(cw, crec, ngate.rearrange("p t (h b) -> p t h b", b=3)[:, :, :, 0], ALU.mult
                                    ).then_inc(s["cs_gate"], 1)
            dve.wait_ge(s["cs_gate"], 1)
            dve.wait_ge(s["cs_valid"], 1)
            nc.vector.tensor_tensor(sC, sC, cw[:, :, :, None].broadcast_to(SH), ALU.mult).then_inc(s["cs_w"], 1)

            def nsa_stats(i, x):
                base = ps[:, 3 * x:3 * x + 3].rearrange("p a n -> p (a n)")
                dve.wait_ge(s["ns_ps"], i * 2 + (x + 1))
                for tt in range(TT):
                    diag = base[:, BOFF[tt] + tt * P:BOFF[tt] + (tt + 1) * P]
                    nc.vector.tensor_tensor(diag, diag, res_mask[:, 0], ALU.add).then_inc(s["ns_masked"], 1)
                for tt in range(TT):
                    dve.wait_ge(s["ns_masked"], i * 8 + (4 * x + tt + 1))
                    nc.vector.tensor_reduce(nmax[:, x, tt:tt + 1], base[:, BOFF[tt]:BOFF[tt] + (tt + 1) * P], AX.X, ALU.max
                                            ).then_inc(s["ns_max"], 1)
                    dve.wait_ge(s["ns_max"], i * 8 + (4 * x + tt + 1))
                    nc.vector.tensor_scalar(nneg[:, x, tt:tt + 1], nmax[:, x, tt:tt + 1], -1.0, None, ALU.mult
                                            ).then_inc(s["ns_neg"], 1)

            def nsa_scale(i, x):
                dve.wait_ge(s["ns_exp"], i * 8 + (4 * x + 4))
                nc.vector.reciprocal(nrec[:, x], nsum[:, x]).then_inc(s["n_rec"], 1)
                dve.wait_ge(s["n_rec"], i * 2 + (x + 1))
                nc.vector.tensor_tensor(nw[:, x, :, None], nrec[:, x, :, None], ngate[:, :, bass.ds(i * 3 + (1 + x), 1)],
                                        ALU.mult).then_inc(s["n_w"], 1)
                dve.wait_ge(s["n_w"], i * 2 + (x + 1))
                for tt in range(TT):
                    pr = prob[:, x, OFF[tt]:OFF[tt] + (tt + 1) * P]
                    nc.vector.tensor_scalar(pr, pr, nw[:, x, tt:tt + 1], None, ALU.mult).then_inc(s["ns_scaled"], 1)

            def nsa_add(i, odd):
                dve.wait_ge(s["no_ps"], i * 4 + (2 * odd + 2))
                rows = slice(odd * HD, odd * HD + HD)
                o = oaT[rows, i] if isinstance(i, int) else oaT[rows, bass.ds(i, 1)].rearrange("p a t -> p (a t)")
                nc.vector.tensor_tensor(o, o, ps[rows, 6 + odd], ALU.add).then_inc(s["oa_acc"], 1)

            dve.wait_ge(s["oa_ready"], TT)
            nsa_stats(0, 0)
            nsa_scale(0, 0)
            nsa_stats(0, 1)
            nsa_scale(0, 1)
            nsa_stats(1, 0)
            with dve.Fori(0, HEADS_N // 2 - 1) as i:
                nsa_scale(i * 2 + 1, 0)
                nsa_stats(i * 2 + 1, 1)
                nsa_add(i, 0)
                nsa_scale(i * 2 + 1, 1)
                nsa_stats(i * 2 + 2, 0)
                nsa_scale(i * 2 + 2, 0)
                nsa_stats(i * 2 + 2, 1)
                nsa_add(i, 1)
                nsa_scale(i * 2 + 2, 1)
                nsa_stats(i * 2 + 3, 0)
            nsa_scale(HEADS_N - 1, 0)
            nsa_stats(HEADS_N - 1, 1)
            nsa_add(HEADS_N // 2 - 1, 0)
            nsa_scale(HEADS_N - 1, 1)
            nsa_add(HEADS_N // 2 - 1, 1)

            for p in range(2):
                dve.wait_ge(s["log_a"], p + 1)
                exponents(HEADS_H + p, gcum[:, p], la[:, p], gdec[p])
            def gla_silu(n):
                dve.wait_ge(s["gr_sig"], n + 1)
                nc.vector.tensor_tensor(gsr[:, n], gsig[:, n % 2], ps[:, n], ALU.mult).then_inc(s["gr_silu"], 1)

            gla_silu(0)
            gla_silu(1)
            for hh in range(HEADS_G):
                gather_scores(HEADS_H + hh, gsc)
                chain_states(HEADS_H + hh, HEADS_H + hh // 2, gst, gchd[:, hh // 2])
                if hh < 2:
                    gla_silu(2 + hh)
                dve.wait_ge(s["gr_silu"], hh + 1)
                head_output(HEADS_H + hh, ggain, gors, gotmp, gsr[:, hh], goT[:, hh], s["gb_ready"])

            for j in range(DC):
                b, x = 4 * (j % 2), 2 * (j % 2)
                dve.wait_ge(s["w_used"], FIRST["merge"] + 3 * j + 3)
                dve.wait_ge(s["mg_sig"], 2 * j + 2)
                nc.vector.tensor_tensor(msig[:, x], msig[:, x], ps[:, b + 2], ALU.mult).then_inc(s["mg_a"], 1)
                nc.vector.tensor_tensor(msig[:, x + 1], msig[:, x + 1], ps[:, b + 3], ALU.mult).then_inc(s["merged"], 1)
                dve.wait_ge(s["mg_a"], j + 1)
                dve.wait_ge(s["merged"], j + 3)
                if j >= 2:
                    dve.wait_ge(s["m_lo"], j - 1)
                nc.vector.tensor_tensor(mtmp[:, j % 2], msig[:, x], msig[:, x + 1], ALU.add).then_inc(s["m_full"], 1)
            dve.wait_ge(s["reloaded"], 32)
            residual_and_input("mix_out", 6)
            ffn(2, 7)
            norm(7, s["credit"])


def kernel(**inputs):
    import numpy as np
    from concourse import bacc
    from concourse.bass_utils import run_bass_kernel_spmd

    g = {n: np.asarray(v) for n, v in inputs.items()}

    def fm(w):
        K, N = w.shape
        return np.ascontiguousarray(w.reshape(K // P, P, N // P, P).transpose(2, 1, 0, 3).reshape(N // P, P, K))

    def down(w):
        return np.ascontiguousarray(w.reshape(HC, P, DC, P).transpose(2, 1, 0, 3).reshape(DC, P, HC * P))

    def cols(v):
        return v.reshape(-1, P).T

    arrays = {"x": np.ascontiguousarray(g["x"][0].reshape(T, DC, P).transpose(2, 1, 0))}
    w = fm(g["hgrn_w_in"][0]).reshape(4, 8, P, D)
    arrays["w_hgrn"] = np.ascontiguousarray(w[[1, 0, 3, 2]].transpose(1, 0, 2, 3).reshape(32, P, D))
    arrays["w_hgrn_out"] = fm(g["hgrn_w_out"][0])
    ffns = [(g["ffn_w_in"][n][:, :FF], g["ffn_w_in"][n][:, FF:], g["ffn_w_down"][n]) for n in range(2)]
    ffns.append((g["w_ffn_gate_2"][0], g["w_ffn_up_2"][0], g["w_ffn_down_2"][0]))
    for n, (gate, up, w_down) in enumerate(ffns):
        both = np.stack([fm(gate), fm(up)], 1).reshape(2, 2 * HC, P, D)
        for half in range(2):
            arrays[f"w_gu{n}{'ab'[half]}"] = np.ascontiguousarray(both[half])
            arrays[f"w_down{n}{'ab'[half]}"] = down(w_down[half * HC * P:(half + 1) * HC * P])

    def tm(w):
        return np.ascontiguousarray(w.reshape(4, 2, P, -1).transpose(0, 2, 1, 3).reshape(4, P, -1))

    AW = GROUPS * HPG * P
    qkv = g["attn_w_qkv"][0]
    arrays["w_attn_v"] = np.concatenate([tm(qkv[:, 2 * AW + n * 512:2 * AW + (n + 1) * 512]) for n in range(GROUPS)])
    w = fm(qkv[:, :2 * AW]).reshape(2, GROUPS, HPG, P, D)
    arrays["w_attn_qk"] = np.ascontiguousarray(w.transpose(2, 1, 0, 3, 4).reshape(24, P, D))
    w = fm(g["attn_w_out"][0]).reshape(2, 4, P, GROUPS, 2, 2, P)
    arrays["w_attn_out"] = np.ascontiguousarray(w.transpose(0, 4, 1, 2, 5, 3, 6).reshape(2 * DC, P, 6 * P))
    arrays["gains"] = np.ascontiguousarray(np.stack([cols(v) for v in (
        g["norm_mix"][0], g["norm_ffn"][0], g["norm_mix"][1], g["norm_ffn"][1], g["final_norm"],
        g["norm_mix_2"][0], g["norm_ffn_2"][0], g["norm_final_2"])], 1))
    arrays["lbl"] = np.ascontiguousarray(g["hgrn_lb_logits"].reshape(3, DC, P).transpose(2, 0, 1))
    arrays["hgain"] = np.ascontiguousarray(g["hgrn_out_norm"].reshape(P, 1))
    arrays["ident"] = np.eye(P, dtype=np.float32)
    arrays["ones"] = np.ones((P, P), np.float32)
    si, ti = np.arange(P)[:, None], np.arange(P)[None, :]
    masks = [(si // (2 << l) == ti // (2 << l)) & (si // (1 << l) % 2 == 0) & (ti // (1 << l) % 2 == 1)
             for l in range(LEVELS)] + [si == ti]
    arrays["lvl_mask"] = np.ascontiguousarray(np.stack(masks, 1).astype(np.float32))
    arrays["reset"] = np.ascontiguousarray(np.broadcast_to((np.arange(T) % C != 0).astype(np.float32), (P, T)))

    w = g["w_in_2"][0]
    cuts = np.cumsum([0, HEADS_N * HD, 12 * HD, 3 * HEADS_N, HEADS_G * HD, HEADS_G * HD, HEADS_G * P, RANK,
                      HEADS_G * P, 2 * D])
    wq, wkv, wgate, wgq, wgk, wgv, wlr, wr, wmerge = [w[:, lo:hi] for lo, hi in zip(cuts[:-1], cuts[1:])]
    wq = wq.reshape(D, 2, 4, HD).transpose(0, 2, 1, 3).reshape(D, 512)
    kv = [wkv[:, n * P:(n + 1) * P] for n in range(6)]
    arrays["w_nsa_fm"] = fm(np.concatenate([wq, kv[0], kv[1], kv[2], kv[4]], 1))
    w = np.concatenate([kv[3], kv[5], wgate], 1)
    arrays["w_nsa_tm"] = np.ascontiguousarray(w.reshape(2, 4, P, TM_COLS).transpose(0, 2, 1, 3).reshape(2, P, -1))
    arrays["w_gla_v"] = tm(wgv)
    arrays["w_gla_fm"] = fm(np.concatenate([wgq, wgk], 1))
    arrays["w_gla_lr"] = fm(np.concatenate([wlr, np.zeros((D, P - RANK), np.float32)], 1))
    arrays["w_gla_r"] = fm(wr)
    up = np.concatenate([g["w_up_nsa_2"][0], g["w_up_gla_2"][0]], 0)
    arrays["w_merge"] = np.ascontiguousarray(
        np.stack([fm(wmerge[:, :D]), fm(wmerge[:, D:]), fm(up)], 1).reshape(3 * DC, P, D))
    arrays["w_mix_out"] = fm(g["w_out_2"][0])
    arrays["cmp_w1"] = np.ascontiguousarray(np.stack(
        [g[n][0].reshape(16, P, P).transpose(1, 0, 2) for n in ("cmp_k_w1_2", "cmp_v_w1_2")], 1))
    zero = np.zeros((P, HD), np.float32)
    arrays["cmp_w2k"] = np.ascontiguousarray(np.concatenate([zero, g["cmp_k_w2_2"][0], zero], 1))
    arrays["cmp_w2v"] = np.ascontiguousarray(g["cmp_v_w2_2"][0])
    arrays["pos_kv"] = np.ascontiguousarray(np.stack(
        [np.concatenate([g[n][0].T] * 2) for n in ("cmp_pe_k_2", "cmp_pe_v_2")], 1))
    arrays["gw2"] = np.ascontiguousarray(g["gla_gate_w2_2"][0])
    arrays["gbias"] = np.ascontiguousarray(g["gla_gate_b_2"][0].reshape(2, P).T)
    arrays["ggain"] = np.ascontiguousarray(g["gla_norm_2"].reshape(P, 1))
    half = 8
    rot = np.zeros((P, P), np.float32)
    for base in (0, HD):
        for m in range(half):
            rot[base + m + half, base + m], rot[base + m, base + m + half] = -1.0, 1.0
    arrays["rot_n"] = rot
    inv = (np.float32(500000.0) ** (-np.arange(half, dtype=np.float32) / np.float32(half))).astype(np.float32)
    ang = (np.arange(T, dtype=np.float32)[None, :] * inv[:, None]).astype(np.float32)
    one, nil = np.ones((HD - 2 * half, T), np.float32), np.zeros((HD - 2 * half, T), np.float32)
    arrays["cos_n"] = np.concatenate([np.cos(ang), np.cos(ang), one] * 2).astype(np.float32)
    arrays["sin_n"] = np.concatenate([np.sin(ang), np.sin(ang), nil] * 2).astype(np.float32)
    blk = np.arange(NB)
    seen = (blk * 16 + 31 <= np.arange(T)[:, None]) & (blk < NB - 1)
    seen = seen.reshape(TT, P, NB).transpose(1, 0, 2).reshape(P, TT * NB)
    arrays["cmp_mask"] = np.ascontiguousarray(np.stack([np.where(seen, 0.0, NEG), seen], 1).astype(np.float32))
    inv = (1.0 / (np.float32(10000.0) ** (np.arange(0, P, 2, dtype=np.float32) / np.float32(P)))).astype(np.float32)
    ang = (np.arange(T, dtype=np.float32)[None, :] * inv[:, None]).astype(np.float32)
    arrays["cos_a"] = np.concatenate([np.cos(ang)] * 2).astype(np.float32)
    arrays["sin_a"] = np.concatenate([np.sin(ang), -np.sin(ang)]).astype(np.float32)
    cur, prev = si >= ti, si <= ti
    first = np.concatenate([np.zeros((P, P), bool), cur], 1)
    later = np.concatenate([prev, cur], 1)
    arrays["win_mask"] = np.ascontiguousarray(
        np.where(np.stack([first, later, later, later], 1), 0.0, NEG).astype(np.float32))
    arrays["res_mask"] = np.ascontiguousarray(
        np.where(np.stack([cur, cur & (si % 4 == ti % 4)], 1), 0.0, NEG).astype(np.float32))

    nc = bacc.Bacc("TRN2", target_bir_lowering=False, num_devices=1)
    aps = {n: nc.dram_tensor("in_" + n, v.shape, F32, kind="ExternalInput").ap() for n, v in arrays.items()}
    aps["h_spill"] = nc.dram_tensor("h_spill", (P, DC, T), F32, kind="Internal").ap()
    out = nc.dram_tensor("out_h", (P, DC, T), F32, kind="ExternalOutput").ap()
    program(nc, aps, out)
    r = run_bass_kernel_spmd(nc, [{"in_" + n: v for n, v in arrays.items()}], core_ids=[0])
    y = r.results[0]["out_h"]
    return np.ascontiguousarray(y.transpose(2, 1, 0).reshape(1, T, D))
```
